# Optimizing a Trainium2 kernel written in Bass

```python
import math
import jax
import jax.numpy as jnp
from jax import lax
import numpy as np

D_MODEL = 1024
BATCH = 1
SEQ = 1024
DEPTH = 1
DEC_BATCH = 8
DEC_SEQ = 1
PAST_LEN = 8192
PAGE_SIZE = 128

RWKV_HEAD_DIM = 64
RWKV_HEADS = D_MODEL // RWKV_HEAD_DIM
RWKV_WIDTH = RWKV_HEADS * RWKV_HEAD_DIM
LORA_DECAY = max(32, int(round(1.8 * D_MODEL ** 0.5 / 32)) * 32)
LORA_ICLR = max(32, int(round(1.8 * D_MODEL ** 0.5 / 32)) * 32)
LORA_VRES = max(32, int(round(1.3 * D_MODEL ** 0.5 / 32)) * 32)
RWKV_GN_EPS = 64e-5
GLA_HEADS = 4
GLA_KEY_WIDTH = D_MODEL // 2
GLA_VAL_WIDTH = D_MODEL
GLA_DK = GLA_KEY_WIDTH // GLA_HEADS
GLA_DV = GLA_VAL_WIDTH // GLA_HEADS
GLA_GATE_RANK = 16
GLA_GATE_NORMALIZER = 16.0
GLA_CHUNK = 64
GLA_NORM_EPS = 1e-5
FFN_HIDDEN = ((((8 * D_MODEL + 2) // 3) + 255) // 256) * 256
NORM_EPS = 1e-6
SHIFT_SIZES = (RWKV_WIDTH, RWKV_WIDTH, RWKV_WIDTH, LORA_DECAY, LORA_ICLR)
REST_SIZES = (GLA_KEY_WIDTH, GLA_KEY_WIDTH, GLA_VAL_WIDTH, GLA_GATE_RANK, D_MODEL, D_MODEL)
N_SHIFT = sum(SHIFT_SIZES)
N_IN = N_SHIFT + sum(REST_SIZES)

kernel_name = "rwkv7_gla_parallel_hybrid_step"

def rmsnorm(x, g, eps=NORM_EPS):
    xf = x.astype(jnp.float32)
    y = xf * lax.rsqrt(jnp.mean(xf * xf, axis=-1, keepdims=True) + eps)
    return (y * g.astype(jnp.float32)).astype(x.dtype)

def split_cols(y, sizes):
    out, start = [], 0
    for s in sizes:
        out.append(y[..., start:start + s])
        start += s
    return out

def token_shift(y, y_prev, mu):
    shifted = jnp.concatenate([y_prev[:, None, :].astype(y.dtype), y[:, :-1]], axis=1)
    return y + mu.astype(y.dtype) * (shifted - y)

def rwkv7_recurrence(r, decay, k, v, kk, a, s0):
    f32 = jnp.float32
    xs = tuple(jnp.swapaxes(t.astype(f32), 0, 1) for t in (r, decay, k, v, kk, a))

    def step(S, inp):
        r_t, w_t, k_t, v_t, kk_t, a_t = inp
        sa = jnp.einsum('bhvk,bhk->bhv', S, -kk_t)
        S = (S * w_t[:, :, None, :]
             + sa[..., None] * (kk_t * a_t)[:, :, None, :]
             + v_t[..., None] * k_t[:, :, None, :])
        o_t = jnp.einsum('bhvk,bhk->bhv', S, r_t)
        return S, o_t

    s_fin, o = lax.scan(step, s0.astype(f32), xs)
    return jnp.swapaxes(o, 0, 1), s_fin

def gla_chunked(q, k, v, log_a, s0):
    f32 = jnp.float32
    B, T, H, _ = q.shape
    DV = v.shape[-1]
    C = math.gcd(T, GLA_CHUNK)
    n = T // C

    def to_chunks(t):
        return t.astype(f32).reshape(B, n, C, H, t.shape[-1]).transpose(1, 0, 3, 2, 4)

    xs = tuple(to_chunks(t) for t in (q, k, v, log_a))
    causal = jnp.tril(jnp.ones((C, C), dtype=bool))

    def step(S, inp):
        qc, kc, vc, gc = inp
        b = jnp.cumsum(gc, axis=2)
        b_last = b[:, :, -1:, :]
        q_dec = qc * jnp.exp(b)
        k_dec = kc * jnp.exp(-b)
        att = jnp.where(causal, jnp.einsum('bhid,bhjd->bhij', q_dec, k_dec), 0.0)
        o = jnp.einsum('bhij,bhjv->bhiv', att, vc) + jnp.einsum('bhid,bhdv->bhiv', q_dec, S)
        S = (S * jnp.exp(b_last)[:, :, 0, :, None]
             + jnp.einsum('bhjd,bhjv->bhdv', kc * jnp.exp(b_last - b), vc))
        return S, o

    s_fin, o = lax.scan(step, s0.astype(f32), xs)
    o = o.transpose(1, 0, 3, 2, 4).reshape(B, T, H, DV)
    return o, s_fin

def hybrid_mixer(xn, prev, v_first, s_wkv0, s_gla0, lp):
    f32 = jnp.float32
    B, T, _ = xn.shape
    proj = xn @ lp['w_in']
    shifted = token_shift(proj[..., :N_SHIFT], prev @ lp['w_in'][:, :N_SHIFT], lp['mu'])
    r, k, v, w_lo, a_lo = split_cols(shifted, SHIFT_SIZES)
    gq, gk, gv, g_lo, gate_a, gate_b = split_cols(proj[..., N_SHIFT:], REST_SIZES)

    hs = (B, T, RWKV_HEADS, RWKV_HEAD_DIM)
    w_log = -jax.nn.softplus(-(lp['w0'] + jnp.tanh(w_lo) @ lp['w2']).astype(f32)) - 0.5
    decay = jnp.exp(-jnp.exp(w_log))
    if v_first is None:
        v_first = v
    else:
        v_lo = token_shift(xn @ lp['vres_w1'], prev @ lp['vres_w1'], lp['vres_mu'])
        v = v + (v_first - v) * jax.nn.sigmoid(lp['vres_v0'] + v_lo @ lp['vres_w2'])
    a = jax.nn.sigmoid((lp['a0'] + a_lo @ lp['a2']).astype(f32))
    kk = (k * lp['k_k']).astype(f32).reshape(hs)
    kk = kk / jnp.maximum(jnp.sqrt(jnp.sum(kk * kk, axis=-1, keepdims=True)), 1e-12)
    k = k.astype(f32) * (1.0 + (a - 1.0) * lp['k_a'].astype(f32))
    r_h = r.astype(f32).reshape(hs)
    k_h = k.reshape(hs)
    v_h = v.astype(f32).reshape(hs)
    o, s_wkv = rwkv7_recurrence(r_h, decay.reshape(hs), k_h, v_h, kk, a.reshape(hs), s_wkv0)
    mean = jnp.mean(o, axis=-1, keepdims=True)
    var = jnp.mean(jnp.square(o - mean), axis=-1, keepdims=True)
    o = ((o - mean) * lax.rsqrt(var + RWKV_GN_EPS) * lp['lnx_g'].astype(f32).reshape(RWKV_HEADS, RWKV_HEAD_DIM)
         + lp['lnx_b'].astype(f32).reshape(RWKV_HEADS, RWKV_HEAD_DIM))
    bonus = jnp.sum(r_h * k_h * lp['r_k'].astype(f32), axis=-1, keepdims=True) * v_h
    rwkv_out = (o + bonus).reshape(B, T, RWKV_WIDTH)

    ks = (B, T, GLA_HEADS, GLA_DK)
    log_a = jax.nn.log_sigmoid((g_lo @ lp['gla_a2'] + lp['gla_ab']).astype(f32)) / GLA_GATE_NORMALIZER
    o_g, s_gla = gla_chunked(gq.reshape(ks) * (GLA_DK ** -0.5), gk.reshape(ks),
                             gv.reshape(B, T, GLA_HEADS, GLA_DV), log_a.reshape(ks), s_gla0)
    o_g = o_g * lax.rsqrt(jnp.mean(o_g * o_g, axis=-1, keepdims=True) + GLA_NORM_EPS) * lp['gla_g'].astype(f32)
    gla_out = o_g.reshape(B, T, GLA_VAL_WIDTH)

    merged = jax.nn.sigmoid(gate_a.astype(f32)) * rwkv_out + jax.nn.sigmoid(gate_b.astype(f32)) * gla_out
    out = merged.astype(xn.dtype) @ lp['w_o']
    return out, xn[:, -1], s_wkv, s_gla, v_first

LAYER_KEYS = {
    'w_in': 'w_in', 'mu': 'mu_shift', 'w0': 'rwkv_w0', 'w2': 'rwkv_w2', 'a0': 'rwkv_a0', 'a2': 'rwkv_a2',
    'k_k': 'rwkv_k_k', 'k_a': 'rwkv_k_a', 'r_k': 'rwkv_r_k', 'lnx_g': 'rwkv_lnx_g', 'lnx_b': 'rwkv_lnx_b',
    'gla_a2': 'gla_a2', 'gla_ab': 'gla_ab', 'gla_g': 'gla_norm_g', 'w_o': 'w_o',
}
VRES_KEYS = {'vres_w1': 'vres_w1', 'vres_mu': 'vres_mu', 'vres_w2': 'vres_w2', 'vres_v0': 'vres_v0'}

def run_group(x, shift_state, wkv_state, gla_state, params):
    h = x
    new_shift, new_wkv, new_gla = [], [], []
    v_first = None
    for l in range(DEPTH):
        lp = {short: params[name][l] for short, name in LAYER_KEYS.items()}
        if l > 0:
            lp.update({short: params[name][l - 1] for short, name in VRES_KEYS.items()})
        xn = rmsnorm(h, params['norm_mix'][l])
        mix, sh, sw, sg, v_first = hybrid_mixer(xn, shift_state[l], v_first, wkv_state[l], gla_state[l], lp)
        h = h + mix.astype(h.dtype)
        xn = rmsnorm(h, params['norm_ffn'][l])
        gate, up = split_cols(xn @ params['ffn_w_gu'][l], (FFN_HIDDEN, FFN_HIDDEN))
        h = h + ((jax.nn.silu(gate) * up) @ params['ffn_w_down'][l]).astype(h.dtype)
        new_shift.append(sh)
        new_wkv.append(sw)
        new_gla.append(sg)
    y = rmsnorm(h, params['norm_final'])
    return y, jnp.stack(new_shift), jnp.stack(new_wkv), jnp.stack(new_gla)

def setup_inputs(seed: int = 0) -> dict:
    key = jax.random.key(seed)
    ks = iter(jax.random.split(key, 40))
    f32 = jnp.float32

    def nrm(shape, scale):
        return jax.random.normal(next(ks), shape, f32) * scale

    def unif(shape, lo, hi):
        return jax.random.uniform(next(ks), shape, f32, lo, hi)

    L, Lv, D = DEPTH, DEPTH - 1, D_MODEL
    return {
        'x_prompt': nrm((BATCH, SEQ, D), 1.0),
        'x_sample': nrm((DEC_BATCH, DEC_SEQ, D), 1.0),
        'state_shift': nrm((L, DEC_BATCH, D), 1.0),
        'state_wkv': nrm((L, DEC_BATCH, RWKV_HEADS, RWKV_HEAD_DIM, RWKV_HEAD_DIM), 0.05),
        'state_gla': nrm((L, DEC_BATCH, GLA_HEADS, GLA_DK, GLA_DV), 0.05),
        'norm_mix': 1.0 + nrm((L, D), 0.05),
        'w_in': nrm((L, D, N_IN), D ** -0.5),
        'mu_shift': unif((L, N_SHIFT), 0.0, 1.0),
        'rwkv_w0': unif((L, RWKV_WIDTH), -6.0, -1.0),
        'rwkv_w2': nrm((L, LORA_DECAY, RWKV_WIDTH), 0.5 * LORA_DECAY ** -0.5),
        'rwkv_a0': nrm((L, RWKV_WIDTH), 0.1),
        'rwkv_a2': nrm((L, LORA_ICLR, RWKV_WIDTH), 0.5 * LORA_ICLR ** -0.5),
        'rwkv_k_k': 0.85 + nrm((L, RWKV_WIDTH), 0.05),
        'rwkv_k_a': 1.0 + nrm((L, RWKV_WIDTH), 0.05),
        'rwkv_r_k': nrm((L, RWKV_HEADS, RWKV_HEAD_DIM), 0.1),
        'rwkv_lnx_g': 1.0 + nrm((L, RWKV_WIDTH), 0.05),
        'rwkv_lnx_b': nrm((L, RWKV_WIDTH), 0.01),
        'vres_w1': nrm((Lv, D, LORA_VRES), D ** -0.5),
        'vres_mu': unif((Lv, LORA_VRES), 0.0, 1.0),
        'vres_w2': nrm((Lv, LORA_VRES, RWKV_WIDTH), 0.5 * LORA_VRES ** -0.5),
        'vres_v0': nrm((Lv, RWKV_WIDTH), 0.1),
        'gla_a2': nrm((L, GLA_GATE_RANK, GLA_KEY_WIDTH), GLA_GATE_RANK ** -0.5),
        'gla_ab': nrm((L, GLA_KEY_WIDTH), 0.01),
        'gla_norm_g': 1.0 + nrm((L, GLA_DV), 0.05),
        'w_o': nrm((L, D, D), D ** -0.5),
        'norm_ffn': 1.0 + nrm((L, D), 0.05),
        'ffn_w_gu': nrm((L, D, 2 * FFN_HIDDEN), D ** -0.5),
        'ffn_w_down': nrm((L, FFN_HIDDEN, D), FFN_HIDDEN ** -0.5),
        'norm_final': 1.0 + nrm((D,), 0.05),
    }

def reference(x_prompt, x_sample, state_shift, state_wkv, state_gla, norm_mix, w_in, mu_shift,
              rwkv_w0, rwkv_w2, rwkv_a0, rwkv_a2, rwkv_k_k, rwkv_k_a, rwkv_r_k, rwkv_lnx_g, rwkv_lnx_b,
              vres_w1, vres_mu, vres_w2, vres_v0, gla_a2, gla_ab, gla_norm_g, w_o, norm_ffn,
              ffn_w_gu, ffn_w_down, norm_final):
    params = {
        'norm_mix': norm_mix, 'w_in': w_in, 'mu_shift': mu_shift,
        'rwkv_w0': rwkv_w0, 'rwkv_w2': rwkv_w2, 'rwkv_a0': rwkv_a0, 'rwkv_a2': rwkv_a2,
        'rwkv_k_k': rwkv_k_k, 'rwkv_k_a': rwkv_k_a, 'rwkv_r_k': rwkv_r_k,
        'rwkv_lnx_g': rwkv_lnx_g, 'rwkv_lnx_b': rwkv_lnx_b,
        'vres_w1': vres_w1, 'vres_mu': vres_mu, 'vres_w2': vres_w2, 'vres_v0': vres_v0,
        'gla_a2': gla_a2, 'gla_ab': gla_ab, 'gla_norm_g': gla_norm_g, 'w_o': w_o,
        'norm_ffn': norm_ffn, 'ffn_w_gu': ffn_w_gu, 'ffn_w_down': ffn_w_down, 'norm_final': norm_final,
    }
    B = x_prompt.shape[0]
    p_shift0 = jnp.zeros((DEPTH, B, D_MODEL), x_prompt.dtype)
    p_wkv0 = jnp.zeros((DEPTH, B, RWKV_HEADS, RWKV_HEAD_DIM, RWKV_HEAD_DIM), jnp.float32)
    p_gla0 = jnp.zeros((DEPTH, B, GLA_HEADS, GLA_DK, GLA_DV), jnp.float32)
    y_prompt, shift_p, wkv_p, gla_p = run_group(x_prompt, p_shift0, p_wkv0, p_gla0, params)
    y_sample, shift_s, wkv_s, gla_s = run_group(x_sample, state_shift, state_wkv, state_gla, params)
    return (y_prompt, y_sample, shift_p, wkv_p, gla_p, shift_s, wkv_s, gla_s)


_drawn_inputs = setup_inputs


def setup_inputs(seed=0):
    import zlib

    import numpy as np

    out = dict(_drawn_inputs(seed))
    spreads = {}
    factors = {'rwkv_lnx_b': 8.0, 'gla_ab': 8.0}
    for name, (base, spread) in spreads.items():
        noise = np.random.default_rng([zlib.crc32(name.encode()), seed]).standard_normal(out[name].shape)
        drawn = base * np.exp(spread * noise) if base else spread * noise
        out[name] = jnp.asarray(drawn.astype(out[name].dtype))
    for name, factor in factors.items():
        out[name] = (out[name] * factor).astype(out[name].dtype)
    return out
```

```python
from contextlib import ExitStack

import concourse.bass as bass
from concourse import mybir

F32 = mybir.dt.float32
I32 = mybir.dt.int32
ACT = mybir.ActivationFunctionType
ALU = mybir.AluOpType
AX_X = mybir.AxisListType.X

P = 128
D = 1024
KT = D // P
T = 1024
NS = 8
TS = T + NS
XC = T + 2 * NS
HD = 64
NP = D // P
CR = 64
NC = T // CR
GH = 4
DK = 128
DV = 256
VT = DV // P
CG = 128
NG = T // CG
F = 2816
FT = F // P
NORM_EPS = 1e-6
GN_EPS = 64e-5
GLA_EPS = 1e-5
GATE_NORM = 16.0
HALF_DECAY = 0.5 * float(2.718281828459045) ** -0.5

XB = [(0, 348), (348, 346), (694, 346)]
XT = [(0, 348), (348, 346), (694, 338)]
TB = [(0, 344), (344, 344), (688, 344)]
PB = [(0, 342), (342, 342), (684, 340)]

LEVELS = [2, 4, 8, 16, 32]
C_ONES, C_BONES, C_ID, C_IDS, C_NIDS = 0, 128, 256, 384, 448
C_MG, C_MK, C_ML, C_M2, C_M2T, C_OFF = 512, 640, 768, 832, 896, 960
C_RR = C_OFF + 64 * len(LEVELS)
C_RG = C_RR + T
C_CAUSAL = C_RG + T
C_DELTA = C_CAUSAL + 128
C_EPS = C_DELTA + NS
NCONST = C_EPS + 3

(P_MUR, P_MUK, P_MUV, P_W0, P_A0, P_KK, P_KA, P_RK, P_LNG, P_LNB) = range(10)
P_CMUR, P_CMUK, P_CMUV, P_HW0, P_HA0, P_CKA = range(10, 16)
NPAR = 16

W_R, W_K, W_V, W_G = 0, 1024, 2048, 3072
W_LORA = 4096
WP = 4224
G_Q, G_K, G_V, G_B = 0, 1024, 2048, 4096
WG = 6144


def hybrid_step(nc, xT, prevT, gains, consts, w_lo, w_glo, mu_lo, w_gla, w_gla2, glapar, w_pair, par,
                gla_s, wkv_s, w_o, w_gu, w_d, yT, shT, wkvp, glap, wkvs, glas):
    with ExitStack() as ctx:
        arena = ctx.enter_context(nc.sbuf_tensor("arena", [P, 53200], F32))
        bank = [ctx.enter_context(nc.psum_tensor(f"bank{n}", [P, 512], F32)) for n in range(8)]

        def sem(name):
            return ctx.enter_context(nc.semaphore(name))

        def at(off, *dims):
            n = 1
            for d in dims:
                n *= d
            assert off + n <= 53200
            v = arena[:, off:off + n]
            if len(dims) == 1:
                return v
            names = "abcd"[:len(dims)]
            return v.rearrange("p (" + " ".join(names) + ") -> p " + " ".join(names),
                               **{names[j]: dims[j] for j in range(1, len(dims))})

        XN = at(0, KT, XC)
        MG = at(8320, KT, TS)
        WB = at(16576, WG)
        PAR = at(22720, NP, NPAR)
        MULO = at(22880, 2)
        GPAR = at(22882, GH + VT)
        CUR = at(22890, 24)
        GCUR = at(22914, 1)
        LO = at(22920, XC)
        SMALL = 23960
        CON = at(24832, NCONST)
        ONES = CON[:, C_ONES:C_ONES + 128]
        BONES = CON[:, C_BONES:C_BONES + 128]
        IDF = CON[:, C_ID:C_ID + 128]
        IDS = CON[:, C_IDS:C_IDS + 64]
        NIDS = CON[:, C_NIDS:C_NIDS + 64]
        GAINS = at(24832 + NCONST, 3, KT)
        A0 = 24832 + NCONST + 3 * KT
        A0 += -A0 % 8

        EPS = [CON[:, C_EPS + j:C_EPS + j + 1] for j in range(3)]

        N_SQ = [at(A0 + 1032 * j, TS) for j in range(2)]
        N_RS = at(A0 + 2064, TS)
        N_WLO = at(A0 + 3096, KT, 128)
        N_T0 = at(A0 + 4120, 1 + XC)
        N_WGLO = at(A0 + 5168, KT, 16)
        o = A0
        def take(n):
            nonlocal o
            s = o
            o += n + (-n % 8)
            return s
        GLO = at(take(XC), XC)
        E0 = at(take(TS), TS)
        LA = at(take(TS), TS)
        GB = at(take(T), T)
        EPG = at(take(T), T)
        EMG = at(take(T), T)
        GK_ = at(take(TS), TS)
        GQ_ = at(take(TS), TS)
        TGB = at(take(2 * TS), VT, TS)
        VTM = at(take(9 * DV), 9, DV)
        ATT = at(take(T), NG, CG)
        KTM = at(take(T), NG, CG)
        OG = at(take(2 * TS), VT, TS)
        SP = [at(take(DV), DV) for _ in range(2)]
        SF = at(take(DV), DV)
        GSQ = at(take(2 * TS), VT, TS)
        GS0 = at(take(NS * DV), NS, DV)
        VEXP = at(take(NS * DV), NS, DV)
        GKS = at(take(128), 128)
        GA2 = at(take(128), 128)
        GDM = at(take(NG), NG)
        GDE = at(take(NG), NG)
        GF = at(take(NG), NG)
        GAS = at(take(NS), NS)
        gla_end = o
        o = A0
        T0 = [at(take(1 + XC), 1 + XC) for _ in range(2)]
        X_ = T0[0][:, 0:T].rearrange("p (c t) -> p c t", t=CR)
        PP = T0[1][:, 0:T].rearrange("p (c t) -> p c t", t=CR)
        R = at(take(TS), TS)
        kofs = take(TS)
        K = at(kofs, TS)
        KTT = at(kofs, NC, CR)
        V = at(take(TS), TS)
        aofs = take(TS)
        A = at(aofs, TS)
        BTT = at(aofs, NC, CR)
        ldofs = take(TS)
        LD = at(ldofs, TS)
        KE = at(ldofs, T)
        bofs = take(TS)
        B = at(bofs, T)
        BE = at(bofs, T)
        EP = at(take(NC * 65), NC, 65)
        emofs = take(TS)
        EM = at(emofs, TS)
        VTT = at(emofs, NC, CR)
        kkofs = take(TS)
        KK = at(kkofs, TS)
        LL = at(kkofs, NC, CR)
        KA = at(take(TS), TS)
        KP = at(take(TS), TS)
        RK = at(take(TS), TS)
        O = at(take(TS), TS)
        TG = at(take(TS), TS)
        AR = at(take(2 * T), NC, 2, CR)
        GT = at(take(2 * T), NC, 2, CR)
        AK = at(take(2 * T), NC, 2, CR)
        Y = at(take(T), NC, CR)
        SS = [at(take(HD), HD) for _ in range(2)]
        SD = at(take(HD), HD)
        RH = at(take(HD), HD)
        U = at(take(HD), HD)
        pair_end = o
        assert max(gla_end, pair_end) <= 53200, (gla_end, pair_end)
        Q_R, Q_KP, Q_V, Q_KK, Q_KA, Q_W = range(6)
        SV = at(SMALL, 6, NP, NS)
        SB = at(SMALL + 384, NP, NS)
        STG = at(SMALL + 448, NP, NS)
        SO = at(SMALL + 512, NP, NS)
        SM_END = SMALL + 576
        assert SM_END <= 24832
        s_ = A0
        S0 = at(s_, HD, HD)
        S1 = at(s_ + 4096, HD, HD)
        S2 = at(s_ + 8192, HD, HD)
        QQ = at(s_ + 12288, 6, HD)
        SA = at(s_ + 12672, HD)
        OO = at(s_ + 12736, HD)
        ST = at(s_ + 12800, 8)
        O2 = at(s_ + 12808, 2 * HD)
        OSQ = at(s_ + 12936, HD)
        XN2 = at(0, KT, TS)
        H = at(16576, KT, TS)
        f_ = A0
        WO = [at(f_ + 1024 * j, KT, 128) for j in range(2)]
        F_SQ = [at(f_ + 2048 + 1032 * j, TS) for j in range(2)]
        F_RS = at(8320 + 6912, TS)
        WGU = [at(8320 + 2048 * j, 2, KT, 128) for j in range(2)]
        f0 = A0
        ACTV = at(f0, FT, TS)
        assert f0 + FT * TS <= 53200, f0
        WD = [at(8320 + 4096, FT, 128), at(8320, FT, 128)]
        Y_SQ = [at(1032 * j, TS) for j in range(2)]
        Y_RS = at(2064, TS)

        x_loaded, con_loaded, par_loaded = sem("x_loaded"), sem("con_loaded"), sem("par_loaded")
        lo_w_loaded = sem("lo_w_loaded")
        done = [sem(f"bank{b}_done") for b in range(3)]
        out_of = [sem(f"bank{b}_evacuated") for b in range(3)]
        sq_ready, sq_used, rs_ready, xn_ready = sem("sq_ready"), sem("sq_used"), sem("rs_ready"), sem("xn_ready")
        v_step = sem("vector_step")
        a_step = sem("scalar_step")
        par_ready = sem("par_ready")
        lo_ready = sem("lo_ready")
        glo_ready = sem("glo_ready")
        mu_ready = sem("mu_ready")
        gw_loaded = sem("gla_weights_loaded")
        gs_loaded = sem("gla_state_loaded")
        gw_used = sem("gla_weights_used")
        g_abs = sem("gla_abs_done")
        g_ln = sem("gla_ln_done")
        g_la = sem("gla_log_decay_ready")
        g_scan = sem("gla_decay_sum_ready")
        g_exp = sem("gla_decays_ready")
        g_kq = sem("gla_kq_ready")
        g_vps = sem("gla_v_done")
        g_v = sem("gla_v_ready")
        g_at = sem("gla_att_done")
        g_am = sem("gla_att_ready")
        g_kt = sem("gla_kt_done")
        g_ktm = sem("gla_kt_ready")
        g_sp = sem("gla_state_ready")
        g_sf = sem("gla_state_scaled")
        g_sps = sem("gla_update_done")
        g_ops = sem("gla_out_done")
        g_og = sem("gla_out_ready")
        g_sq = sem("gla_square_ready")
        g_rt = sem("gla_root_ready")
        g_kst = sem("gla_samplek_done")
        g_ksm = sem("gla_samplek_ready")
        g_vx = sem("gla_samplev_ready")
        g_out = sem("gla_outer_done")
        g_s1 = sem("gla_sample_state_ready")
        g_os = sem("gla_sample_out_done")
        g_stored = sem("gla_stored")
        g_head = sem("gla_head_done")
        pw = sem("pair_weights_loaded")
        pw_used = sem("pair_weights_used")
        p_start = sem("pair_buffers_free")
        cur = sem("pair_params_ready")
        ksq = sem("k_square_ready")
        ldr = sem("decay_sum_ready")
        ept = sem("decays_ready")
        rkr = sem("bonus_product_ready")
        gram_in = sem("gram_inputs_ready")
        tr_done = sem("transposes_done")
        tr_ready = sem("transposes_ready")
        gram_done = sem("gram_done")
        gram_ready = sem("gram_ready")
        inv_p = sem("inverse_LX_done")
        inv_pr = sem("inverse_LX_ready")
        inv_x = sem("inverse_XLX_done")
        inv_xr = sem("inverse_ready")
        rhs_done, rhs_ready = sem("rhs_done"), sem("rhs_ready")
        u_done, u_ready = sem("u_done"), sem("u_ready")
        s_done, s_ready, s_scaled = sem("state_update_done"), sem("state_ready"), sem("state_scaled")
        o_done, o_ready = sem("pair_out_done"), sem("pair_out_ready")
        cen_ready, var_sq = sem("centred_ready"), sem("centred_square_ready")
        s_stored = sem("pair_state_stored")
        state_new = sem("sample_state_ready")
        st_loaded = sem("sample_state_loaded")
        sv_done = sem("sample_values_transposed")
        sv_ready = sem("sample_values_ready")
        pool_step = sem("gpsimd_step")
        sa_step = sem("sample_vector_step")
        so_ready, so_done = sem("sample_out_ready"), sem("sample_out_transposed")
        osq_ready = sem("sample_root_ready")
        mg_ready = sem("merged_ready")
        h_loaded = sem("h_loaded")
        wo_loaded = [sem(f"wo_loaded{j}") for j in range(2)]
        wo_used = sem("wo_used")
        h_ready = sem("h_ready")
        sq2, sq2_used, rs2 = sem("ffn_square_ready"), sem("ffn_square_used"), sem("ffn_root_ready")
        xn2_ready = sem("ffn_input_ready")
        gu_loaded = [sem(f"gate_up_loaded{j}") for j in range(2)]
        gu_used = sem("gate_up_used")
        silu_ready = sem("silu_ready")
        act_ready = sem("activations_ready")
        wd_loaded = [sem(f"down_loaded{j}") for j in range(2)]
        wd_used = sem("down_used")
        y_ready = sem("h_final_ready")
        sq3, sq3_used, rs3 = sem("final_square_ready"), sem("final_square_used"), sem("final_root_ready")
        yn_ready = sem("y_ready")
        stored, shift_stored = sem("stored"), sem("shift_stored")

        J_NORM, J_LO, J_GLO = 1, 2, 3
        J_GLA, PER_GLA = 3, 6
        J_PAIR, PER_PAIR = J_GLA + GH * PER_GLA, 10
        J_WO = J_PAIR + NP * PER_PAIR
        J_N2 = J_WO + KT + 1
        J_FFN = J_N2
        J_DOWN = J_FFN + 2 * FT
        J_N3 = J_DOWN + KT + 1

        block = ctx.enter_context(nc.Block())

        @block.sync
        def _(sp):
            for kt in range(KT):
                sp.dma_start(XN[:, kt, 0:TS], xT[kt, :, :]).then_inc(x_loaded, 16)
            sp.dma_start(CON, consts[:, :]).then_inc(con_loaded, 16)
            sp.dma_start(N_WLO, w_lo.rearrange("p (k n) -> p k n", n=128)).then_inc(lo_w_loaded, 16)
            sp.dma_start(N_WGLO, w_glo.rearrange("p (k n) -> p k n", n=16)).then_inc(lo_w_loaded, 16)
            sp.dma_start(XN[:, :, TS:XC], prevT[:, :, :]).then_inc(par_loaded, 16)
            sp.dma_start(PAR[:, :, 0:10], par[:, :, :]).then_inc(par_loaded, 16)
            sp.dma_start(GAINS, gains[:, :, :]).then_inc(par_loaded, 16)
            sp.dma_start(MULO[:, 0:1], mu_lo[:, :]).then_inc(par_loaded, 16)
            sp.dma_start(GPAR, glapar[:, :]).then_inc(par_loaded, 16)
            with sp.Fori(0, GH) as h:
                sp.wait_ge(done[2], h * PER_GLA + (J_GLA - 1))
                sp.dma_start(WB, w_gla[h, :, :]).then_inc(gw_loaded, 16)
                sp.dma_start(GA2[0:16, :], w_gla2[h, :, :]).then_inc(gw_loaded, 16)
            sp.wait_ge(done[2], J_PAIR - 1)
            with sp.Fori(0, NP) as i:
                sp.wait_ge(done[2], i * PER_PAIR + (J_PAIR - 4))
                sp.dma_start(WB[:, 0:WP], w_pair[i, :, :]).then_inc(pw, 16)
            sp.wait_ge(p_start, NP + 1)
            sp.dma_start(S0.rearrange("p a b -> p (a b)"), wkv_s[:, :]).then_inc(st_loaded, 16)
            sp.wait_ge(state_new, 1)
            sp.dma_start(wkvs[:, :], S0.rearrange("p a b -> p (a b)")).then_inc(stored, 16)
            sp.wait_ge(mg_ready, 1)
            for m in range(2):
                sp.dma_start(WO[m], w_o[m, :, :].rearrange("p (k n) -> p k n", n=128)).then_inc(wo_loaded[m], 16)
            for kt in range(KT):
                sp.dma_start(H[:, kt, :], xT[kt, :, :]).then_inc(h_loaded, 16)
            with sp.Fori(0, KT // 2 - 1) as g:
                for j in range(2):
                    sp.wait_ge(done[2], g * 2 + (J_WO + 1 + j))
                    sp.dma_start(WO[j], w_o[g * 2 + (2 + j), :, :].rearrange("p (k n) -> p k n", n=128)
                                 ).then_inc(wo_loaded[j], 16)
            sp.wait_ge(done[2], J_WO + KT)
            for j in range(2):
                sp.dma_start(WGU[j].rearrange("p a k n -> p (a k n)"), w_gu[j, :, :]).then_inc(gu_loaded[j], 16)
            with sp.Fori(0, FT // 2 - 1) as g:
                for j in range(2):
                    sp.wait_ge(done[2], g * 4 + (J_FFN + 2 + 2 * j))
                    sp.dma_start(WGU[j].rearrange("p a k n -> p (a k n)"), w_gu[g * 2 + (2 + j), :, :]
                                 ).then_inc(gu_loaded[j], 16)
            sp.dma_start(WD[0].rearrange("p k n -> p (k n)"), w_d[0, :, :]).then_inc(wd_loaded[0], 16)
            sp.wait_ge(done[2], J_DOWN)
            sp.dma_start(WD[1].rearrange("p k n -> p (k n)"), w_d[1, :, :]).then_inc(wd_loaded[1], 16)
            with sp.Fori(0, KT // 2 - 1) as g:
                for j in range(2):
                    sp.wait_ge(done[2], g * 2 + (J_DOWN + 1 + j))
                    sp.dma_start(WD[j].rearrange("p k n -> p (k n)"), w_d[g * 2 + (2 + j), :, :]
                                 ).then_inc(wd_loaded[j], 16)
            for kt in range(KT):
                sp.wait_ge(yn_ready, kt + 1)
                sp.dma_start(yT[kt, :, :], H[:, kt, :]).then_inc(stored, 16)
            sp.wait_ge(g_stored, 32 * GH)
            sp.wait_ge(s_stored, 16 * NP)
            sp.wait_ge(shift_stored, 16)
            sp.wait_ge(stored, 16 * (1 + KT))

        @block.gpsimd
        def _(pool):
            pool.wait_ge(xn_ready, KT)
            pool.dma_start(shT[:, :, :], XN[:, :, T - 1:TS]).then_inc(shift_stored, 16)
            with pool.Fori(0, GH) as h:
                pool.wait_ge(g_head, h + 1)
                pool.nop(nofuse=True)
                pool.dma_start(GS0, gla_s[h, :, :].rearrange("p (b v) -> p b v", v=DV)).then_inc(gs_loaded, 16)
                pool.wait_ge(g_sp, h * (NG + 1) + (NG + 1))
                pool.nop(nofuse=True)
                pool.dma_start(glap[h, :, :], SP[0]).then_inc(g_stored, 16)
                pool.wait_ge(g_s1, h * NS + NS)
                pool.nop(nofuse=True)
                pool.dma_start(glas[h, :, :].rearrange("p (b v) -> p b v", v=DV), GS0).then_inc(g_stored, 16)
            with pool.Fori(0, NP) as i:
                pool.wait_ge(s_ready, i * (NC + 1) + (NC + 1))
                pool.nop(nofuse=True)
                pool.dma_start(wkvp[i, :, :], SS[0]).then_inc(s_stored, 16)
            pool.wait_ge(sv_ready, 12)
            nc.gpsimd.tensor_tensor(S1, QQ[:, Q_V, :].unsqueeze(2).to_broadcast([P, HD, HD]),
                                    QQ[:, Q_KP, :].unsqueeze(1).to_broadcast([P, HD, HD]), ALU.mult).then_inc(pool_step, 1)

        @block.tensor
        def _(pe):
            def mm(out, lhsT, rhs, start, stop):
                return nc.tensor.matmul(out, lhsT, rhs, start=start, stop=stop)

            def gate(s, value):
                pe.wait_ge(s, value)
                pe.nop(nofuse=True)

            def project(weight, src, blocks, before):
                for b, (c0, n) in enumerate(blocks):
                    gate(out_of[b], before)
                    for kt in range(KT):
                        last = mm(bank[b][0:weight(kt).shape[1], 0:n], weight(kt), src[:, kt, c0:c0 + n],
                                  kt == 0, kt == KT - 1)
                    last.then_inc(done[b], 1)

            pe.wait_ge(con_loaded, 16)
            for kt in range(KT):
                pe.wait_ge(sq_ready, kt + 1)
                for b, (c0, n) in enumerate(TB):
                    last = mm(bank[b][:, 0:n], ONES, N_SQ[kt % 2][:, c0:c0 + n], kt == 0, kt == KT - 1)
                    if kt == KT - 1:
                        last.then_inc(done[b], 1)
                    elif b == 2:
                        last.then_inc(sq_used, 1)
            pe.wait_ge(lo_w_loaded, 32)
            pe.wait_ge(xn_ready, KT)
            pe.wait_ge(par_loaded, 16 * 5)
            project(lambda kt: N_WLO[:, kt, :], XN, XB, J_NORM)
            project(lambda kt: N_WGLO[:, kt, :], XN, XB, J_LO)

            with pe.Fori(0, GH) as h:
                j0 = h * PER_GLA + J_GLA
                gate(gw_loaded, h * 32 + 32)
                gate(g_head, h + 1)
                for b, (c0, n) in enumerate(XT):
                    gate(out_of[b], j0)
                    mm(bank[b][:, 0:n], GA2[0:16, :], GLO[0:16, c0:c0 + n], True, True).then_inc(done[b], 1)
                for vt in range(VT):
                    project(lambda kt: WB[:, G_B + vt * 1024 + kt * 128:G_B + vt * 1024 + kt * 128 + 128],
                            XN, XT, j0 + (1 + vt))
                for tt in range(9):
                    rows = P if tt < 8 else NS
                    if tt >= 2:
                        gate(g_v, h * 9 + (tt - 1))
                    for kt in range(KT):
                        last = mm(bank[3 + tt % 2][0:rows, 0:DV], XN[:, kt, tt * P:tt * P + rows],
                                  WB[:, G_V + kt * DV:G_V + (kt + 1) * DV], kt == 0, kt == KT - 1)
                    last.then_inc(g_vps, 1)
                project(lambda kt: WB[:, G_K + kt * 128:G_K + kt * 128 + 128], XN, XT, j0 + 3)
                project(lambda kt: WB[:, G_Q + kt * 128:G_Q + kt * 128 + 128], XN, XT, j0 + 4)
                for q in range(2):
                    if q == 0:
                        gate(out_of[2], j0 + 4)
                    else:
                        gate(g_ktm, h * 2 + 1)
                    for c in range(4):
                        cc = 4 * q + c
                        last = nc.tensor.transpose(bank[5][:, c * CG:(c + 1) * CG],
                                                   GK_[:, cc * CG:(cc + 1) * CG], IDF)
                    last.then_inc(g_kt, 1)
                    if q == 0:
                        gate(out_of[2], j0 + 5)
                    else:
                        gate(g_am, h * 2 + 1)
                    for c in range(4):
                        cc = 4 * q + c
                        last = mm(bank[6][:, c * CG:(c + 1) * CG], GK_[:, cc * CG:(cc + 1) * CG],
                                  GQ_[:, cc * CG:(cc + 1) * CG], True, True)
                    last.then_inc(g_at, 1)
                gate(g_ktm, h * 2 + 2)
                gate(g_am, h * 2 + 2)
                gate(g_v, h * 9 + 9)
                for c in range(NG):
                    gate(g_sp, h * (NG + 1) + (c + 1))
                    mm(bank[4][:, 0:DV], KTM[:, c, :], VTM[:, c, :], True, True).then_inc(g_sps, 1)
                    if c:
                        gate(g_og, h * (NG + 1) + c)
                    for vt in range(VT):
                        mm(bank[7][:, vt * CG:(vt + 1) * CG], VTM[:, c, vt * P:(vt + 1) * P], ATT[:, c, :],
                           True, False)
                        last = mm(bank[7][:, vt * CG:(vt + 1) * CG], SP[c % 2][:, vt * P:(vt + 1) * P],
                                  GQ_[:, c * CG:(c + 1) * CG], False, True)
                    last.then_inc(g_ops, 1)
                mm(bank[3][0:NS, 0:P], GK_[:, T:TS], IDF, True, True).then_inc(g_kst, 1)
                gate(g_ksm, h + 1)
                gate(g_vx, h + 1)
                for q in range(4):
                    if q >= 2:
                        gate(g_s1, h * NS + (2 * q - 2))
                    mm(bank[3 + 2 * (q % 2)][:, :], GKS[0:NS, :],
                       VEXP[0:NS, 2 * q:2 * q + 2, :].rearrange("p a b -> p (a b)"), True, True).then_inc(g_out, 1)
                gate(g_s1, h * NS + NS)
                for b in range(NS):
                    for vt in range(VT):
                        last = mm(bank[6][:, vt * NS + b:vt * NS + b + 1], GS0[:, b, vt * P:(vt + 1) * P],
                                  GQ_[:, T + b:T + b + 1], True, True)
                last.then_inc(g_os, 1)
                gate(g_sq, h + 1)
                for b, (c0, n) in enumerate(TB):
                    gate(out_of[b], j0 + 5)
                    for vt in range(VT):
                        last = mm(bank[b][:, 0:n], ONES, GSQ[:, vt, c0:c0 + n], vt == 0, vt == VT - 1)
                    last.then_inc(done[b], 1)

            with pe.Fori(0, NP) as i:
                j0 = i * PER_PAIR + J_PAIR
                gate(pw, i * 16 + 16)
                gate(p_start, i + 1)
                for r0, job in ((0, 1), (64, 2)):
                    for b, (c0, n) in enumerate(XT):
                        gate(out_of[b], j0 + (job - 1))
                        mm(bank[b][:, 0:n], WB[r0:r0 + 64, W_LORA:W_LORA + 128], LO[r0:r0 + 64, c0:c0 + n],
                           True, True).then_inc(done[b], 1)
                for q, w in enumerate((W_K, W_R, W_V, W_G)):
                    for b, (c0, n) in enumerate(XT if w == W_G else XB):
                        gate(out_of[b], j0 + (2 + q))
                        for kt in range(KT):
                            last = mm(bank[b][:, 0:n], WB[:, w + kt * 128:w + kt * 128 + 128],
                                      XN[:, kt, c0:c0 + n], kt == 0, kt == KT - 1)
                        last.then_inc(done[b], 1)
                gate(ksq, i + 1)
                for b, (c0, n) in enumerate(TB):
                    gate(out_of[b], j0 + 6)
                    mm(bank[b][:, 0:n], BONES, EM[:, c0:c0 + n], True, True).then_inc(done[b], 1)
                gate(rkr, i + 1)
                for b, (c0, n) in enumerate(TB):
                    gate(out_of[b], j0 + 7)
                    mm(bank[b][:, 0:n], BONES, RK[:, c0:c0 + n], True, True).then_inc(done[b], 1)
                gate(gram_in, i * 4 + 4)
                for n_, (src, idn) in enumerate(((V, IDS), (KE, IDS), (BE, NIDS))):
                    for hf in range(2):
                        m = 2 * n_ + hf
                        if m >= 2:
                            gate(tr_ready, i * 6 + (m - 1))
                        for c in range(8):
                            for e in range(2):
                                r = slice(64 * e, 64 * e + 64)
                                last = mm(bank[6 + m % 2][r, c * CR:(c + 1) * CR],
                                          src[r, (8 * hf + c) * CR:(8 * hf + c + 1) * CR], idn[r, :], True, True)
                        last.then_inc(tr_done, 1)
                for q in range(4):
                    if q:
                        gate(gram_ready, i * 12 + 3 * q)
                    for g, src in ((3, BE), (4, KE)):
                        for c in range(4):
                            for e in range(2):
                                r = slice(64 * e, 64 * e + 64)
                                cc = 4 * q + c
                                last = mm(bank[g][r, c * 128:(c + 1) * 128], src[r, cc * CR:(cc + 1) * CR],
                                          AR[r, cc, :, :].rearrange("p a t -> p (a t)"), True, True)
                        last.then_inc(gram_done, 1)
                    for c in range(4):
                        for e in range(2):
                            r = slice(64 * e, 64 * e + 64)
                            cc = 4 * q + c
                            last = mm(bank[5][r, c * CR:(c + 1) * CR], AR[r, cc, 0, :],
                                      BE[r, cc * CR:(cc + 1) * CR], True, True)
                    last.then_inc(gram_done, 1)
                gate(tr_ready, i * 6 + 6)
                for lv in range(len(LEVELS)):
                    for hf in range(2):
                        if lv == 0:
                            gate(inv_xr, i * 12 + 2)
                        else:
                            gate(inv_xr, i * 12 + 2 + 2 * (lv - 1) + hf + 1)
                        for c in range(8):
                            for e in range(2):
                                r = slice(64 * e, 64 * e + 64)
                                last = mm(bank[3 + hf][r, c * CR:(c + 1) * CR], GT[r, 8 * hf + c, 0, :],
                                          X_[r, 8 * hf + c, :], True, True)
                        last.then_inc(inv_p, 1)
                    for hf in range(2):
                        gate(inv_pr, i * 10 + (2 * lv + hf + 1))
                        for c in range(8):
                            for e in range(2):
                                r = slice(64 * e, 64 * e + 64)
                                cc = 8 * hf + c
                                if lv < len(LEVELS) - 1:
                                    mm(bank[5 + hf][r, c * CR:(c + 1) * CR], Y[r, cc, :], PP[r, cc, :], True, True)
                                last = mm(bank[3 + hf][r, c * CR:(c + 1) * CR], PP[r, cc, :], Y[r, cc, :], True, True)
                        last.then_inc(inv_x, 1)
                gate(inv_xr, i * 12 + 12)
                for c in range(NC):
                    S = SS[c % 2]
                    gate(s_ready, i * (NC + 1) + (c + 1))
                    for e in range(2):
                        r = slice(64 * e, 64 * e + 64)
                        mm(bank[3][r, 0:HD], AK[r, c, 0, :], VTT[r, c, :], True, False)
                        last = mm(bank[3][r, 0:HD], AR[r, c, 0, :], S[r, :], False, True)
                    last.then_inc(rhs_done, 1)
                    gate(rhs_ready, i * NC + (c + 1))
                    for e in range(2):
                        r = slice(64 * e, 64 * e + 64)
                        last = mm(bank[4][r, 0:HD], Y[r, c, :], RH[r, :], True, True)
                    last.then_inc(u_done, 1)
                    gate(u_ready, i * NC + (c + 1))
                    for e in range(2):
                        r = slice(64 * e, 64 * e + 64)
                        mm(bank[5][r, 0:HD], KTT[r, c, :], VTT[r, c, :], True, False)
                        last = mm(bank[5][r, 0:HD], BTT[r, c, :], U[r, :], False, True)
                    last.then_inc(s_done, 1)
                    ob = bank[6 + c // 8]
                    for e in range(2):
                        r = slice(64 * e, 64 * e + 64)
                        cols = slice((c % 8) * CR, (c % 8 + 1) * CR)
                        mm(ob[r, cols], VTT[r, c, :], AK[r, c, 1, :], True, False)
                        mm(ob[r, cols], S[r, :], AR[r, c, 1, :], False, False)
                        last = mm(ob[r, cols], U[r, :], GT[r, c, 1, :], False, True)
                    last.then_inc(o_done, 1)
                gate(o_ready, i * 2 + 2)
                for b, (c0, n) in enumerate(PB):
                    gate(out_of[b], j0 + 8)
                    mm(bank[b][:, 0:n], BONES, O[:, c0:c0 + n], True, True).then_inc(done[b], 1)
                gate(var_sq, i + 1)
                for b, (c0, n) in enumerate(PB):
                    gate(out_of[b], j0 + 9)
                    mm(bank[b][:, 0:n], BONES, KA[:, c0:c0 + n], True, True).then_inc(done[b], 1)

            pe.wait_ge(p_start, NP + 1)
            for g in range(3):
                last = nc.tensor.transpose(bank[3][:, g * P:(g + 1) * P],
                                           SV[:, 2 * g:2 * g + 2, :, :].rearrange("p a b c -> p (a b c)"), IDF)
            last.then_inc(sv_done, 1)
            pe.wait_ge(so_ready, 2)
            mm(bank[4][:, 0:64], O2[0:64, :], CON[0:64, C_ID:C_ID + 64], True, True).then_inc(so_done, 1)

            pe.wait_ge(mg_ready, 1)
            with pe.Fori(0, KT // 2) as g:
                for j in range(2):
                    gate(wo_loaded[j], g * 16 + 16)
                    for b, (c0, n) in enumerate(TB):
                        gate(out_of[b], g * 2 + (J_WO + j))
                        for kt in range(KT):
                            last = mm(bank[b][:, 0:n], WO[j][:, kt, :], MG[:, kt, c0:c0 + n], kt == 0, kt == KT - 1)
                        last.then_inc(done[b], 1)

            def mean_square(sq, used, bufs, before):
                for kt in range(KT):
                    pe.wait_ge(sq, kt + 1)
                    for b, (c0, n) in enumerate(TB):
                        if kt == 0:
                            pe.wait_ge(out_of[b], before)
                        last = mm(bank[b][:, 0:n], ONES, bufs[kt % 2][:, c0:c0 + n], kt == 0, kt == KT - 1)
                        if kt == KT - 1:
                            last.then_inc(done[b], 1)
                        elif b == 2:
                            last.then_inc(used, 1)

            mean_square(sq2, sq2_used, F_SQ, J_N2 - 1)
            pe.wait_ge(xn2_ready, KT)
            with pe.Fori(0, FT // 2) as g:
                for j in range(2):
                    gate(gu_loaded[j], g * 16 + 16)
                    for q in range(2):
                        for b, (c0, n) in enumerate(TB):
                            gate(out_of[b], g * 4 + (J_FFN + 2 * j + q))
                            for kt in range(KT):
                                last = mm(bank[b][:, 0:n],
                                          WGU[j][:, q, kt, :], XN2[:, kt, c0:c0 + n], kt == 0, kt == KT - 1)
                            last.then_inc(done[b], 1)
            with pe.Fori(0, KT // 2) as g:
                for j in range(2):
                    gate(wd_loaded[j], g * 16 + 16)
                    for b, (c0, n) in enumerate(TB):
                        gate(out_of[b], g * 2 + (J_DOWN + j))
                        for kt in range(FT):
                            last = mm(bank[b][:, 0:n], WD[j][:, kt, :], ACTV[:, kt, c0:c0 + n], kt == 0, kt == FT - 1)
                        last.then_inc(done[b], 1)
            mean_square(sq3, sq3_used, Y_SQ, J_N3 - 1)

        @block.scalar
        def _(act):
            def f(out, in_, func, bias=0.0, scale=1.0):
                return nc.scalar.activation(out, in_, func, bias=bias, scale=scale)

            for kt in range(KT):
                if kt == 0:
                    act.wait_ge(x_loaded, 16 * KT)
                if kt >= 2:
                    act.wait_ge(sq_used, kt - 1)
                f(N_SQ[kt % 2], XN[:, kt, 0:TS], ACT.Square).then_inc(sq_ready, 1)
            act.wait_ge(con_loaded, 16)
            act.wait_ge(par_loaded, 16 * 5)
            for b, (c0, n) in enumerate(TB):
                act.wait_ge(done[b], J_NORM)
                f(N_RS[:, c0:c0 + n], bank[b][:, 0:n], ACT.Sqrt, EPS[0], 1.0 / D).then_inc(out_of[b], 1)
            for b, (c0, n) in enumerate(XB):
                act.wait_ge(done[b], J_LO)
                f(N_T0[:, 1 + c0:1 + c0 + n], bank[b][:, 0:n], ACT.Copy, scale=MULO[:, 0:1]).then_inc(mu_ready, 1)
            for b, (c0, n) in enumerate(XB):
                act.wait_ge(done[b], J_GLO)
                nc.scalar.copy(GLO[0:16, c0:c0 + n], bank[b][0:16, 0:n]).then_inc(out_of[b], 1)
            act.wait_ge(lo_ready, 1)
            f(LO[0:64, 0:TS], LO[0:64, 0:TS], ACT.Tanh).then_inc(a_step, 1)


            with act.Fori(0, GH) as h:
                j0 = h * PER_GLA + J_GLA
                act.wait_ge(g_head, h + 1)
                for b, (c0, n) in enumerate(XT):
                    act.wait_ge(done[b], j0 + 1)
                    f(E0[:, c0:c0 + n], bank[b][:, 0:n], ACT.Abs, GCUR).then_inc(g_abs, 1)
                act.wait_ge(g_abs, h * 3 + 3)
                f(E0, E0, ACT.Exp, scale=-1.0).then_inc(a_step, 1)
                act.wait_ge(a_step, h + 2)
                f(E0, E0, ACT.Ln, bias=1.0).then_inc(g_ln, 1)
                for vt in range(VT):
                    for b, (c0, n) in enumerate(XT):
                        act.wait_ge(done[b], j0 + (2 + vt))
                        f(TGB[:, vt, c0:c0 + n], bank[b][:, 0:n], ACT.Tanh, scale=0.5).then_inc(out_of[b], 1)
                act.wait_ge(g_scan, h + 1)
                f(EPG, GB, ACT.Exp, scale=1.0 / GATE_NORM).then_inc(g_exp, 1)
                f(EMG, GB, ACT.Exp, scale=-1.0 / GATE_NORM).then_inc(g_exp, 1)
                f(GDM, GDE, ACT.Exp, scale=1.0 / GATE_NORM).then_inc(g_exp, 1)
                f(GAS, LA[:, T:TS], ACT.Exp, scale=1.0 / GATE_NORM).then_inc(g_exp, 1)
                for tt in range(9):
                    rows = P if tt < 8 else NS
                    act.wait_ge(g_vps, h * 9 + (tt + 1))
                    nc.scalar.copy(VTM[0:rows, tt, :], bank[3 + tt % 2][0:rows, 0:DV]).then_inc(g_v, 1)
                for q in range(2):
                    act.wait_ge(g_kt, h * 2 + (q + 1))
                    nc.scalar.copy(KTM[:, 4 * q:4 * q + 4, :].rearrange("p a b -> p (a b)"), bank[5][:, :]).then_inc(g_ktm, 1)
                for c in range(NG):
                    act.wait_ge(g_sp, h * (NG + 1) + (c + 1))
                    f(SF, SP[c % 2], ACT.Copy, scale=GF[:, c:c + 1]).then_inc(g_sf, 1)
                    act.wait_ge(g_ops, h * NG + (c + 1))
                    nc.scalar.copy(OG[:, :, c * CG:(c + 1) * CG],
                                   bank[7][:, 0:DV].rearrange("p (a b) -> p a b", b=CG)).then_inc(g_og, 1)
                act.wait_ge(g_kst, h + 1)
                nc.scalar.copy(GKS[0:NS, :], bank[3][0:NS, 0:P]).then_inc(g_ksm, 1)
                act.wait_ge(g_os, h + 1)
                nc.scalar.copy(OG[:, :, T:TS], bank[6][:, 0:VT * NS].rearrange("p (a b) -> p a b", b=NS)).then_inc(g_og, 1)
                act.wait_ge(g_og, h * (NG + 1) + NG + 1)
                f(GSQ, OG, ACT.Square).then_inc(g_sq, 1)
                for b, (c0, n) in enumerate(TB):
                    act.wait_ge(done[b], j0 + 6)
                    f(E0[:, c0:c0 + n], bank[b][:, 0:n], ACT.Sqrt, EPS[2], 1.0 / DV).then_inc(out_of[b], 1)

            with act.Fori(0, NP) as i:
                j0 = i * PER_PAIR + J_PAIR
                act.wait_ge(p_start, i + 1)
                for dst, bias, job in ((LD, P_HW0, 1), (A, P_HA0, 2)):
                    for b, (c0, n) in enumerate(XT):
                        act.wait_ge(done[b], j0 + job)
                        f(dst[:, c0:c0 + n], bank[b][:, 0:n], ACT.Tanh, CUR[:, bias:bias + 1], 0.5).then_inc(out_of[b], 1)
                for q, mu in enumerate((P_MUK, P_MUR, P_MUV)):
                    for b, (c0, n) in enumerate(XB):
                        act.wait_ge(done[b], j0 + (3 + q))
                        if q == 2 and b == 0:
                            act.wait_ge(out_of[2], j0 + 3)
                        f(T0[q % 2][:, 1 + c0:1 + c0 + n], bank[b][:, 0:n], ACT.Copy, scale=CUR[:, mu:mu + 1]
                          ).then_inc(mu_ready, 1)
                    if q == 0:
                        act.wait_ge(out_of[2], j0 + 3)
                        f(EM, K, ACT.Square, scale=CUR[:, P_KK:P_KK + 1]).then_inc(ksq, 1)
                for b, (c0, n) in enumerate(XT):
                    act.wait_ge(done[b], j0 + 6)
                    f(TG[:, c0:c0 + n], bank[b][:, 0:n], ACT.Tanh, scale=0.5).then_inc(out_of[b], 1)
                for b, (c0, n) in enumerate(TB):
                    act.wait_ge(done[b], j0 + 7)
                    f(O[:, c0:c0 + n], bank[b][:, 0:n], ACT.Sqrt).then_inc(out_of[b], 1)
                act.wait_ge(ldr, i + 1)
                f(EP[:, :, 1:65], B.rearrange("p (c t) -> p c t", t=CR), ACT.Exp).then_inc(ept, 1)
                f(EM[:, 0:T], B, ACT.Exp, scale=-1.0).then_inc(ept, 1)
                f(SV[:, Q_W, i, :], LD[:, T:TS], ACT.Exp).then_inc(ept, 1)
                act.wait_ge(gram_in, i * 4 + 4)
                for n_, dst in enumerate((VTT, KTT, BTT)):
                    for hf in range(2):
                        m = 2 * n_ + hf
                        act.wait_ge(tr_done, i * 6 + (m + 1))
                        nc.scalar.copy(dst[:, 8 * hf:8 * hf + 8, :].rearrange("p a b -> p (a b)"),
                                       bank[6 + m % 2][:, :]).then_inc(tr_ready, 1)
                for c in range(NC):
                    act.wait_ge(s_ready, i * (NC + 1) + (c + 1))
                    f(SD, SS[c % 2], ACT.Copy, scale=EP[:, c, 64:65]).then_inc(s_scaled, 1)
                    if c % 8 == 7:
                        act.wait_ge(o_done, i * NC + (c + 1))
                        nc.scalar.copy(O[:, (c - 7) * CR:(c + 1) * CR], bank[6 + c // 8][:, :]).then_inc(o_ready, 1)
                act.wait_ge(out_of[2], j0 + 9)
                f(KA[:, 0:T], O[:, 0:T], ACT.Square).then_inc(var_sq, 1)
                for b, (c0, n) in enumerate(PB):
                    act.wait_ge(done[b], j0 + 10)
                    f(KP[:, c0:c0 + n], bank[b][:, 0:n], ACT.Sqrt, EPS[1],
                      1.0 / HD).then_inc(out_of[b], 1)

            act.wait_ge(sv_done, 1)
            for g in range(3):
                for q in range(2):
                    for e in range(2):
                        nc.scalar.copy(QQ[64 * e:64 * e + 64, 2 * g + q, :],
                                       bank[3][64 * q:64 * q + 64, g * P + 64 * e:g * P + 64 * e + 64]).then_inc(sv_ready, 1)
            act.wait_ge(sa_step, 1)
            f(ST[:, 4:5], ST[:, 3:4], ACT.Sqrt, EPS[1], 1.0 / HD).then_inc(osq_ready, 1)
            act.wait_ge(so_done, 1)
            nc.scalar.copy(SO.rearrange("p a b -> p (a b)"), bank[4][:, 0:64]).then_inc(a_step, 1)

            def squares(bufs, ready, used, job):
                for kt in range(KT):
                    act.wait_ge(out_of[2], job + kt + 1)
                    if kt >= 2:
                        act.wait_ge(used, kt - 1)
                    f(bufs[kt % 2], H[:, kt, :], ACT.Square).then_inc(ready, 1)

            def roots(dst, job):
                for b, (c0, n) in enumerate(TB):
                    act.wait_ge(done[b], job)
                    f(dst[:, c0:c0 + n], bank[b][:, 0:n], ACT.Sqrt, EPS[0], 1.0 / D).then_inc(out_of[b], 1)

            squares(F_SQ, sq2, sq2_used, J_WO)
            roots(F_RS, J_N2)
            with act.Fori(0, FT) as ft:
                for b, (c0, n) in enumerate(TB):
                    act.wait_ge(done[b], ft * 2 + (J_FFN + 1))
                    f(ACTV[:, ft, c0:c0 + n], bank[b][:, 0:n], ACT.Silu).then_inc(out_of[b], 1)
            act.wait_ge(done[2], J_DOWN)
            squares(Y_SQ, sq3, sq3_used, J_DOWN)
            roots(Y_RS, J_N3)

        @block.vector
        def _(dve):
            V_ = nc.vector
            steps = [0]

            def step(ins):
                ins.then_inc(v_step, 1)
                steps[0] += 1
                dve.wait_ge(v_step, steps[0])

            def loop_step(i, per):
                base, n = steps[0], [0]

                def inner(ins):
                    ins.then_inc(v_step, 1)
                    n[0] += 1
                    dve.wait_ge(v_step, i * per + (base + n[0]))

                def end(passes):
                    assert n[0] == per, n[0]
                    steps[0] = base + per * passes
                return inner, end

            def over(a, n):
                return a.unsqueeze(1).to_broadcast([a.shape[0], n, a.shape[1]])

            def each(a, n):
                return a.unsqueeze(2).to_broadcast([a.shape[0], a.shape[1], n])

            dve.wait_ge(par_loaded, 16 * 5)
            dve.wait_ge(con_loaded, 16)
            V_.tensor_scalar(PAR[:, :, P_CMUR:P_CMUR + 3], PAR[:, :, P_MUR:P_MUR + 3], -1.0, 1.0, ALU.mult, ALU.add)
            V_.tensor_scalar(PAR[:, :, P_HW0:P_HW0 + 2], PAR[:, :, P_W0:P_W0 + 2], 0.5, None, ALU.mult)
            V_.tensor_scalar(PAR[:, :, P_CKA:P_CKA + 1], PAR[:, :, P_KA:P_KA + 1], -1.0, 1.0, ALU.mult, ALU.add)
            V_.tensor_scalar(MULO[:, 1:2], MULO[:, 0:1], -1.0, 1.0, ALU.mult, ALU.add)
            step(V_.memset(N_T0[:, 0:1], 0.0))
            for b in range(3):
                dve.wait_ge(out_of[b], J_NORM)
            step(V_.reciprocal(N_RS, N_RS))
            for kt in range(KT):
                V_.scalar_tensor_tensor(XN[:, kt, 0:TS], XN[:, kt, 0:TS], GAINS[:, 0, kt:kt + 1], N_RS,
                                        ALU.mult, ALU.mult).then_inc(xn_ready, 1)

            def shift(dst, t0, rest, ready, job):
                for b, (c0, n) in enumerate(XB):
                    dve.wait_ge(mu_ready, ready(b))
                    m = min(n, T - c0)
                    ins = V_.scalar_tensor_tensor(dst[:, c0:c0 + m], bank[b][:, 0:m], rest, t0[:, c0:c0 + m],
                                                  ALU.mult, ALU.add)
                    if b == 2:
                        ins = V_.scalar_tensor_tensor(dst[:, T:TS], bank[b][:, T - c0:TS - c0], rest,
                                                      t0[:, 1 + TS:1 + XC], ALU.mult, ALU.add)
                    ins.then_inc(out_of[b], 1)

            shift(LO, N_T0, MULO[:, 1:2], lambda b: b + 1, J_LO)
            dve.wait_ge(out_of[2], J_LO)
            step(V_.memset(ATT[:, 0:1, 0:1], 0.0))
            V_.memset(GDE, 0.0).then_inc(lo_ready, 1)

            for b in range(3):
                dve.wait_ge(out_of[b], J_GLO)
            step(V_.memset(ATT.rearrange("p a b -> p (a b)"), 0.0))
            with dve.Fori(0, GH) as h:
                st, end = loop_step(h, 10)
                j0 = h * PER_GLA + J_GLA
                V_.memset(SP[0], 0.0).then_inc(g_sp, 1)
                V_.tensor_copy(GCUR, GPAR[:, bass.ds(h, 1)]).then_inc(g_head, 1)
                dve.wait_ge(g_head, h + 1)
                for b, (c0, n) in enumerate(XT):
                    dve.wait_ge(g_abs, h * 3 + (b + 1))
                    V_.tensor_scalar(LA[:, c0:c0 + n], bank[b][:, 0:n], GCUR, 0.0, ALU.add, ALU.min).then_inc(out_of[b], 1)
                dve.wait_ge(out_of[2], j0 + 1)
                dve.wait_ge(g_ln, h + 1)
                st(V_.tensor_tensor(LA, LA, E0, ALU.subtract))
                st(V_.tensor_tensor_scan(GB, CON[:, C_RG:C_RG + T], LA[:, 0:T], 0.0, ALU.mult, ALU.add))
                B3 = GB.rearrange("p (c t) -> p c t", t=CG)
                st(V_.tensor_copy(GDE, B3[:, :, CG // 2 - 1]))
                V_.tensor_tensor(B3, B3, each(GDE, CG), ALU.subtract).then_inc(g_scan, 1)
                dve.wait_ge(g_exp, h * 4 + 4)
                E3 = EPG.rearrange("p (c t) -> p c t", t=CG)
                st(V_.tensor_copy(GF[:, NG - 1:NG], E3[:, NG - 1, CG - 1:CG]))
                st(V_.tensor_tensor(GF[:, 0:NG - 1], E3[:, 0:NG - 1, CG - 1], GDM[:, 1:NG], ALU.mult))
                for b, (c0, n) in enumerate(XT):
                    dve.wait_ge(done[b], j0 + 4)
                    m = min(n, T - c0)
                    ins = V_.tensor_tensor(GK_[:, c0:c0 + m], bank[b][:, 0:m], EMG[:, c0:c0 + m], ALU.mult)
                    if b == 2:
                        ins = V_.tensor_copy(GK_[:, T:TS], bank[b][:, T - c0:TS - c0])
                    ins.then_inc(out_of[b], 1)
                for b, (c0, n) in enumerate(XT):
                    dve.wait_ge(done[b], j0 + 5)
                    m = min(n, T - c0)
                    ins = V_.scalar_tensor_tensor(GQ_[:, c0:c0 + m], bank[b][:, 0:m], DK ** -0.5, EPG[:, c0:c0 + m],
                                                  ALU.mult, ALU.mult)
                    if b == 2:
                        ins = V_.tensor_scalar(GQ_[:, T:TS], bank[b][:, T - c0:TS - c0], DK ** -0.5, None, ALU.mult)
                    ins.then_inc(out_of[b], 1)
                for q in range(2):
                    dve.wait_ge(g_at, h * 2 + (q + 1))
                    dve.nop(nofuse=True)
                    V_.copy_predicated(ATT[:, 4 * q:4 * q + 4, :],
                                       over(CON[:, C_CAUSAL:C_CAUSAL + CG].bitcast(I32), 4),
                                       bank[6][:, :].rearrange("p (a b) -> p a b", b=CG)).then_inc(g_am, 1)
                for c in range(NG):
                    dve.wait_ge(g_sps, h * NG + (c + 1))
                    dve.wait_ge(g_sf, h * NG + (c + 1))
                    V_.scalar_tensor_tensor(SP[(c + 1) % 2], bank[4][:, 0:DV], GF[:, c:c + 1], SF,
                                            ALU.mult, ALU.add).then_inc(g_sp, 1)
                dve.wait_ge(g_v, h * 9 + 9)
                V_.tensor_tensor(VEXP[0:NS, :, :], over(VTM[0:NS, 8, :], NS), each(CON[0:NS, C_DELTA:C_DELTA + NS], DV),
                                 ALU.mult).then_inc(g_vx, 1)
                dve.wait_ge(gs_loaded, h * 16 + 16)
                for q in range(4):
                    dve.wait_ge(g_out, h * 4 + (q + 1))
                    for j in range(2):
                        b = 2 * q + j
                        V_.scalar_tensor_tensor(GS0[:, b, :], GS0[:, b, :], GAS[:, b:b + 1],
                                                bank[3 + 2 * (q % 2)][:, j * DV:(j + 1) * DV],
                                                ALU.mult, ALU.add).then_inc(g_s1, 1)
                for b in range(3):
                    dve.wait_ge(out_of[b], j0 + 6)
                st(V_.reciprocal(E0, E0))
                for vt in range(VT):
                    st(V_.scalar_tensor_tensor(OG[:, vt, :], OG[:, vt, :], GPAR[:, GH + vt:GH + vt + 1], E0,
                                               ALU.mult, ALU.mult))
                    st(V_.scalar_tensor_tensor(MG[:, h * 2 + vt, :], TGB[:, vt, :], 1.0, OG[:, vt, :],
                                               ALU.add, ALU.mult))
                dve.wait_ge(g_stored, h * 32 + 32)
                end(GH)

            step(V_.memset(EP[:, :, 0:1], 1.0))
            with dve.Fori(0, NP) as i:
                st, end = loop_step(i, 20)
                j0 = i * PER_PAIR + J_PAIR
                mu0 = i * 9 + 3
                V_.memset(T0[0][:, 0:1], 0.0)
                V_.memset(T0[1][:, 0:1], 0.0)
                V_.memset(SS[0], 0.0).then_inc(s_ready, 1)
                V_.tensor_copy(CUR[:, 0:NPAR], PAR[:, i, :]).then_inc(p_start, 1)
                dve.wait_ge(p_start, i + 1)
                dve.wait_ge(s_ready, i * (NC + 1) + 1)

                def par1(j):
                    return CUR[:, j:j + 1]

                for b in range(3):
                    dve.wait_ge(out_of[b], j0 + 1)
                st(V_.tensor_scalar(LD, LD, -HALF_DECAY, -HALF_DECAY, ALU.mult, ALU.add))
                V_.tensor_tensor_scan(B, CON[:, C_RR:C_RR + T], LD[:, 0:T], 0.0, ALU.mult, ALU.add).then_inc(ldr, 1)
                for b in range(3):
                    dve.wait_ge(out_of[b], j0 + 2)
                st(V_.tensor_scalar(A, A, 0.5, 0.5, ALU.mult, ALU.add))
                shift(K, T0[0], par1(P_CMUK), lambda b: mu0 + (b + 1), None)
                dve.wait_ge(out_of[2], j0 + 3)
                st(V_.tensor_scalar(KP, A, par1(P_KA), par1(P_CKA), ALU.mult, ALU.add))
                st(V_.tensor_tensor(KP, KP, K, ALU.mult))
                shift(R, T0[1], par1(P_CMUR), lambda b: mu0 + (4 + b), None)
                dve.wait_ge(out_of[2], j0 + 4)
                V_.scalar_tensor_tensor(RK, R, par1(P_RK), KP, ALU.mult, ALU.mult).then_inc(rkr, 1)
                shift(V, T0[0], par1(P_CMUV), lambda b: mu0 + (7 + b), None)
                for b in range(3):
                    dve.wait_ge(out_of[b], j0 + 7)
                st(V_.tensor_scalar(O, O, 1e-12, None, ALU.max))
                st(V_.reciprocal(O, O))
                st(V_.scalar_tensor_tensor(KK, K, par1(P_KK), O, ALU.mult, ALU.mult))
                st(V_.tensor_tensor(KA, KK, A, ALU.mult))
                for q, src in ((Q_R, R), (Q_KP, KP), (Q_V, V), (Q_KK, KK), (Q_KA, KA)):
                    V_.tensor_copy(SV[:, q, i, :], src[:, T:TS])
                dve.wait_ge(ept, i * 3 + 3)
                KK3 = KK[:, 0:T].rearrange("p (c t) -> p c t", t=CR)
                R3 = R[:, 0:T].rearrange("p (c t) -> p c t", t=CR)
                V_.tensor_tensor(AR[:, :, 0, :], KK3, EP[:, :, 0:CR], ALU.mult).then_inc(gram_in, 1)
                V_.tensor_tensor(AR[:, :, 1, :], R3, EP[:, :, 1:CR + 1], ALU.mult).then_inc(gram_in, 1)
                V_.tensor_tensor(BE, KA[:, 0:T], EM[:, 0:T], ALU.mult).then_inc(gram_in, 1)
                V_.tensor_tensor(KE, KP[:, 0:T], EM[:, 0:T], ALU.mult).then_inc(gram_in, 1)
                for b, (c0, n) in enumerate(TB):
                    dve.wait_ge(done[b], j0 + 8)
                    V_.tensor_tensor(RK[:, c0:c0 + n], bank[b][:, 0:n], V[:, c0:c0 + n], ALU.mult).then_inc(out_of[b], 1)
                for q in range(4):
                    cs = slice(4 * q, 4 * q + 4)
                    for g, dst, m0 in ((3, GT, C_MG), (4, AK, C_MK)):
                        dve.wait_ge(gram_done, i * 12 + (3 * q + g - 2))
                        V_.tensor_tensor(dst[:, cs, :, :].rearrange("p c a t -> p c (a t)"),
                                         bank[g][:, :].rearrange("p (c t) -> p c t", t=2 * CR),
                                         over(CON[:, m0:m0 + 2 * CR], 4), ALU.mult).then_inc(gram_ready, 1)
                    dve.wait_ge(gram_done, i * 12 + (3 * q + 3))
                    V_.tensor_tensor(LL[:, cs, :], bank[5][:, 0:4 * CR].rearrange("p (c t) -> p c t", t=CR),
                                     over(CON[:, C_ML:C_ML + CR], 4), ALU.mult).then_inc(gram_ready, 1)
                dve.wait_ge(gram_ready, i * 12 + 12)
                st(V_.tensor_tensor(PP, LL, over(CON[:, C_M2:C_M2 + CR], NC), ALU.mult))
                V_.tensor_tensor(X_, over(IDS, NC), PP, ALU.subtract).then_inc(inv_xr, 1)
                dve.wait_ge(inv_xr, i * 12 + 1)
                st(V_.tensor_tensor(PP, GT[:, :, 0, :], over(CON[:, C_M2T:C_M2T + CR], NC), ALU.mult))
                V_.tensor_tensor(Y, over(IDS, NC), PP, ALU.subtract).then_inc(inv_xr, 1)
                dve.wait_ge(inv_xr, i * 12 + 2)
                for lv in range(len(LEVELS)):
                    off = CON[:, C_OFF + 64 * lv:C_OFF + 64 * lv + 64]
                    for hf in range(2):
                        cs = slice(8 * hf, 8 * hf + 8)
                        dve.wait_ge(inv_p, i * 10 + (2 * lv + hf + 1))
                        V_.tensor_tensor(PP[:, cs, :], bank[3 + hf][:, :].rearrange("p (c t) -> p c t", t=CR),
                                         over(off, 8), ALU.mult).then_inc(inv_pr, 1)
                    for hf in range(2):
                        cs = slice(8 * hf, 8 * hf + 8)
                        dve.wait_ge(inv_x, i * 10 + (2 * lv + hf + 1))
                        if lv < len(LEVELS) - 1:
                            V_.tensor_tensor(X_[:, cs, :], X_[:, cs, :],
                                             bank[5 + hf][:, :].rearrange("p (c t) -> p c t", t=CR), ALU.subtract)
                        V_.tensor_tensor(Y[:, cs, :], Y[:, cs, :],
                                         bank[3 + hf][:, :].rearrange("p (c t) -> p c t", t=CR),
                                         ALU.subtract).then_inc(inv_xr, 1)
                for c in range(NC):
                    dve.wait_ge(rhs_done, i * NC + (c + 1))
                    V_.tensor_copy(RH, bank[3][:, 0:HD]).then_inc(rhs_ready, 1)
                    dve.wait_ge(u_done, i * NC + (c + 1))
                    V_.tensor_copy(U, bank[4][:, 0:HD]).then_inc(u_ready, 1)
                    dve.wait_ge(s_done, i * NC + (c + 1))
                    dve.wait_ge(s_scaled, i * NC + (c + 1))
                    V_.scalar_tensor_tensor(SS[(c + 1) % 2], bank[5][:, 0:HD], EP[:, c, CR:CR + 1], SD,
                                            ALU.mult, ALU.add).then_inc(s_ready, 1)
                dve.wait_ge(o_ready, i * 2 + 2)
                for b, (c0, n) in enumerate(PB):
                    dve.wait_ge(done[b], j0 + 9)
                    V_.scalar_tensor_tensor(O[:, c0:c0 + n], bank[b][:, 0:n], -1.0 / HD, O[:, c0:c0 + n],
                                            ALU.mult, ALU.add).then_inc(out_of[b], 1)
                for b in range(3):
                    dve.wait_ge(out_of[b], j0 + 10)
                st(V_.reciprocal(KP[:, 0:T], KP[:, 0:T]))
                st(V_.tensor_tensor(O[:, 0:T], O[:, 0:T], KP[:, 0:T], ALU.mult))
                st(V_.tensor_scalar(O[:, 0:T], O[:, 0:T], par1(P_LNG), par1(P_LNB), ALU.mult, ALU.add))
                st(V_.tensor_tensor(O[:, 0:T], O[:, 0:T], RK[:, 0:T], ALU.add))
                st(V_.scalar_tensor_tensor(O[:, 0:T], TG[:, 0:T], 1.0, O[:, 0:T], ALU.add, ALU.mult))
                st(V_.tensor_tensor(MG[:, i, 0:T], MG[:, i, 0:T], O[:, 0:T], ALU.add))
                st(V_.tensor_copy(STG[:, i, :], TG[:, T:TS]))
                st(V_.tensor_copy(SB[:, i, :], RK[:, T:TS]))
                st(V_.memset(ST, 0.0))
                dve.wait_ge(s_stored, i * 16 + 16)
                st(V_.memset(ST, 0.0))
                end(NP)
            V_.memset(ST, 0.0).then_inc(p_start, 1)

            dve.wait_ge(sv_ready, 12)
            dve.wait_ge(st_loaded, 16)

            def vec(q):
                return QQ[:, q, :]

            step(V_.tensor_tensor(S2, S0, over(vec(Q_KK), HD), ALU.mult))
            step(V_.tensor_reduce(SA, S2, AX_X, ALU.add))
            step(V_.tensor_tensor(S2, each(SA, HD), over(vec(Q_KA), HD), ALU.mult))
            step(V_.tensor_tensor(S0, S0, over(vec(Q_W), HD), ALU.mult))
            step(V_.tensor_tensor(S0, S0, S2, ALU.subtract))
            dve.wait_ge(pool_step, 1)
            V_.tensor_tensor(S0, S0, S1, ALU.add).then_inc(state_new, 1)
            dve.wait_ge(state_new, 1)
            step(V_.tensor_tensor(S2, S0, over(vec(Q_R), HD), ALU.mult))
            step(V_.tensor_reduce(OO, S2, AX_X, ALU.add))
            step(V_.tensor_reduce(ST[:, 0:1], OO, AX_X, ALU.add))
            step(V_.tensor_scalar(ST[:, 1:2], ST[:, 0:1], 1.0 / HD, None, ALU.mult))
            step(V_.tensor_scalar(OO, OO, ST[:, 1:2], None, ALU.subtract))
            step(V_.tensor_tensor(OSQ, OO, OO, ALU.mult))
            V_.tensor_reduce(ST[:, 3:4], OSQ, AX_X, ALU.add).then_inc(sa_step, 1)
            dve.wait_ge(osq_ready, 1)
            step(V_.reciprocal(ST[:, 5:6], ST[:, 4:5]))
            for e in range(2):
                V_.tensor_scalar(O2[0:64, e * HD:(e + 1) * HD], OO[64 * e:64 * e + 64, :],
                                 ST[64 * e:64 * e + 64, 5:6], None, ALU.mult).then_inc(so_ready, 1)
            dve.wait_ge(a_step, 2 + GH)
            step(V_.tensor_tensor(SO, SO, each(PAR[:, :, P_LNG], NS), ALU.mult))
            step(V_.tensor_tensor(SO, SO, each(PAR[:, :, P_LNB], NS), ALU.add))
            step(V_.tensor_tensor(SO, SO, SB, ALU.add))
            step(V_.scalar_tensor_tensor(SO, STG, 1.0, SO, ALU.add, ALU.mult))
            V_.tensor_tensor(MG[:, :, T:TS], MG[:, :, T:TS], SO, ALU.add).then_inc(mg_ready, 1)

            dve.wait_ge(h_loaded, 16 * KT)
            with dve.Fori(0, KT) as m:
                for b, (c0, n) in enumerate(TB):
                    dve.wait_ge(done[b], m + (J_WO + 1))
                    V_.scalar_tensor_tensor(H[:, m, c0:c0 + n], bank[b][:, 0:n], 0.5, H[:, m, c0:c0 + n],
                                            ALU.mult, ALU.add).then_inc(out_of[b], 1)
            for b in range(3):
                dve.wait_ge(out_of[b], J_N2)
            step(V_.reciprocal(F_RS, F_RS))
            for kt in range(KT):
                V_.scalar_tensor_tensor(XN2[:, kt, :], H[:, kt, :], GAINS[:, 1, kt:kt + 1], F_RS,
                                        ALU.mult, ALU.mult).then_inc(xn2_ready, 1)
            with dve.Fori(0, FT) as ft:
                for b, (c0, n) in enumerate(TB):
                    dve.wait_ge(out_of[b], ft * 2 + (J_FFN + 1))
                    dve.wait_ge(done[b], ft * 2 + (J_FFN + 2))
                    V_.tensor_tensor(ACTV[:, ft, c0:c0 + n], bank[b][:, 0:n], ACTV[:, ft, c0:c0 + n],
                                     ALU.mult).then_inc(out_of[b], 1)
            with dve.Fori(0, KT) as m:
                for b, (c0, n) in enumerate(TB):
                    dve.wait_ge(done[b], m + (J_DOWN + 1))
                    V_.tensor_tensor(H[:, m, c0:c0 + n], bank[b][:, 0:n], H[:, m, c0:c0 + n],
                                     ALU.add).then_inc(out_of[b], 1)
            for b in range(3):
                dve.wait_ge(out_of[b], J_N3)
            step(V_.reciprocal(Y_RS, Y_RS))
            for kt in range(KT):
                V_.scalar_tensor_tensor(H[:, kt, :], H[:, kt, :], GAINS[:, 2, kt:kt + 1], Y_RS,
                                        ALU.mult, ALU.mult).then_inc(yn_ready, 1)


def constants():
    import numpy as np
    c = np.zeros((P, NCONST), np.float32)
    t = np.arange(P) % HD
    j = np.arange(CR)
    eye = np.eye(HD, dtype=np.float32)
    c[:, C_ONES:C_ONES + 128] = 1
    c[:, C_BONES:C_BONES + 128] = np.arange(P)[:, None] // HD == np.arange(P)[None] // HD
    c[:, C_ID:C_ID + 128] = np.eye(P)
    c[:, C_IDS:C_IDS + 64] = np.concatenate([eye, eye])
    c[:, C_NIDS:C_NIDS + 64] = -np.concatenate([eye, eye])
    strict = t[:, None] < j[None]
    incl = t[:, None] <= j[None]
    c[:, C_MG:C_MG + 64], c[:, C_MG + 64:C_MG + 128] = strict, -1.0 * incl
    c[:, C_MK:C_MK + 64], c[:, C_MK + 64:C_MK + 128] = strict, incl
    c[:, C_ML:C_ML + 64] = t[:, None] > j[None]
    pair = (t[:, None] // 2 == j[None] // 2)
    c[:, C_M2:C_M2 + 64] = pair & (t[:, None] > j[None])
    c[:, C_M2T:C_M2T + 64] = pair & (t[:, None] < j[None])
    for n, m in enumerate(LEVELS):
        c[:, C_OFF + 64 * n:C_OFF + 64 * n + 64] = ((t[:, None] // (2 * m) == j[None] // (2 * m))
                                                    & (t[:, None] // m > j[None] // m))
    c[:, C_RR:C_RR + T] = np.arange(T) % CR != 0
    c[:, C_RG:C_RG + T] = np.arange(T) % CG != 0
    c[:, C_CAUSAL:C_CAUSAL + CG] = np.arange(P)[:, None] <= np.arange(CG)[None]
    c[:NS, C_DELTA:C_DELTA + NS] = np.eye(NS)
    c[:, C_EPS:C_EPS + 3] = np.array([NORM_EPS, GN_EPS, GLA_EPS], np.float32)
    return c


def kernel(**inputs):
    import numpy as np
    import concourse.bacc as bacc
    from concourse.bass_utils import run_bass_kernel_spmd as run
    a = {k: np.asarray(v) for k, v in inputs.items()}

    def chans(x):
        return x.T.reshape(KT, P, -1)

    def tiles(w, c0, n):
        return w[:, c0:c0 + n].reshape(-1, P, n).transpose(1, 0, 2).reshape(P, -1)

    w = a["w_in"][0]
    q0, k0, v0, gl0, ga0, gb0 = 3200, 3712, 4224, 5248, 5264, 6288
    wgu, wd = a["ffn_w_gu"][0], a["ffn_w_down"][0]
    mu = a["mu_shift"][0]
    percol = [mu[0:D], mu[D:2 * D], mu[2 * D:3 * D], a["rwkv_w0"][0], a["rwkv_a0"][0], a["rwkv_k_k"][0],
              a["rwkv_k_a"][0], a["rwkv_r_k"][0].reshape(D), a["rwkv_lnx_g"][0], a["rwkv_lnx_b"][0]]
    ins = {
        "xT": np.concatenate([chans(a["x_prompt"][0]), chans(a["x_sample"][:, 0])], 2),
        "prevT": chans(a["state_shift"][0]).transpose(1, 0, 2),
        "gains": np.stack([a["norm_mix"][0], a["norm_ffn"][0], a["norm_final"]]).reshape(3, KT, P).transpose(2, 0, 1),
        "consts": constants(),
        "w_lo": tiles(w, 3072, 128),
        "w_glo": tiles(w, gl0, 16),
        "mu_lo": mu[3072:3200].reshape(P, 1),
        "w_gla": np.stack([np.concatenate([tiles(w, q0 + h * DK, DK), tiles(w, k0 + h * DK, DK),
                                           tiles(w, v0 + h * DV, DV), tiles(w, gb0 + h * DV, 128),
                                           tiles(w, gb0 + h * DV + 128, 128)], 1) for h in range(GH)]),
        "w_gla2": np.stack([a["gla_a2"][0][:, h * DK:(h + 1) * DK] for h in range(GH)]),
        "glapar": np.concatenate([a["gla_ab"][0].reshape(GH, DK).T, a["gla_norm_g"][0].reshape(VT, P).T], 1),
        "w_pair": np.stack([np.concatenate([tiles(w, i * 128, 128), tiles(w, D + i * 128, 128),
                                            tiles(w, 2 * D + i * 128, 128), tiles(w, ga0 + i * 128, 128),
                                            np.concatenate([a["rwkv_w2"][0][:, i * 128:i * 128 + 128],
                                                            a["rwkv_a2"][0][:, i * 128:i * 128 + 128]], 0)], 1)
                            for i in range(NP)]),
        "par": np.stack(percol, 1).reshape(NP, P, 10).transpose(1, 0, 2),
        "gla_s": a["state_gla"][0].transpose(1, 2, 0, 3).reshape(GH, DK, NS * DV),
        "wkv_s": a["state_wkv"][0].reshape(NS, NP, 2, HD * HD).transpose(2, 1, 0, 3).reshape(P, HD * HD),
        "w_o": np.stack([tiles(a["w_o"][0], m * 128, 128) for m in range(KT)]),
        "w_gu": np.stack([np.concatenate([tiles(wgu, f * 128, 128), tiles(wgu, F + f * 128, 128)], 1)
                          for f in range(FT)]),
        "w_d": np.stack([tiles(wd, m * 128, 128) for m in range(KT)]),
    }
    ins = {k: np.ascontiguousarray(v) for k, v in ins.items()}
    outs = {"yT": (KT, P, TS), "shT": (P, KT, 1 + NS), "wkvp": (NP, P, HD), "glap": (GH, DK, DV),
            "wkvs": (P, HD * HD), "glas": (GH, DK, NS * DV)}
    nc = bacc.Bacc("TRN2", target_bir_lowering=False, num_devices=1)
    args = [nc.dram_tensor("in_" + k, v.shape, F32, kind="ExternalInput").ap() for k, v in ins.items()]
    args += [nc.dram_tensor("out_" + k, s, F32, kind="ExternalOutput").ap() for k, s in outs.items()]
    hybrid_step(nc, *args)
    res = run(nc, [{"in_" + k: v for k, v in ins.items()}], core_ids=[0]).results[0]
    r = {k: np.asarray(res["out_" + k]) for k in outs}
    y = r["yT"].reshape(D, TS).T
    sh = r["shT"].transpose(2, 1, 0).reshape(1 + NS, D)
    wkvp = r["wkvp"].reshape(NP * 2, HD, HD).transpose(0, 2, 1)
    wkvs = r["wkvs"].reshape(2, NP, NS, HD, HD).transpose(2, 1, 0, 3, 4).reshape(NS, 2 * NP, HD, HD)
    glas = r["glas"].reshape(GH, DK, NS, DV).transpose(2, 0, 1, 3)
    return tuple(np.ascontiguousarray(v) for v in (
        y[None, :T], y[T:, None], sh[None, :1], wkvp[None, None], r["glap"][None, None],
        sh[None, 1:], wkvs[None], glas[None]))
```

```python
from contextlib import ExitStack

import concourse.bass as bass
from concourse import mybir

F32 = mybir.dt.float32
I32 = mybir.dt.int32
ACT = mybir.ActivationFunctionType
ALU = mybir.AluOpType
AX_X = mybir.AxisListType.X

P = 128
D = 1024
KT = D // P
T = 1024
NS = 8
TS = T + NS
XC = T + 2 * NS
HD = 64
NP = D // P
CR = 64
NC = T // CR
GH = 4
DK = 128
DV = 256
VT = DV // P
CG = 128
NG = T // CG
F = 2816
FT = F // P
NORM_EPS = 1e-6
GN_EPS = 64e-5
GLA_EPS = 1e-5
GATE_NORM = 16.0
HALF_DECAY = 0.5 * float(2.718281828459045) ** -0.5

XB = [(0, 348), (348, 346), (694, 346)]
XT = [(0, 348), (348, 346), (694, 338)]
TB = [(0, 344), (344, 344), (688, 344)]
PB = [(0, 342), (342, 342), (684, 340)]

LEVELS = [2, 4, 8, 16, 32]
C_ONES, C_BONES, C_ID, C_IDS, C_NIDS = 0, 128, 256, 384, 448
C_MG, C_MK, C_ML, C_M2, C_M2T, C_OFF = 512, 640, 768, 832, 896, 960
C_MGB = C_OFF + 64 * len(LEVELS)
C_OFFB = C_MGB + 128
C_RR = C_OFFB + 128 * len(LEVELS)
C_RG = C_RR + T
C_CAUSAL = C_RG + T
C_DELTA = C_CAUSAL + 128
C_EPS = C_DELTA + NS
NCONST = C_EPS + 3

(P_MUR, P_MUK, P_MUV, P_W0, P_A0, P_KK, P_KA, P_RK, P_LNG, P_LNB) = range(10)
P_CMUR, P_CMUK, P_CMUV, P_HW0, P_HA0, P_CKA = range(10, 16)
NPAR = 16

W_R, W_K, W_V, W_G = 0, 1024, 2048, 3072
W_LORA = 4096
WP = 4224
G_Q, G_K, G_V, G_B = 0, 1024, 2048, 4096
WG = 6144


def hybrid_step(nc, xT, prevT, gains, consts, w_lo, w_glo, mu_lo, w_gla, w_gla2, glapar, w_pair, par,
                gla_s, wkv_s, w_o, w_gu, w_d, yT, shT, wkvp, glap, wkvs, glas):
    with ExitStack() as ctx:
        arena = ctx.enter_context(nc.sbuf_tensor("arena", [P, 53200], F32))
        bank = [ctx.enter_context(nc.psum_tensor(f"bank{n}", [P, 512], F32)) for n in range(8)]

        def sem(name):
            return ctx.enter_context(nc.semaphore(name))

        def at(off, *dims):
            n = 1
            for d in dims:
                n *= d
            assert off + n <= 53200
            v = arena[:, off:off + n]
            if len(dims) == 1:
                return v
            names = "abcd"[:len(dims)]
            return v.rearrange("p (" + " ".join(names) + ") -> p " + " ".join(names),
                               **{names[j]: dims[j] for j in range(1, len(dims))})

        XN = at(0, KT, XC)
        MG = at(8320, KT, TS)
        WB = at(16576, WG)
        PAR = at(22720, NP, NPAR)
        MULO = at(22880, 2)
        GPAR = at(22882, GH + VT)
        CUR = at(22890, 24)
        GCUR = at(22914, 1)
        LO = at(22920, XC)
        SMALL = 23960
        CON = at(24832, NCONST)
        ONES = CON[:, C_ONES:C_ONES + 128]
        BONES = CON[:, C_BONES:C_BONES + 128]
        IDF = CON[:, C_ID:C_ID + 128]
        IDS = CON[:, C_IDS:C_IDS + 64]
        NIDS = CON[:, C_NIDS:C_NIDS + 64]
        GAINS = at(24832 + NCONST, 3, KT)
        A0 = 24832 + NCONST + 3 * KT
        A0 += -A0 % 8

        EPS = [CON[:, C_EPS + j:C_EPS + j + 1] for j in range(3)]

        N_SQ = [at(A0 + 1032 * j, TS) for j in range(2)]
        N_RS = at(A0 + 2064, TS)
        N_WLO = at(A0 + 3096, KT, 128)
        N_T0 = at(A0 + 4120, 1 + XC)
        N_WGLO = at(A0 + 5168, KT, 16)
        o = A0
        def take(n):
            nonlocal o
            s = o
            o += n + (-n % 8)
            return s
        GLO = at(take(XC), XC)
        E0 = at(take(TS), TS)
        LA = at(take(TS), TS)
        GB = at(take(T), T)
        EPG = at(take(T), T)
        EMG = at(take(T), T)
        GK_ = at(take(TS), TS)
        GQ_ = at(take(TS), TS)
        TGB = at(take(2 * TS), VT, TS)
        VTM = at(take(9 * DV), 9, DV)
        ATT = at(take(T), NG, CG)
        KTM = at(take(T), NG, CG)
        OG = at(take(2 * TS), VT, TS)
        SP = [at(take(DV), DV) for _ in range(2)]
        SF = at(take(DV), DV)
        GSQ = at(take(2 * TS), VT, TS)
        GS0 = at(take(NS * DV), NS, DV)
        VEXP = at(take(NS * DV), NS, DV)
        GKS = at(take(128), 128)
        GA2 = at(take(128), 128)
        GDM = at(take(NG), NG)
        GDE = at(take(NG), NG)
        GF = at(take(NG), NG)
        GAS = at(take(NS), NS)
        gla_end = o
        o = A0
        t0ofs = take(1 + XC)
        T0 = at(t0ofs, 1 + XC)
        X_ = at(t0ofs, NC, CR)
        kofs = take(TS)
        K = at(kofs, TS)
        R = at(take(TS), TS)
        V = at(take(TS), TS)
        aofs = take(TS)
        A = at(aofs, TS)
        BE = at(aofs, T)
        PPB = [at(aofs + 1024 * j, 8, 2 * CR) for j in range(2)]
        KE = at(take(T), T)
        ldofs = take(TS)
        LD = at(ldofs, TS)
        B = at(ldofs, T)
        PP = at(ldofs, NC, CR)
        KP = at(take(TS), TS)
        EM = at(take(TS), TS)
        epofs = take(NC * 65)
        EP = at(epofs, NC, 65)
        GTB = [at(epofs, 8, 2 * CR), at(16576 + WP, 8, 2 * CR)]
        RK = at(take(TS), TS)
        TG = at(take(TS), TS)
        O = at(take(T), T)
        AR = at(take(2 * T), NC, 2, CR)
        GT = at(take(T), NC, CR)
        AK = at(take(2 * T), NC, 2, CR)
        Y = at(take(T), NC, CR)
        YB = [at(take(T), 8, 2 * CR), CON[:, C_RG:C_RG + T].rearrange("p (a b) -> p a b", b=2 * CR)]
        VTT = at(take(T), NC, CR)
        KTT = at(take(T), NC, CR)
        BTT = at(take(T), NC, CR)
        SS = [at(take(HD), HD) for _ in range(2)]
        SD = at(take(HD), HD)
        RH = at(take(HD), HD)
        U = at(take(HD), HD)
        DC = at(take(NC), NC)
        LNP = at(take(2), 2)
        pair_end = o
        assert max(gla_end, pair_end) <= 53200, (gla_end, pair_end)
        Q_R, Q_KP, Q_V, Q_KK, Q_KA, Q_W = range(6)
        SV = at(SMALL, 6, NP, NS)
        SB = at(SMALL + 384, NP, NS)
        STG = at(SMALL + 448, NP, NS)
        SO = at(SMALL + 512, NP, NS)
        SM_END = SMALL + 576
        assert SM_END <= 24832
        s_ = A0
        S0 = at(s_, HD, HD)
        S1 = at(s_ + 4096, HD, HD)
        S2 = at(s_ + 8192, HD, HD)
        QQ = at(s_ + 12288, 6, HD)
        SA = at(s_ + 12672, HD)
        OO = at(s_ + 12736, HD)
        ST = at(s_ + 12800, 8)
        O2 = at(s_ + 12808, 2 * HD)
        OSQ = at(s_ + 12936, HD)
        XN2 = at(0, KT, TS)
        H = at(16576, KT, TS)
        f_ = A0
        WO = [at(f_ + 1024 * j, KT, 128) for j in range(2)]
        F_SQ = [at(f_ + 2048 + 1032 * j, TS) for j in range(2)]
        F_RS = at(8320 + 6912, TS)
        WGU = [at(8320 + 2048 * j, 2, KT, 128) for j in range(2)]
        f0 = A0
        ACTV = at(f0, FT, TS)
        assert f0 + FT * TS <= 53200, f0
        WD = [at(8320 + 4096, FT, 128), at(8320, FT, 128)]
        Y_SQ = [at(1032 * j, TS) for j in range(2)]
        Y_RS = at(2064, TS)

        x_loaded, con_loaded, par_loaded = sem("x_loaded"), sem("con_loaded"), sem("par_loaded")
        lo_w_loaded = sem("lo_w_loaded")
        done = [sem(f"bank{b}_done") for b in range(3)]
        out_of = [sem(f"bank{b}_evacuated") for b in range(3)]
        sq_ready, sq_used, rs_ready, xn_ready = sem("sq_ready"), sem("sq_used"), sem("rs_ready"), sem("xn_ready")
        v_step = sem("vector_step")
        a_step = sem("scalar_step")
        par_ready = sem("par_ready")
        lo_ready = sem("lo_ready")
        glo_ready = sem("glo_ready")
        mu_ready = sem("mu_ready")
        gw_loaded = sem("gla_weights_loaded")
        gs_loaded = sem("gla_state_loaded")
        gw_used = sem("gla_weights_used")
        g_abs = sem("gla_abs_done")
        g_ln = sem("gla_ln_done")
        g_la = sem("gla_log_decay_ready")
        g_scan = sem("gla_decay_sum_ready")
        g_exp = sem("gla_decays_ready")
        g_kq = sem("gla_kq_ready")
        g_vps = sem("gla_v_done")
        g_v = sem("gla_v_ready")
        g_at = sem("gla_att_done")
        g_am = sem("gla_att_ready")
        g_kt = sem("gla_kt_done")
        g_ktm = sem("gla_kt_ready")
        g_sp = sem("gla_state_ready")
        g_sf = sem("gla_state_scaled")
        g_sps = sem("gla_update_done")
        g_ops = sem("gla_out_done")
        g_og = sem("gla_out_ready")
        g_sq = sem("gla_square_ready")
        g_rt = sem("gla_root_ready")
        g_kst = sem("gla_samplek_done")
        g_ksm = sem("gla_samplek_ready")
        g_vx = sem("gla_samplev_ready")
        g_out = sem("gla_outer_done")
        g_s1 = sem("gla_sample_state_ready")
        g_os = sem("gla_sample_out_done")
        g_stored = sem("gla_stored")
        g_head = sem("gla_head_done")
        pw = sem("pair_weights_loaded")
        pw_used = sem("pair_weights_used")
        p_start = sem("pair_buffers_free")
        kk_ready = sem("kk_ready")
        merged = sem("pair_merged")
        pairs_over = sem("pairs_over")
        ksq = sem("k_square_ready")
        ldr = sem("decay_sum_ready")
        ept = sem("decays_ready")
        rkr = sem("bonus_product_ready")
        gram_in = sem("gram_inputs_ready")
        tr_done = sem("transposes_done")
        tr_ready = sem("transposes_ready")
        gram_done = sem("gram_done")
        gram_ready = sem("gram_ready")
        inv_p = sem("inverse_LX_done")
        inv_c, inv_b = sem("inverse_LX_ready"), sem("inverse_LX_blocks_ready")
        inv_xd, inv_yd = sem("inverse_X_step_done"), sem("inverse_Y_step_done")
        inv_xr, inv_yr, inv_yb = sem("inverse_X_ready"), sem("inverse_Y_ready"), sem("inverse_Y_blocks_ready")
        rhs_done, rhs_ready = sem("rhs_done"), sem("rhs_ready")
        u_done, u_ready = sem("u_done"), sem("u_ready")
        s_done, s_ready, s_scaled = sem("state_update_done"), sem("state_ready"), sem("state_scaled")
        o_done, o_ready = sem("pair_out_done"), sem("pair_out_ready")
        cen_ready, var_sq = sem("centred_ready"), sem("centred_square_ready")
        s_stored = sem("pair_state_stored")
        state_new = sem("sample_state_ready")
        st_loaded = sem("sample_state_loaded")
        sv_done = sem("sample_values_transposed")
        sv_ready = sem("sample_values_ready")
        pool_step = sem("gpsimd_step")
        sa_step = sem("sample_vector_step")
        so_ready, so_done = sem("sample_out_ready"), sem("sample_out_transposed")
        osq_ready = sem("sample_root_ready")
        mg_ready = sem("merged_ready")
        h_loaded = sem("h_loaded")
        wo_loaded = [sem(f"wo_loaded{j}") for j in range(2)]
        wo_used = sem("wo_used")
        h_ready = sem("h_ready")
        sq2, sq2_used, rs2 = sem("ffn_square_ready"), sem("ffn_square_used"), sem("ffn_root_ready")
        xn2_ready = sem("ffn_input_ready")
        gu_loaded = [sem(f"gate_up_loaded{j}") for j in range(2)]
        gu_used = sem("gate_up_used")
        silu_ready = sem("silu_ready")
        act_ready = sem("activations_ready")
        wd_loaded = [sem(f"down_loaded{j}") for j in range(2)]
        wd_used = sem("down_used")
        y_ready = sem("h_final_ready")
        sq3, sq3_used, rs3 = sem("final_square_ready"), sem("final_square_used"), sem("final_root_ready")
        yn_ready = sem("y_ready")
        stored, shift_stored = sem("stored"), sem("shift_stored")

        J_NORM, J_LO, J_GLO = 1, 2, 3
        J_GLA, PER_GLA = 3, 6
        J_PAIR, PER_PAIR = J_GLA + GH * PER_GLA, 10
        J_WO = J_PAIR + NP * PER_PAIR
        J_N2 = J_WO + KT + 1
        J_FFN = J_N2
        J_DOWN = J_FFN + 2 * FT
        J_N3 = J_DOWN + KT + 1

        SLOTS = 3 * NC
        PRODUCTS = [(job, b, kt, n) for job, n in (("W", 1), ("A", 1), ("K", KT), ("R", KT), ("N", 1), ("V", KT))
                    for b in range(3) for kt in range(n)]

        def slot(m):
            return m * (SLOTS - 2) // len(PRODUCTS)

        ends = {(job, b): slot(m) for m, (job, b, kt, n) in enumerate(PRODUCTS) if kt == n - 1}
        JOB = {"W": 1, "A": 2, "K": 3, "R": 4, "N": 5, "V": 6}

        def base(i):
            return J_PAIR if isinstance(i, int) and i == 0 else i * PER_PAIR + (J_PAIR - 2)

        YBANK = (7, 4)

        block = ctx.enter_context(nc.Block())

        @block.sync
        def _(sp):
            for kt in range(KT):
                sp.dma_start(XN[:, kt, 0:TS], xT[kt, :, :]).then_inc(x_loaded, 16)
            sp.dma_start(CON, consts[:, :]).then_inc(con_loaded, 16)
            sp.dma_start(N_WLO, w_lo.rearrange("p (k n) -> p k n", n=128)).then_inc(lo_w_loaded, 16)
            sp.dma_start(N_WGLO, w_glo.rearrange("p (k n) -> p k n", n=16)).then_inc(lo_w_loaded, 16)
            sp.dma_start(XN[:, :, TS:XC], prevT[:, :, :]).then_inc(par_loaded, 16)
            sp.dma_start(PAR[:, :, 0:10], par[:, :, :]).then_inc(par_loaded, 16)
            sp.dma_start(GAINS, gains[:, :, :]).then_inc(par_loaded, 16)
            sp.dma_start(MULO[:, 0:1], mu_lo[:, :]).then_inc(par_loaded, 16)
            sp.dma_start(GPAR, glapar[:, :]).then_inc(par_loaded, 16)
            with sp.Fori(0, GH) as h:
                sp.wait_ge(done[2], h * PER_GLA + (J_GLA - 1))
                sp.dma_start(WB, w_gla[h, :, :]).then_inc(gw_loaded, 16)
                sp.dma_start(GA2[0:16, :], w_gla2[h, :, :]).then_inc(gw_loaded, 16)
            sp.wait_ge(done[2], J_PAIR - 1)
            sp.dma_start(WB[:, 0:WP], w_pair[0, :, :]).then_inc(pw, 16)
            with sp.Fori(1, NP) as i:
                sp.wait_ge(done[2], i * PER_PAIR + (J_PAIR - 3))
                sp.dma_start(WB[:, 0:WP], w_pair[i, :, :]).then_inc(pw, 16)
            sp.wait_ge(pairs_over, 1)
            sp.dma_start(S0.rearrange("p a b -> p (a b)"), wkv_s[:, :]).then_inc(st_loaded, 16)
            sp.wait_ge(state_new, 1)
            sp.dma_start(wkvs[:, :], S0.rearrange("p a b -> p (a b)")).then_inc(stored, 16)
            sp.wait_ge(mg_ready, 1)
            for m in range(2):
                sp.dma_start(WO[m], w_o[m, :, :].rearrange("p (k n) -> p k n", n=128)).then_inc(wo_loaded[m], 16)
            for kt in range(KT):
                sp.dma_start(H[:, kt, :], xT[kt, :, :]).then_inc(h_loaded, 16)
            with sp.Fori(0, KT // 2 - 1) as g:
                for j in range(2):
                    sp.wait_ge(done[2], g * 2 + (J_WO + 1 + j))
                    sp.dma_start(WO[j], w_o[g * 2 + (2 + j), :, :].rearrange("p (k n) -> p k n", n=128)
                                 ).then_inc(wo_loaded[j], 16)
            sp.wait_ge(done[2], J_WO + KT)
            for j in range(2):
                sp.dma_start(WGU[j].rearrange("p a k n -> p (a k n)"), w_gu[j, :, :]).then_inc(gu_loaded[j], 16)
            with sp.Fori(0, FT // 2 - 1) as g:
                for j in range(2):
                    sp.wait_ge(done[2], g * 4 + (J_FFN + 2 + 2 * j))
                    sp.dma_start(WGU[j].rearrange("p a k n -> p (a k n)"), w_gu[g * 2 + (2 + j), :, :]
                                 ).then_inc(gu_loaded[j], 16)
            sp.dma_start(WD[0].rearrange("p k n -> p (k n)"), w_d[0, :, :]).then_inc(wd_loaded[0], 16)
            sp.wait_ge(done[2], J_DOWN)
            sp.dma_start(WD[1].rearrange("p k n -> p (k n)"), w_d[1, :, :]).then_inc(wd_loaded[1], 16)
            with sp.Fori(0, KT // 2 - 1) as g:
                for j in range(2):
                    sp.wait_ge(done[2], g * 2 + (J_DOWN + 1 + j))
                    sp.dma_start(WD[j].rearrange("p k n -> p (k n)"), w_d[g * 2 + (2 + j), :, :]
                                 ).then_inc(wd_loaded[j], 16)
            for kt in range(KT):
                sp.wait_ge(yn_ready, kt + 1)
                sp.dma_start(yT[kt, :, :], H[:, kt, :]).then_inc(stored, 16)
            sp.wait_ge(g_stored, 32 * GH)
            sp.wait_ge(s_stored, 16 * NP)
            sp.wait_ge(shift_stored, 16)
            sp.wait_ge(stored, 16 * (1 + KT))

        @block.gpsimd
        def _(pool):
            pool.wait_ge(xn_ready, KT)
            pool.dma_start(shT[:, :, :], XN[:, :, T - 1:TS]).then_inc(shift_stored, 16)
            with pool.Fori(0, GH) as h:
                pool.wait_ge(g_head, h + 1)
                pool.nop(nofuse=True)
                pool.dma_start(GS0, gla_s[h, :, :].rearrange("p (b v) -> p b v", v=DV)).then_inc(gs_loaded, 16)
                pool.wait_ge(g_sp, h * (NG + 1) + (NG + 1))
                pool.nop(nofuse=True)
                pool.dma_start(glap[h, :, :], SP[0]).then_inc(g_stored, 16)
                pool.wait_ge(g_s1, h * NS + NS)
                pool.nop(nofuse=True)
                pool.dma_start(glas[h, :, :].rearrange("p (b v) -> p b v", v=DV), GS0).then_inc(g_stored, 16)
            with pool.Fori(0, NP) as i:
                pool.wait_ge(s_ready, i * (NC + 1) + (NC + 1))
                pool.nop(nofuse=True)
                pool.dma_start(wkvp[i, :, :], SS[0]).then_inc(s_stored, 16)
            pool.wait_ge(sv_ready, 12)
            nc.gpsimd.tensor_tensor(S1, QQ[:, Q_V, :].unsqueeze(2).to_broadcast([P, HD, HD]),
                                    QQ[:, Q_KP, :].unsqueeze(1).to_broadcast([P, HD, HD]), ALU.mult).then_inc(pool_step, 1)

        @block.tensor
        def _(pe):
            def mm(out, lhsT, rhs, start, stop):
                return nc.tensor.matmul(out, lhsT, rhs, start=start, stop=stop)

            def gate(s, value):
                pe.wait_ge(s, value)
                pe.nop(nofuse=True)

            def project(weight, src, blocks, before):
                for b, (c0, n) in enumerate(blocks):
                    gate(out_of[b], before)
                    for kt in range(KT):
                        last = mm(bank[b][0:weight(kt).shape[1], 0:n], weight(kt), src[:, kt, c0:c0 + n],
                                  kt == 0, kt == KT - 1)
                    last.then_inc(done[b], 1)

            pe.wait_ge(con_loaded, 16)
            for kt in range(KT):
                pe.wait_ge(sq_ready, kt + 1)
                for b, (c0, n) in enumerate(TB):
                    last = mm(bank[b][:, 0:n], ONES, N_SQ[kt % 2][:, c0:c0 + n], kt == 0, kt == KT - 1)
                    if kt == KT - 1:
                        last.then_inc(done[b], 1)
                    elif b == 2:
                        last.then_inc(sq_used, 1)
            pe.wait_ge(lo_w_loaded, 32)
            pe.wait_ge(xn_ready, KT)
            pe.wait_ge(par_loaded, 16 * 5)
            project(lambda kt: N_WLO[:, kt, :], XN, XB, J_NORM)
            project(lambda kt: N_WGLO[:, kt, :], XN, XB, J_LO)

            with pe.Fori(0, GH) as h:
                j0 = h * PER_GLA + J_GLA
                gate(gw_loaded, h * 32 + 32)
                gate(g_head, h + 1)
                for b, (c0, n) in enumerate(XT):
                    gate(out_of[b], j0)
                    mm(bank[b][:, 0:n], GA2[0:16, :], GLO[0:16, c0:c0 + n], True, True).then_inc(done[b], 1)
                for vt in range(VT):
                    project(lambda kt: WB[:, G_B + vt * 1024 + kt * 128:G_B + vt * 1024 + kt * 128 + 128],
                            XN, XT, j0 + (1 + vt))
                for tt in range(9):
                    rows = P if tt < 8 else NS
                    if tt >= 2:
                        gate(g_v, h * 9 + (tt - 1))
                    for kt in range(KT):
                        last = mm(bank[3 + tt % 2][0:rows, 0:DV], XN[:, kt, tt * P:tt * P + rows],
                                  WB[:, G_V + kt * DV:G_V + (kt + 1) * DV], kt == 0, kt == KT - 1)
                    last.then_inc(g_vps, 1)
                project(lambda kt: WB[:, G_K + kt * 128:G_K + kt * 128 + 128], XN, XT, j0 + 3)
                project(lambda kt: WB[:, G_Q + kt * 128:G_Q + kt * 128 + 128], XN, XT, j0 + 4)
                for q in range(2):
                    if q == 0:
                        gate(out_of[2], j0 + 4)
                    else:
                        gate(g_ktm, h * 2 + 1)
                    for c in range(4):
                        cc = 4 * q + c
                        last = nc.tensor.transpose(bank[5][:, c * CG:(c + 1) * CG],
                                                   GK_[:, cc * CG:(cc + 1) * CG], IDF)
                    last.then_inc(g_kt, 1)
                    if q == 0:
                        gate(out_of[2], j0 + 5)
                    else:
                        gate(g_am, h * 2 + 1)
                    for c in range(4):
                        cc = 4 * q + c
                        last = mm(bank[6][:, c * CG:(c + 1) * CG], GK_[:, cc * CG:(cc + 1) * CG],
                                  GQ_[:, cc * CG:(cc + 1) * CG], True, True)
                    last.then_inc(g_at, 1)
                gate(g_ktm, h * 2 + 2)
                gate(g_am, h * 2 + 2)
                gate(g_v, h * 9 + 9)
                for c in range(NG):
                    gate(g_sp, h * (NG + 1) + (c + 1))
                    mm(bank[4][:, 0:DV], KTM[:, c, :], VTM[:, c, :], True, True).then_inc(g_sps, 1)
                    if c:
                        gate(g_og, h * (NG + 1) + c)
                    for vt in range(VT):
                        mm(bank[7][:, vt * CG:(vt + 1) * CG], VTM[:, c, vt * P:(vt + 1) * P], ATT[:, c, :],
                           True, False)
                        last = mm(bank[7][:, vt * CG:(vt + 1) * CG], SP[c % 2][:, vt * P:(vt + 1) * P],
                                  GQ_[:, c * CG:(c + 1) * CG], False, True)
                    last.then_inc(g_ops, 1)
                mm(bank[3][0:NS, 0:P], GK_[:, T:TS], IDF, True, True).then_inc(g_kst, 1)
                gate(g_ksm, h + 1)
                gate(g_vx, h + 1)
                for q in range(4):
                    if q >= 2:
                        gate(g_s1, h * NS + (2 * q - 2))
                    mm(bank[3 + 2 * (q % 2)][:, :], GKS[0:NS, :],
                       VEXP[0:NS, 2 * q:2 * q + 2, :].rearrange("p a b -> p (a b)"), True, True).then_inc(g_out, 1)
                gate(g_s1, h * NS + NS)
                for b in range(NS):
                    for vt in range(VT):
                        last = mm(bank[6][:, vt * NS + b:vt * NS + b + 1], GS0[:, b, vt * P:(vt + 1) * P],
                                  GQ_[:, T + b:T + b + 1], True, True)
                last.then_inc(g_os, 1)
                gate(g_sq, h + 1)
                for b, (c0, n) in enumerate(TB):
                    gate(out_of[b], j0 + 5)
                    for vt in range(VT):
                        last = mm(bank[b][:, 0:n], ONES, GSQ[:, vt, c0:c0 + n], vt == 0, vt == VT - 1)
                    last.then_inc(done[b], 1)

            HALVES = [slice(64 * e, 64 * e + 64) for e in range(2)]

            def projection(i, m):
                job, b, kt, count = PRODUCTS[m]
                c0, n = {"W": XT, "A": XT, "N": TB}.get(job, XB)[b]
                if m == 0:
                    gate(pw, i * 16 + 16)
                    gate(p_start, i + 1)
                if job == "N" and b == 0:
                    gate(ksq, i + 1)
                if kt == 0:
                    gate(out_of[b], base(i) + (JOB[job] - 1))
                if job in "WA":
                    r = HALVES["WA".index(job)]
                    last = mm(bank[b][:, 0:n], WB[r, W_LORA:W_LORA + 128], LO[r, c0:c0 + n], True, True)
                elif job == "N":
                    last = mm(bank[b][:, 0:n], BONES, EM[:, c0:c0 + n], True, True)
                else:
                    w = {"K": W_K, "R": W_R, "V": W_V}[job] + kt * 128
                    last = mm(bank[b][:, 0:n], WB[:, w:w + 128], XN[:, kt, c0:c0 + n], kt == 0, kt == KT - 1)
                if kt == count - 1:
                    last.then_inc(done[b], 1)

            def chunk_step(i, c, stage):
                S = SS[c % 2]
                if stage == 0:
                    gate(s_ready, i * (NC + 1) + (c + 1))
                    for r in HALVES:
                        mm(bank[3][r, 0:HD], AK[r, c, 0, :], VTT[r, c, :], True, False)
                        last = mm(bank[3][r, 0:HD], AR[r, c, 0, :], S[r, :], False, True)
                    last.then_inc(rhs_done, 1)
                if stage == 1:
                    if c == 0:
                        gate(inv_yb, i * 24 + 24)
                    gate(rhs_ready, i * NC + (c + 1))
                    mm(bank[4][:, 0:HD], YB[c // 8][:, c % 8, :], RH, True, True).then_inc(u_done, 1)
                if stage == 2:
                    gate(u_ready, i * NC + (c + 1))
                    for r in HALVES:
                        mm(bank[5][r, 0:HD], KTT[r, c, :], VTT[r, c, :], True, False)
                        last = mm(bank[5][r, 0:HD], BTT[r, c, :], U[r, :], False, True)
                    last.then_inc(s_done, 1)
                    ob = bank[6 + c // 8]
                    cols = slice((c % 8) * CR, (c % 8 + 1) * CR)
                    for r in HALVES:
                        mm(ob[r, cols], VTT[r, c, :], AK[r, c, 1, :], True, False)
                        mm(ob[r, cols], S[r, :], AR[r, c, 1, :], False, False)
                        last = mm(ob[r, cols], U[r, :], GT[r, c, :], False, True)
                    last.then_inc(o_done, 1)

            def head_sums(src, blocks, before):
                for b, (c0, n) in enumerate(blocks):
                    gate(out_of[b], before)
                    mm(bank[b][:, 0:n], BONES, src[:, c0:c0 + n], True, True).then_inc(done[b], 1)

            def merge_gate(m, before):
                b, kt = divmod(m, KT)
                c0, n = XT[b]
                if kt == 0:
                    gate(out_of[b], before)
                last = mm(bank[b][:, 0:n], WB[:, W_G + kt * 128:W_G + kt * 128 + 128],
                          XN[:, kt, c0:c0 + n], kt == 0, kt == KT - 1)
                if kt == KT - 1:
                    last.then_inc(done[b], 1)

            def chunk_products(i, previous):
                job = base(i) + 6
                if previous:
                    gate(o_ready, (i - 1) * 2 + 2)
                    head_sums(O, PB, job)
                    job = job + 1
                gate(gram_in, i * 4 + 4)
                for n_, (src, idn) in enumerate(((V, IDS), (KE, IDS), (BE, NIDS))):
                    for hf in range(2):
                        m = 2 * n_ + hf
                        if m >= 2:
                            gate(tr_ready, i * 6 + (m - 1))
                        for c in range(8):
                            for r in HALVES:
                                last = mm(bank[6 + m % 2][r, c * CR:(c + 1) * CR],
                                          src[r, (8 * hf + c) * CR:(8 * hf + c + 1) * CR], idn[r, :], True, True)
                        last.then_inc(tr_done, 1)
                for q in range(4):
                    if q:
                        gate(gram_ready, i * 12 + 3 * q)
                    for g, src in ((3, BE), (4, KE)):
                        for c in range(4):
                            for r in HALVES:
                                cc = 4 * q + c
                                last = mm(bank[g][r, c * 128:(c + 1) * 128], src[r, cc * CR:(cc + 1) * CR],
                                          AR[r, cc, :, :].rearrange("p a t -> p (a t)"), True, True)
                        last.then_inc(gram_done, 1)
                    for c in range(4):
                        for r in HALVES:
                            cc = 4 * q + c
                            last = mm(bank[5][r, c * CR:(c + 1) * CR], AR[r, cc, 0, :],
                                      BE[r, cc * CR:(cc + 1) * CR], True, True)
                    last.then_inc(gram_done, 1)
                if previous:
                    gate(var_sq, i)
                    head_sums(EM[:, 0:T], PB, job)
                    job = job + 1
                gate(tr_ready, i * 6 + 6)
                LAST = len(LEVELS) - 1
                for lv in range(len(LEVELS)):
                    fill = 6 * lv
                    for hf in range(2):
                        if lv == 0:
                            gate(inv_xr, i * 9 + 1)
                        else:
                            gate(inv_xr, i * 9 + (2 * lv + hf))
                            if hf == 1:
                                gate(inv_yr, i * 11 + (2 * lv + 1))
                        for c in range(8):
                            last = mm(bank[3 + hf][:, c * CR:(c + 1) * CR], GTB[hf][:, c, :], X_[:, 8 * hf + c, :], True, True)
                        last.then_inc(inv_p, 1)
                        for _ in range(1 + hf):
                            if lv < LAST:
                                merge_gate(fill, job)
                            fill += 1
                    if lv == LAST:
                        gate(rkr, i + 1)
                        head_sums(RK, TB, job + 1)
                    for hf in range(2):
                        if lv < LAST:
                            gate(inv_c, i * 8 + (2 * lv + hf + 1))
                            gate(inv_yb, i * 24 + (4 * lv + 2 * hf + 2))
                            for c in range(8):
                                cc = 8 * hf + c
                                last = mm(bank[5 + hf][:, c * CR:(c + 1) * CR], YB[hf][:, c, :], PP[:, cc, :], True, True)
                            last.then_inc(inv_xd, 1)
                        gate(inv_b, i * 10 + (2 * lv + hf + 1))
                        if lv == LAST:
                            gate(inv_yr, i * 11 + (2 * lv + hf))
                        for c in range(8):
                            cc = 8 * hf + c
                            last = mm(bank[YBANK[hf]][:, c * CR:(c + 1) * CR], PPB[hf][:, c, :], Y[:, cc, :], True, True)
                        last.then_inc(inv_yd, 1)
                        for _ in range(1 + hf):
                            if lv < LAST:
                                merge_gate(fill, job)
                            fill += 1

            for m in range(len(PRODUCTS)):
                projection(0, m)
            chunk_products(0, False)
            with pe.Fori(1, NP) as i:
                for s in range(SLOTS):
                    chunk_step(i - 1, s // 3, s % 3)
                    for m in range(len(PRODUCTS)):
                        if slot(m) == s:
                            projection(i, m)
                chunk_products(i, True)
            for s in range(SLOTS):
                chunk_step(NP - 1, s // 3, s % 3)
            pe.wait_ge(o_ready, 2 * NP)
            head_sums(O, PB, J_WO - 2)
            pe.wait_ge(var_sq, NP)
            head_sums(EM[:, 0:T], PB, J_WO - 1)

            pe.wait_ge(pairs_over, 1)
            for g in range(3):
                last = nc.tensor.transpose(bank[3][:, g * P:(g + 1) * P],
                                           SV[:, 2 * g:2 * g + 2, :, :].rearrange("p a b c -> p (a b c)"), IDF)
            last.then_inc(sv_done, 1)
            pe.wait_ge(so_ready, 2)
            mm(bank[4][:, 0:64], O2[0:64, :], CON[0:64, C_ID:C_ID + 64], True, True).then_inc(so_done, 1)

            pe.wait_ge(mg_ready, 1)
            with pe.Fori(0, KT // 2) as g:
                for j in range(2):
                    gate(wo_loaded[j], g * 16 + 16)
                    for b, (c0, n) in enumerate(TB):
                        gate(out_of[b], g * 2 + (J_WO + j))
                        for kt in range(KT):
                            last = mm(bank[b][:, 0:n], WO[j][:, kt, :], MG[:, kt, c0:c0 + n], kt == 0, kt == KT - 1)
                        last.then_inc(done[b], 1)

            def mean_square(sq, used, bufs, before):
                for kt in range(KT):
                    pe.wait_ge(sq, kt + 1)
                    for b, (c0, n) in enumerate(TB):
                        if kt == 0:
                            pe.wait_ge(out_of[b], before)
                        last = mm(bank[b][:, 0:n], ONES, bufs[kt % 2][:, c0:c0 + n], kt == 0, kt == KT - 1)
                        if kt == KT - 1:
                            last.then_inc(done[b], 1)
                        elif b == 2:
                            last.then_inc(used, 1)

            mean_square(sq2, sq2_used, F_SQ, J_N2 - 1)
            pe.wait_ge(xn2_ready, KT)
            with pe.Fori(0, FT // 2) as g:
                for j in range(2):
                    gate(gu_loaded[j], g * 16 + 16)
                    for q in range(2):
                        for b, (c0, n) in enumerate(TB):
                            gate(out_of[b], g * 4 + (J_FFN + 2 * j + q))
                            for kt in range(KT):
                                last = mm(bank[b][:, 0:n],
                                          WGU[j][:, q, kt, :], XN2[:, kt, c0:c0 + n], kt == 0, kt == KT - 1)
                            last.then_inc(done[b], 1)
            with pe.Fori(0, KT // 2) as g:
                for j in range(2):
                    gate(wd_loaded[j], g * 16 + 16)
                    for b, (c0, n) in enumerate(TB):
                        gate(out_of[b], g * 2 + (J_DOWN + j))
                        for kt in range(FT):
                            last = mm(bank[b][:, 0:n], WD[j][:, kt, :], ACTV[:, kt, c0:c0 + n], kt == 0, kt == FT - 1)
                        last.then_inc(done[b], 1)
            mean_square(sq3, sq3_used, Y_SQ, J_N3 - 1)

        @block.scalar
        def _(act):
            def f(out, in_, func, bias=0.0, scale=1.0):
                return nc.scalar.activation(out, in_, func, bias=bias, scale=scale)

            for kt in range(KT):
                if kt == 0:
                    act.wait_ge(x_loaded, 16 * KT)
                if kt >= 2:
                    act.wait_ge(sq_used, kt - 1)
                f(N_SQ[kt % 2], XN[:, kt, 0:TS], ACT.Square).then_inc(sq_ready, 1)
            act.wait_ge(con_loaded, 16)
            act.wait_ge(par_loaded, 16 * 5)
            for b, (c0, n) in enumerate(TB):
                act.wait_ge(done[b], J_NORM)
                f(N_RS[:, c0:c0 + n], bank[b][:, 0:n], ACT.Sqrt, EPS[0], 1.0 / D).then_inc(out_of[b], 1)
            for b, (c0, n) in enumerate(XB):
                act.wait_ge(done[b], J_LO)
                f(N_T0[:, 1 + c0:1 + c0 + n], bank[b][:, 0:n], ACT.Copy, scale=MULO[:, 0:1]).then_inc(mu_ready, 1)
            for b, (c0, n) in enumerate(XB):
                act.wait_ge(done[b], J_GLO)
                nc.scalar.copy(GLO[0:16, c0:c0 + n], bank[b][0:16, 0:n]).then_inc(out_of[b], 1)
            act.wait_ge(lo_ready, 1)
            f(LO[0:64, 0:TS], LO[0:64, 0:TS], ACT.Tanh).then_inc(a_step, 1)


            with act.Fori(0, GH) as h:
                j0 = h * PER_GLA + J_GLA
                act.wait_ge(g_head, h + 1)
                for b, (c0, n) in enumerate(XT):
                    act.wait_ge(done[b], j0 + 1)
                    f(E0[:, c0:c0 + n], bank[b][:, 0:n], ACT.Abs, GCUR).then_inc(g_abs, 1)
                act.wait_ge(g_abs, h * 3 + 3)
                f(E0, E0, ACT.Exp, scale=-1.0).then_inc(a_step, 1)
                act.wait_ge(a_step, h + 2)
                f(E0, E0, ACT.Ln, bias=1.0).then_inc(g_ln, 1)
                for vt in range(VT):
                    for b, (c0, n) in enumerate(XT):
                        act.wait_ge(done[b], j0 + (2 + vt))
                        f(TGB[:, vt, c0:c0 + n], bank[b][:, 0:n], ACT.Tanh, scale=0.5).then_inc(out_of[b], 1)
                act.wait_ge(g_scan, h + 1)
                f(EPG, GB, ACT.Exp, scale=1.0 / GATE_NORM).then_inc(g_exp, 1)
                f(EMG, GB, ACT.Exp, scale=-1.0 / GATE_NORM).then_inc(g_exp, 1)
                f(GDM, GDE, ACT.Exp, scale=1.0 / GATE_NORM).then_inc(g_exp, 1)
                f(GAS, LA[:, T:TS], ACT.Exp, scale=1.0 / GATE_NORM).then_inc(g_exp, 1)
                for tt in range(9):
                    rows = P if tt < 8 else NS
                    act.wait_ge(g_vps, h * 9 + (tt + 1))
                    nc.scalar.copy(VTM[0:rows, tt, :], bank[3 + tt % 2][0:rows, 0:DV]).then_inc(g_v, 1)
                for q in range(2):
                    act.wait_ge(g_kt, h * 2 + (q + 1))
                    nc.scalar.copy(KTM[:, 4 * q:4 * q + 4, :].rearrange("p a b -> p (a b)"), bank[5][:, :]).then_inc(g_ktm, 1)
                for c in range(NG):
                    act.wait_ge(g_sp, h * (NG + 1) + (c + 1))
                    f(SF, SP[c % 2], ACT.Copy, scale=GF[:, c:c + 1]).then_inc(g_sf, 1)
                    act.wait_ge(g_ops, h * NG + (c + 1))
                    nc.scalar.copy(OG[:, :, c * CG:(c + 1) * CG],
                                   bank[7][:, 0:DV].rearrange("p (a b) -> p a b", b=CG)).then_inc(g_og, 1)
                act.wait_ge(g_kst, h + 1)
                nc.scalar.copy(GKS[0:NS, :], bank[3][0:NS, 0:P]).then_inc(g_ksm, 1)
                act.wait_ge(g_os, h + 1)
                nc.scalar.copy(OG[:, :, T:TS], bank[6][:, 0:VT * NS].rearrange("p (a b) -> p a b", b=NS)).then_inc(g_og, 1)
                act.wait_ge(g_og, h * (NG + 1) + NG + 1)
                f(GSQ, OG, ACT.Square).then_inc(g_sq, 1)
                for b, (c0, n) in enumerate(TB):
                    act.wait_ge(done[b], j0 + 6)
                    f(E0[:, c0:c0 + n], bank[b][:, 0:n], ACT.Sqrt, EPS[2], 1.0 / DV).then_inc(out_of[b], 1)

            def first_phase(i, s):
                j0 = base(i)

                def tanh(dst, job, b, bias):
                    c0, n = XT[b]
                    act.wait_ge(done[b], j0 + JOB[job])
                    f(dst[:, c0:c0 + n], bank[b][:, 0:n], ACT.Tanh, CUR[:, bias:bias + 1], 0.5).then_inc(out_of[b], 1)

                def mix(job, b, mu):
                    c0, n = XB[b]
                    act.wait_ge(done[b], j0 + JOB[job])
                    if job != "K" and b == 0:
                        act.wait_ge(out_of[2], j0 + (4 if job == "V" else 3))
                    f(T0[:, 1 + c0:1 + c0 + n], bank[b][:, 0:n], ACT.Copy, scale=CUR[:, mu:mu + 1]).then_inc(mu_ready, 1)

                def squares_of_k():
                    act.wait_ge(out_of[2], j0 + 3)
                    f(EM, K, ACT.Square, scale=CUR[:, P_KK:P_KK + 1]).then_inc(ksq, 1)

                def root(b):
                    c0, n = TB[b]
                    act.wait_ge(done[b], j0 + JOB["N"])
                    f(EM[:, c0:c0 + n], bank[b][:, 0:n], ACT.Sqrt).then_inc(out_of[b], 1)

                def decays():
                    act.wait_ge(ldr, i + 1)
                    f(EP[:, :, 1:65], B.rearrange("p (c t) -> p c t", t=CR), ACT.Exp).then_inc(ept, 1)
                    f(SV[:, Q_W, i, :], LD[:, T:TS], ACT.Exp).then_inc(ept, 1)

                def inverse_decays():
                    act.wait_ge(kk_ready, i + 1)
                    f(EM[:, 0:T], B, ACT.Exp, scale=-1.0).then_inc(ept, 1)

                for b in range(3):
                    if s == ends["W", b] + 1:
                        tanh(LD, "W", b, P_HW0)
                    if s == ends["A", b] + 1:
                        tanh(A, "A", b, P_HA0)
                    for job, mu in (("K", P_MUK), ("R", P_MUR), ("V", P_MUV)):
                        if s == ends[job, b] + 1:
                            mix(job, b, mu)
                    if s == ends["N", b] + 1:
                        root(b)
                if s == ends["A", 2] + 3:
                    decays()
                if s == ends["K", 2] + 2:
                    squares_of_k()
                if s == SLOTS:
                    inverse_decays()

            def chunk_side(i, s):
                c = s // 3
                if s % 3 == 0:
                    act.wait_ge(s_ready, i * (NC + 1) + (c + 1))
                    f(SD, SS[c % 2], ACT.Copy, scale=DC[:, c:c + 1]).then_inc(s_scaled, 1)
                if s % 3 == 2 and c % 8 == 7:
                    act.wait_ge(o_done, i * NC + (c + 1))
                    nc.scalar.copy(O[:, (c - 7) * CR:(c + 1) * CR], bank[6 + c // 8][:, :]).then_inc(o_ready, 1)

            def norm_square(i, job):
                act.wait_ge(out_of[2], job)
                f(EM[:, 0:T], O, ACT.Square).then_inc(var_sq, 1)

            def norm_root(i, job):
                for b, (c0, n) in enumerate(PB):
                    act.wait_ge(done[b], job)
                    f(EM[:, c0:c0 + n], bank[b][:, 0:n], ACT.Sqrt, EPS[1], 1.0 / HD).then_inc(out_of[b], 1)

            def second_phase(i, previous):
                job = base(i) + 6
                act.wait_ge(gram_in, i * 4 + 4)
                for n_, dst in enumerate((VTT, KTT, BTT)):
                    for hf in range(2):
                        m = 2 * n_ + hf
                        act.wait_ge(tr_done, i * 6 + (m + 1))
                        nc.scalar.copy(dst[:, 8 * hf:8 * hf + 8, :].rearrange("p a b -> p (a b)"),
                                       bank[6 + m % 2][:, :]).then_inc(tr_ready, 1)
                if previous:
                    norm_square(i, job + 1)
                    norm_root(i, job + 2)
                    job = job + 2
                for lv in range(len(LEVELS) + 1):
                    for hf in range(2):
                        act.wait_ge(inv_yr, i * 11 + (1 if lv == 0 else 2 * lv + hf))
                        for e in range(2):
                            r = slice(64 * e, 64 * e + 64)
                            nc.scalar.copy(YB[hf][r, :, r], Y[r, 8 * hf:8 * hf + 8, :]).then_inc(inv_yb, 1)
                    for b, (c0, n) in enumerate(XT):
                        if lv != (3, 4, 4)[b]:
                            continue
                        if previous and b == 0:
                            act.wait_ge(merged, i)
                        act.wait_ge(done[b], job + 1)
                        f(TG[:, c0:c0 + n], bank[b][:, 0:n], ACT.Tanh, scale=0.5).then_inc(out_of[b], 1)

            act.wait_ge(p_start, 1)
            for s in range(SLOTS + 1):
                first_phase(0, s)
            second_phase(0, False)
            with act.Fori(1, NP) as i:
                act.wait_ge(p_start, i + 1)
                for s in range(SLOTS):
                    chunk_side(i - 1, s)
                    first_phase(i, s)
                first_phase(i, SLOTS)
                second_phase(i, True)
            for s in range(SLOTS):
                chunk_side(NP - 1, s)
            norm_square(NP, J_WO - 1)
            norm_root(NP, J_WO)

            act.wait_ge(sv_done, 1)
            for g in range(3):
                for q in range(2):
                    for e in range(2):
                        nc.scalar.copy(QQ[64 * e:64 * e + 64, 2 * g + q, :],
                                       bank[3][64 * q:64 * q + 64, g * P + 64 * e:g * P + 64 * e + 64]).then_inc(sv_ready, 1)
            act.wait_ge(sa_step, 1)
            f(ST[:, 4:5], ST[:, 3:4], ACT.Sqrt, EPS[1], 1.0 / HD).then_inc(osq_ready, 1)
            act.wait_ge(so_done, 1)
            nc.scalar.copy(SO.rearrange("p a b -> p (a b)"), bank[4][:, 0:64]).then_inc(a_step, 1)

            def squares(bufs, ready, used, job):
                for kt in range(KT):
                    act.wait_ge(out_of[2], job + kt + 1)
                    if kt >= 2:
                        act.wait_ge(used, kt - 1)
                    f(bufs[kt % 2], H[:, kt, :], ACT.Square).then_inc(ready, 1)

            def roots(dst, job):
                for b, (c0, n) in enumerate(TB):
                    act.wait_ge(done[b], job)
                    f(dst[:, c0:c0 + n], bank[b][:, 0:n], ACT.Sqrt, EPS[0], 1.0 / D).then_inc(out_of[b], 1)

            squares(F_SQ, sq2, sq2_used, J_WO)
            roots(F_RS, J_N2)
            with act.Fori(0, FT) as ft:
                for b, (c0, n) in enumerate(TB):
                    act.wait_ge(done[b], ft * 2 + (J_FFN + 1))
                    f(ACTV[:, ft, c0:c0 + n], bank[b][:, 0:n], ACT.Silu).then_inc(out_of[b], 1)
            act.wait_ge(done[2], J_DOWN)
            squares(Y_SQ, sq3, sq3_used, J_DOWN)
            roots(Y_RS, J_N3)

        @block.vector
        def _(dve):
            V_ = nc.vector
            steps = [0]

            def step(ins):
                ins.then_inc(v_step, 1)
                steps[0] += 1
                dve.wait_ge(v_step, steps[0])

            def loop_step(i, per):
                base, n = steps[0], [0]

                def inner(ins):
                    ins.then_inc(v_step, 1)
                    n[0] += 1
                    dve.wait_ge(v_step, i * per + (base + n[0]))

                def end(passes):
                    assert n[0] == per, n[0]
                    steps[0] = base + per * passes
                return inner, end

            def over(a, n):
                return a.unsqueeze(1).to_broadcast([a.shape[0], n, a.shape[1]])

            def each(a, n):
                return a.unsqueeze(2).to_broadcast([a.shape[0], a.shape[1], n])

            dve.wait_ge(par_loaded, 16 * 5)
            dve.wait_ge(con_loaded, 16)
            V_.tensor_scalar(PAR[:, :, P_CMUR:P_CMUR + 3], PAR[:, :, P_MUR:P_MUR + 3], -1.0, 1.0, ALU.mult, ALU.add)
            V_.tensor_scalar(PAR[:, :, P_HW0:P_HW0 + 2], PAR[:, :, P_W0:P_W0 + 2], 0.5, None, ALU.mult)
            V_.tensor_scalar(PAR[:, :, P_CKA:P_CKA + 1], PAR[:, :, P_KA:P_KA + 1], -1.0, 1.0, ALU.mult, ALU.add)
            V_.tensor_scalar(MULO[:, 1:2], MULO[:, 0:1], -1.0, 1.0, ALU.mult, ALU.add)
            step(V_.memset(N_T0[:, 0:1], 0.0))
            for b in range(3):
                dve.wait_ge(out_of[b], J_NORM)
            step(V_.reciprocal(N_RS, N_RS))
            for kt in range(KT):
                V_.scalar_tensor_tensor(XN[:, kt, 0:TS], XN[:, kt, 0:TS], GAINS[:, 0, kt:kt + 1], N_RS,
                                        ALU.mult, ALU.mult).then_inc(xn_ready, 1)

            def shift(dst, t0, rest, ready, job):
                for b, (c0, n) in enumerate(XB):
                    dve.wait_ge(mu_ready, ready(b))
                    m = min(n, T - c0)
                    ins = V_.scalar_tensor_tensor(dst[:, c0:c0 + m], bank[b][:, 0:m], rest, t0[:, c0:c0 + m],
                                                  ALU.mult, ALU.add)
                    if b == 2:
                        ins = V_.scalar_tensor_tensor(dst[:, T:TS], bank[b][:, T - c0:TS - c0], rest,
                                                      t0[:, 1 + TS:1 + XC], ALU.mult, ALU.add)
                    ins.then_inc(out_of[b], 1)

            shift(LO, N_T0, MULO[:, 1:2], lambda b: b + 1, J_LO)
            dve.wait_ge(out_of[2], J_LO)
            step(V_.memset(ATT[:, 0:1, 0:1], 0.0))
            V_.memset(GDE, 0.0).then_inc(lo_ready, 1)

            for b in range(3):
                dve.wait_ge(out_of[b], J_GLO)
            step(V_.memset(ATT.rearrange("p a b -> p (a b)"), 0.0))
            with dve.Fori(0, GH) as h:
                st, end = loop_step(h, 10)
                j0 = h * PER_GLA + J_GLA
                V_.memset(SP[0], 0.0).then_inc(g_sp, 1)
                V_.tensor_copy(GCUR, GPAR[:, bass.ds(h, 1)]).then_inc(g_head, 1)
                dve.wait_ge(g_head, h + 1)
                for b, (c0, n) in enumerate(XT):
                    dve.wait_ge(g_abs, h * 3 + (b + 1))
                    V_.tensor_scalar(LA[:, c0:c0 + n], bank[b][:, 0:n], GCUR, 0.0, ALU.add, ALU.min).then_inc(out_of[b], 1)
                dve.wait_ge(out_of[2], j0 + 1)
                dve.wait_ge(g_ln, h + 1)
                st(V_.tensor_tensor(LA, LA, E0, ALU.subtract))
                st(V_.tensor_tensor_scan(GB, CON[:, C_RG:C_RG + T], LA[:, 0:T], 0.0, ALU.mult, ALU.add))
                B3 = GB.rearrange("p (c t) -> p c t", t=CG)
                st(V_.tensor_copy(GDE, B3[:, :, CG // 2 - 1]))
                V_.tensor_tensor(B3, B3, each(GDE, CG), ALU.subtract).then_inc(g_scan, 1)
                dve.wait_ge(g_exp, h * 4 + 4)
                E3 = EPG.rearrange("p (c t) -> p c t", t=CG)
                st(V_.tensor_copy(GF[:, NG - 1:NG], E3[:, NG - 1, CG - 1:CG]))
                st(V_.tensor_tensor(GF[:, 0:NG - 1], E3[:, 0:NG - 1, CG - 1], GDM[:, 1:NG], ALU.mult))
                for b, (c0, n) in enumerate(XT):
                    dve.wait_ge(done[b], j0 + 4)
                    m = min(n, T - c0)
                    ins = V_.tensor_tensor(GK_[:, c0:c0 + m], bank[b][:, 0:m], EMG[:, c0:c0 + m], ALU.mult)
                    if b == 2:
                        ins = V_.tensor_copy(GK_[:, T:TS], bank[b][:, T - c0:TS - c0])
                    ins.then_inc(out_of[b], 1)
                for b, (c0, n) in enumerate(XT):
                    dve.wait_ge(done[b], j0 + 5)
                    m = min(n, T - c0)
                    ins = V_.scalar_tensor_tensor(GQ_[:, c0:c0 + m], bank[b][:, 0:m], DK ** -0.5, EPG[:, c0:c0 + m],
                                                  ALU.mult, ALU.mult)
                    if b == 2:
                        ins = V_.tensor_scalar(GQ_[:, T:TS], bank[b][:, T - c0:TS - c0], DK ** -0.5, None, ALU.mult)
                    ins.then_inc(out_of[b], 1)
                for q in range(2):
                    dve.wait_ge(g_at, h * 2 + (q + 1))
                    dve.nop(nofuse=True)
                    V_.copy_predicated(ATT[:, 4 * q:4 * q + 4, :],
                                       over(CON[:, C_CAUSAL:C_CAUSAL + CG].bitcast(I32), 4),
                                       bank[6][:, :].rearrange("p (a b) -> p a b", b=CG)).then_inc(g_am, 1)
                for c in range(NG):
                    dve.wait_ge(g_sps, h * NG + (c + 1))
                    dve.wait_ge(g_sf, h * NG + (c + 1))
                    V_.scalar_tensor_tensor(SP[(c + 1) % 2], bank[4][:, 0:DV], GF[:, c:c + 1], SF,
                                            ALU.mult, ALU.add).then_inc(g_sp, 1)
                dve.wait_ge(g_v, h * 9 + 9)
                V_.tensor_tensor(VEXP[0:NS, :, :], over(VTM[0:NS, 8, :], NS), each(CON[0:NS, C_DELTA:C_DELTA + NS], DV),
                                 ALU.mult).then_inc(g_vx, 1)
                dve.wait_ge(gs_loaded, h * 16 + 16)
                for q in range(4):
                    dve.wait_ge(g_out, h * 4 + (q + 1))
                    for j in range(2):
                        b = 2 * q + j
                        V_.scalar_tensor_tensor(GS0[:, b, :], GS0[:, b, :], GAS[:, b:b + 1],
                                                bank[3 + 2 * (q % 2)][:, j * DV:(j + 1) * DV],
                                                ALU.mult, ALU.add).then_inc(g_s1, 1)
                for b in range(3):
                    dve.wait_ge(out_of[b], j0 + 6)
                st(V_.reciprocal(E0, E0))
                for vt in range(VT):
                    st(V_.scalar_tensor_tensor(OG[:, vt, :], OG[:, vt, :], GPAR[:, GH + vt:GH + vt + 1], E0,
                                               ALU.mult, ALU.mult))
                    st(V_.scalar_tensor_tensor(MG[:, h * 2 + vt, :], TGB[:, vt, :], 1.0, OG[:, vt, :],
                                               ALU.add, ALU.mult))
                dve.wait_ge(g_stored, h * 32 + 32)
                end(GH)

            for j in range(2):
                step(V_.memset(YB[j].rearrange("p a b -> p (a b)"), 0.0))

            def par1(j):
                return CUR[:, j:j + 1]

            def first_phase(i, s, st):
                j0 = base(i)
                mu0 = i * 9 + 3

                def log_decay():
                    for b in range(3):
                        dve.wait_ge(out_of[b], j0 + 1)
                    st(V_.tensor_scalar(LD, LD, -HALF_DECAY, -HALF_DECAY, ALU.mult, ALU.add))
                    V_.tensor_tensor_scan(B, CON[:, C_RR:C_RR + T], B, 0.0, ALU.mult, ALU.add).then_inc(ldr, 1)

                def rate():
                    for b in range(3):
                        dve.wait_ge(out_of[b], j0 + 2)
                    st(V_.tensor_scalar(A, A, 0.5, 0.5, ALU.mult, ALU.add))
                    st(V_.tensor_scalar(KP, A, par1(P_KA), par1(P_CKA), ALU.mult, ALU.add))

                def shift_block(dst, job, b, rest):
                    c0, n = XB[b]
                    dve.wait_ge(mu_ready, mu0 + (3 * "KRV".index(job) + b + 1))
                    m = min(n, T - c0)
                    ins = V_.scalar_tensor_tensor(dst[:, c0:c0 + m], bank[b][:, 0:m], par1(rest), T0[:, c0:c0 + m],
                                                  ALU.mult, ALU.add)
                    if b == 2:
                        ins = V_.scalar_tensor_tensor(dst[:, T:TS], bank[b][:, T - c0:TS - c0], par1(rest),
                                                      T0[:, 1 + TS:1 + XC], ALU.mult, ALU.add)
                    ins.then_inc(out_of[b], 1)

                def scale_k():
                    dve.wait_ge(out_of[2], j0 + 3)
                    st(V_.tensor_tensor(KP, KP, K, ALU.mult))

                def unit_k(b):
                    c0, n = TB[b]
                    dve.wait_ge(out_of[b], j0 + 5)
                    st(V_.tensor_scalar(EM[:, c0:c0 + n], EM[:, c0:c0 + n], 1e-12, None, ALU.max))
                    st(V_.reciprocal(EM[:, c0:c0 + n], EM[:, c0:c0 + n]))

                def kk():
                    V_.scalar_tensor_tensor(K, K, par1(P_KK), EM, ALU.mult, ALU.mult).then_inc(kk_ready, 1)
                    dve.wait_ge(kk_ready, i + 1)
                    st(V_.tensor_tensor(A, K, A, ALU.mult))

                def keep_samples():
                    dve.wait_ge(out_of[2], j0 + 6)
                    for q, src in ((Q_R, R), (Q_KP, KP), (Q_KK, K), (Q_KA, A), (Q_V, V)):
                        st(V_.tensor_copy(SV[:, q, i, :], src[:, T:TS]))

                def decayed_keys():
                    dve.wait_ge(ept, i * 3 + 3)
                    V_.tensor_tensor(KE, KP[:, 0:T], EM[:, 0:T], ALU.mult).then_inc(gram_in, 1)
                    V_.tensor_tensor(BE, BE, EM[:, 0:T], ALU.mult).then_inc(gram_in, 1)

                for b in range(3):
                    for dst, job, rest in ((K, "K", P_CMUK), (R, "R", P_CMUR), (V, "V", P_CMUV)):
                        if s == ends[job, b] + 1:
                            shift_block(dst, job, b, rest)
                    if s == ends["N", 2] + 2 + 3 * b:
                        unit_k(b)
                if s == ends["W", 2] + 2:
                    log_decay()
                if s == ends["A", 2] + 4:
                    rate()
                if s == ends["K", 2] + 2:
                    scale_k()
                if s == ends["N", 2] + 11:
                    kk()
                if s == SLOTS:
                    keep_samples()
                    decayed_keys()

            def chunk_side(i, s):
                c = s // 3
                if s % 3 == 0:
                    dve.wait_ge(rhs_done, i * NC + (c + 1))
                    V_.tensor_copy(RH, bank[3][:, 0:HD]).then_inc(rhs_ready, 1)
                if s % 3 == 1:
                    dve.wait_ge(u_done, i * NC + (c + 1))
                    V_.tensor_copy(U, bank[4][:, 0:HD]).then_inc(u_ready, 1)
                if s % 3 == 2:
                    dve.wait_ge(s_done, i * NC + (c + 1))
                    dve.wait_ge(s_scaled, i * NC + (c + 1))
                    V_.scalar_tensor_tensor(SS[(c + 1) % 2], bank[5][:, 0:HD], DC[:, c:c + 1], SD,
                                            ALU.mult, ALU.add).then_inc(s_ready, 1)

            def centre(i, job, st):
                st(V_.tensor_copy(LNP, PAR[:, i, P_LNG:P_LNG + 2]))
                dve.wait_ge(o_ready, i * 2 + 2)
                for b, (c0, n) in enumerate(PB):
                    dve.wait_ge(done[b], job)
                    V_.scalar_tensor_tensor(O[:, c0:c0 + n], bank[b][:, 0:n], -1.0 / HD, O[:, c0:c0 + n],
                                            ALU.mult, ALU.add).then_inc(out_of[b], 1)

            def merge(i, job, part, st):
                if part < 3:
                    c0, n = PB[part]
                    dve.wait_ge(out_of[part], job)
                    st(V_.reciprocal(EM[:, c0:c0 + n], EM[:, c0:c0 + n]))
                    st(V_.tensor_tensor(O[:, c0:c0 + n], O[:, c0:c0 + n], EM[:, c0:c0 + n], ALU.mult))
                if part == 3:
                    st(V_.tensor_scalar(O, O, LNP[:, 0:1], LNP[:, 1:2], ALU.mult, ALU.add))
                    st(V_.tensor_tensor(O, O, RK[:, 0:T], ALU.add))
                if part == 4:
                    st(V_.scalar_tensor_tensor(O, TG[:, 0:T], 1.0, O, ALU.add, ALU.mult))
                    st(V_.tensor_copy(STG[:, i, :], TG[:, T:TS]))
                    st(V_.tensor_copy(SB[:, i, :], RK[:, T:TS]))
                    V_.tensor_tensor(MG[:, i, 0:T], MG[:, i, 0:T], O, ALU.add).then_inc(merged, 1)

            def second_phase(i, previous, st):
                job = base(i) + 6
                K3 = K[:, 0:T].rearrange("p (c t) -> p c t", t=CR)
                R3 = R[:, 0:T].rearrange("p (c t) -> p c t", t=CR)
                V_.tensor_tensor(AR[:, :, 0, :], K3, EP[:, :, 0:CR], ALU.mult).then_inc(gram_in, 1)
                V_.tensor_tensor(AR[:, :, 1, :], R3, EP[:, :, 1:CR + 1], ALU.mult).then_inc(gram_in, 1)
                st(V_.tensor_copy(DC, EP[:, :, CR]))
                if previous:
                    centre(i - 1, job + 1, st)
                    job = job + 2
                for q in range(4):
                    cs = slice(4 * q, 4 * q + 4)
                    dve.wait_ge(gram_done, i * 12 + (3 * q + 1))
                    g4 = bank[3][:, :].rearrange("p (c a t) -> p c a t", a=2, t=CR)
                    V_.tensor_tensor(GTB[q // 2][:, 4 * (q % 2):4 * (q % 2) + 4, :].rearrange("p c (h t) -> p c h t", t=CR),
                                     g4[:, :, 0:1, :].to_broadcast([P, 4, 2, CR]),
                                     over(CON[:, C_MGB:C_MGB + 2 * CR], 4).rearrange("p c (h t) -> p c h t", t=CR),
                                     ALU.mult)
                    V_.tensor_tensor(Y[:, cs, :], g4[:, :, 0, :], over(CON[:, C_M2T:C_M2T + CR], 4), ALU.mult)
                    V_.tensor_tensor(GT[:, cs, :], g4[:, :, 1, :], over(CON[:, C_MG + CR:C_MG + 2 * CR], 4),
                                     ALU.mult).then_inc(gram_ready, 1)
                    dve.wait_ge(gram_done, i * 12 + (3 * q + 2))
                    V_.tensor_tensor(AK[:, cs, :, :].rearrange("p c a t -> p c (a t)"),
                                     bank[4][:, :].rearrange("p (c t) -> p c t", t=2 * CR),
                                     over(CON[:, C_MK:C_MK + 2 * CR], 4), ALU.mult).then_inc(gram_ready, 1)
                    dve.wait_ge(gram_done, i * 12 + (3 * q + 3))
                    V_.tensor_tensor(X_[:, cs, :], bank[5][:, 0:4 * CR].rearrange("p (c t) -> p c t", t=CR),
                                     over(CON[:, C_M2:C_M2 + CR], 4), ALU.mult).then_inc(gram_ready, 1)
                dve.wait_ge(gram_ready, i * 12 + 12)
                V_.tensor_tensor(X_, over(IDS, NC), X_, ALU.subtract).then_inc(inv_xr, 1)
                V_.tensor_tensor(Y, over(IDS, NC), Y, ALU.subtract).then_inc(inv_yr, 1)
                for lv in range(len(LEVELS)):
                    for hf in range(2):
                        cs = slice(8 * hf, 8 * hf + 8)
                        lx = bank[3 + hf][:, :].rearrange("p (c t) -> p c t", t=CR)
                        dve.wait_ge(inv_p, i * 10 + (2 * lv + hf + 1))
                        if lv < len(LEVELS) - 1:
                            V_.tensor_tensor(PP[:, cs, :], lx, over(CON[:, C_OFF + 64 * lv:C_OFF + 64 * lv + 64], 8),
                                             ALU.mult).then_inc(inv_c, 1)
                        V_.tensor_tensor(PPB[hf].rearrange("p c (h t) -> p c h t", t=CR),
                                         lx.unsqueeze(2).to_broadcast([P, 8, 2, CR]),
                                         over(CON[:, C_OFFB + 128 * lv:C_OFFB + 128 * lv + 128], 8).rearrange(
                                             "p c (h t) -> p c h t", t=CR), ALU.mult).then_inc(inv_b, 1)
                    for hf in range(2):
                        cs = slice(8 * hf, 8 * hf + 8)
                        if lv < len(LEVELS) - 1:
                            dve.wait_ge(inv_xd, i * 8 + (2 * lv + hf + 1))
                            V_.tensor_tensor(X_[:, cs, :], X_[:, cs, :],
                                             bank[5 + hf][:, :].rearrange("p (c t) -> p c t", t=CR),
                                             ALU.subtract).then_inc(inv_xr, 1)
                        dve.wait_ge(inv_yd, i * 10 + (2 * lv + hf + 1))
                        V_.tensor_tensor(Y[:, cs, :], Y[:, cs, :],
                                         bank[YBANK[hf]][:, :].rearrange("p (c t) -> p c t", t=CR),
                                         ALU.subtract).then_inc(inv_yr, 1)
                        if previous:
                            merge(i - 1, job, 2 * lv + hf, st)
                    if lv == 2:
                        V_.scalar_tensor_tensor(RK, R, par1(P_RK), KP, ALU.mult, ALU.mult).then_inc(rkr, 1)
                for b, (c0, n) in enumerate(TB):
                    dve.wait_ge(done[b], job + 2)
                    V_.tensor_tensor(RK[:, c0:c0 + n], bank[b][:, 0:n], V[:, c0:c0 + n], ALU.mult).then_inc(out_of[b], 1)
                if previous:
                    dve.wait_ge(s_stored, i * 16)
                V_.memset(SS[0], 0.0).then_inc(s_ready, 1)

            def begin(i):
                V_.memset(T0[:, 0:1], 0.0)
                V_.memset(EP[:, :, 0:1], 1.0)
                V_.tensor_copy(CUR[:, 0:NPAR], PAR[:, i, :]).then_inc(p_start, 1)
                dve.wait_ge(p_start, i + 1)

            begin(0)
            for s in range(SLOTS + 1):
                first_phase(0, s, step)
            second_phase(0, False, step)
            with dve.Fori(1, NP) as i:
                st, end = loop_step(i - 1, 29)
                begin(i)
                for s in range(SLOTS):
                    chunk_side(i - 1, s)
                    first_phase(i, s, st)
                first_phase(i, SLOTS, st)
                second_phase(i, True, st)
                end(NP - 1)
            for s in range(SLOTS):
                chunk_side(NP - 1, s)
            centre(NP - 1, J_WO - 1, step)
            for part in range(5):
                merge(NP - 1, J_WO, part, step)
            dve.wait_ge(s_stored, 16 * NP)
            dve.wait_ge(merged, NP)
            V_.memset(ST, 0.0).then_inc(pairs_over, 1)

            dve.wait_ge(sv_ready, 12)
            dve.wait_ge(st_loaded, 16)

            def vec(q):
                return QQ[:, q, :]

            step(V_.tensor_tensor(S2, S0, over(vec(Q_KK), HD), ALU.mult))
            step(V_.tensor_reduce(SA, S2, AX_X, ALU.add))
            step(V_.tensor_tensor(S2, each(SA, HD), over(vec(Q_KA), HD), ALU.mult))
            step(V_.tensor_tensor(S0, S0, over(vec(Q_W), HD), ALU.mult))
            step(V_.tensor_tensor(S0, S0, S2, ALU.subtract))
            dve.wait_ge(pool_step, 1)
            V_.tensor_tensor(S0, S0, S1, ALU.add).then_inc(state_new, 1)
            dve.wait_ge(state_new, 1)
            step(V_.tensor_tensor(S2, S0, over(vec(Q_R), HD), ALU.mult))
            step(V_.tensor_reduce(OO, S2, AX_X, ALU.add))
            step(V_.tensor_reduce(ST[:, 0:1], OO, AX_X, ALU.add))
            step(V_.tensor_scalar(ST[:, 1:2], ST[:, 0:1], 1.0 / HD, None, ALU.mult))
            step(V_.tensor_scalar(OO, OO, ST[:, 1:2], None, ALU.subtract))
            step(V_.tensor_tensor(OSQ, OO, OO, ALU.mult))
            V_.tensor_reduce(ST[:, 3:4], OSQ, AX_X, ALU.add).then_inc(sa_step, 1)
            dve.wait_ge(osq_ready, 1)
            step(V_.reciprocal(ST[:, 5:6], ST[:, 4:5]))
            for e in range(2):
                V_.tensor_scalar(O2[0:64, e * HD:(e + 1) * HD], OO[64 * e:64 * e + 64, :],
                                 ST[64 * e:64 * e + 64, 5:6], None, ALU.mult).then_inc(so_ready, 1)
            dve.wait_ge(a_step, 2 + GH)
            step(V_.tensor_tensor(SO, SO, each(PAR[:, :, P_LNG], NS), ALU.mult))
            step(V_.tensor_tensor(SO, SO, each(PAR[:, :, P_LNB], NS), ALU.add))
            step(V_.tensor_tensor(SO, SO, SB, ALU.add))
            step(V_.scalar_tensor_tensor(SO, STG, 1.0, SO, ALU.add, ALU.mult))
            V_.tensor_tensor(MG[:, :, T:TS], MG[:, :, T:TS], SO, ALU.add).then_inc(mg_ready, 1)

            dve.wait_ge(h_loaded, 16 * KT)
            with dve.Fori(0, KT) as m:
                for b, (c0, n) in enumerate(TB):
                    dve.wait_ge(done[b], m + (J_WO + 1))
                    V_.scalar_tensor_tensor(H[:, m, c0:c0 + n], bank[b][:, 0:n], 0.5, H[:, m, c0:c0 + n],
                                            ALU.mult, ALU.add).then_inc(out_of[b], 1)
            for b in range(3):
                dve.wait_ge(out_of[b], J_N2)
            step(V_.reciprocal(F_RS, F_RS))
            for kt in range(KT):
                V_.scalar_tensor_tensor(XN2[:, kt, :], H[:, kt, :], GAINS[:, 1, kt:kt + 1], F_RS,
                                        ALU.mult, ALU.mult).then_inc(xn2_ready, 1)
            with dve.Fori(0, FT) as ft:
                for b, (c0, n) in enumerate(TB):
                    dve.wait_ge(out_of[b], ft * 2 + (J_FFN + 1))
                    dve.wait_ge(done[b], ft * 2 + (J_FFN + 2))
                    V_.tensor_tensor(ACTV[:, ft, c0:c0 + n], bank[b][:, 0:n], ACTV[:, ft, c0:c0 + n],
                                     ALU.mult).then_inc(out_of[b], 1)
            with dve.Fori(0, KT) as m:
                for b, (c0, n) in enumerate(TB):
                    dve.wait_ge(done[b], m + (J_DOWN + 1))
                    V_.tensor_tensor(H[:, m, c0:c0 + n], bank[b][:, 0:n], H[:, m, c0:c0 + n],
                                     ALU.add).then_inc(out_of[b], 1)
            for b in range(3):
                dve.wait_ge(out_of[b], J_N3)
            step(V_.reciprocal(Y_RS, Y_RS))
            for kt in range(KT):
                V_.scalar_tensor_tensor(H[:, kt, :], H[:, kt, :], GAINS[:, 2, kt:kt + 1], Y_RS,
                                        ALU.mult, ALU.mult).then_inc(yn_ready, 1)


def constants():
    import numpy as np
    c = np.zeros((P, NCONST), np.float32)
    t = np.arange(P) % HD
    j = np.arange(CR)
    eye = np.eye(HD, dtype=np.float32)
    c[:, C_ONES:C_ONES + 128] = 1
    c[:, C_BONES:C_BONES + 128] = np.arange(P)[:, None] // HD == np.arange(P)[None] // HD
    c[:, C_ID:C_ID + 128] = np.eye(P)
    c[:, C_IDS:C_IDS + 64] = np.concatenate([eye, eye])
    c[:, C_NIDS:C_NIDS + 64] = -np.concatenate([eye, eye])
    strict = t[:, None] < j[None]
    incl = t[:, None] <= j[None]
    c[:, C_MG:C_MG + 64], c[:, C_MG + 64:C_MG + 128] = strict, -1.0 * incl
    head = (np.arange(P)[:, None] // HD == np.arange(P)[None] // HD)
    c[:, C_MGB:C_MGB + 128] = head & np.tile(strict, (1, 2))
    c[:, C_MK:C_MK + 64], c[:, C_MK + 64:C_MK + 128] = strict, incl
    c[:, C_ML:C_ML + 64] = t[:, None] > j[None]
    pair = (t[:, None] // 2 == j[None] // 2)
    c[:, C_M2:C_M2 + 64] = pair & (t[:, None] > j[None])
    c[:, C_M2T:C_M2T + 64] = pair & (t[:, None] < j[None])
    for n, m in enumerate(LEVELS):
        off = (t[:, None] // (2 * m) == j[None] // (2 * m)) & (t[:, None] // m > j[None] // m)
        c[:, C_OFF + 64 * n:C_OFF + 64 * n + 64] = off
        c[:, C_OFFB + 128 * n:C_OFFB + 128 * n + 128] = head & np.tile(off, (1, 2))
    c[:, C_RR:C_RR + T] = np.arange(T) % CR != 0
    c[:, C_RG:C_RG + T] = np.arange(T) % CG != 0
    c[:, C_CAUSAL:C_CAUSAL + CG] = np.arange(P)[:, None] <= np.arange(CG)[None]
    c[:NS, C_DELTA:C_DELTA + NS] = np.eye(NS)
    c[:, C_EPS:C_EPS + 3] = np.array([NORM_EPS, GN_EPS, GLA_EPS], np.float32)
    return c


def kernel(**inputs):
    import numpy as np
    import concourse.bacc as bacc
    from concourse.bass_utils import run_bass_kernel_spmd as run
    a = {k: np.asarray(v) for k, v in inputs.items()}

    def chans(x):
        return x.T.reshape(KT, P, -1)

    def tiles(w, c0, n):
        return w[:, c0:c0 + n].reshape(-1, P, n).transpose(1, 0, 2).reshape(P, -1)

    w = a["w_in"][0]
    q0, k0, v0, gl0, ga0, gb0 = 3200, 3712, 4224, 5248, 5264, 6288
    wgu, wd = a["ffn_w_gu"][0], a["ffn_w_down"][0]
    mu = a["mu_shift"][0]
    percol = [mu[0:D], mu[D:2 * D], mu[2 * D:3 * D], a["rwkv_w0"][0], a["rwkv_a0"][0], a["rwkv_k_k"][0],
              a["rwkv_k_a"][0], a["rwkv_r_k"][0].reshape(D), a["rwkv_lnx_g"][0], a["rwkv_lnx_b"][0]]
    ins = {
        "xT": np.concatenate([chans(a["x_prompt"][0]), chans(a["x_sample"][:, 0])], 2),
        "prevT": chans(a["state_shift"][0]).transpose(1, 0, 2),
        "gains": np.stack([a["norm_mix"][0], a["norm_ffn"][0], a["norm_final"]]).reshape(3, KT, P).transpose(2, 0, 1),
        "consts": constants(),
        "w_lo": tiles(w, 3072, 128),
        "w_glo": tiles(w, gl0, 16),
        "mu_lo": mu[3072:3200].reshape(P, 1),
        "w_gla": np.stack([np.concatenate([tiles(w, q0 + h * DK, DK), tiles(w, k0 + h * DK, DK),
                                           tiles(w, v0 + h * DV, DV), tiles(w, gb0 + h * DV, 128),
                                           tiles(w, gb0 + h * DV + 128, 128)], 1) for h in range(GH)]),
        "w_gla2": np.stack([a["gla_a2"][0][:, h * DK:(h + 1) * DK] for h in range(GH)]),
        "glapar": np.concatenate([a["gla_ab"][0].reshape(GH, DK).T, a["gla_norm_g"][0].reshape(VT, P).T], 1),
        "w_pair": np.stack([np.concatenate([tiles(w, i * 128, 128), tiles(w, D + i * 128, 128),
                                            tiles(w, 2 * D + i * 128, 128), tiles(w, ga0 + i * 128, 128),
                                            np.concatenate([a["rwkv_w2"][0][:, i * 128:i * 128 + 128],
                                                            a["rwkv_a2"][0][:, i * 128:i * 128 + 128]], 0)], 1)
                            for i in range(NP)]),
        "par": np.stack(percol, 1).reshape(NP, P, 10).transpose(1, 0, 2),
        "gla_s": a["state_gla"][0].transpose(1, 2, 0, 3).reshape(GH, DK, NS * DV),
        "wkv_s": a["state_wkv"][0].reshape(NS, NP, 2, HD * HD).transpose(2, 1, 0, 3).reshape(P, HD * HD),
        "w_o": np.stack([tiles(a["w_o"][0], m * 128, 128) for m in range(KT)]),
        "w_gu": np.stack([np.concatenate([tiles(wgu, f * 128, 128), tiles(wgu, F + f * 128, 128)], 1)
                          for f in range(FT)]),
        "w_d": np.stack([tiles(wd, m * 128, 128) for m in range(KT)]),
    }
    ins = {k: np.ascontiguousarray(v) for k, v in ins.items()}
    outs = {"yT": (KT, P, TS), "shT": (P, KT, 1 + NS), "wkvp": (NP, P, HD), "glap": (GH, DK, DV),
            "wkvs": (P, HD * HD), "glas": (GH, DK, NS * DV)}
    nc = bacc.Bacc("TRN2", target_bir_lowering=False, num_devices=1)
    args = [nc.dram_tensor("in_" + k, v.shape, F32, kind="ExternalInput").ap() for k, v in ins.items()]
    args += [nc.dram_tensor("out_" + k, s, F32, kind="ExternalOutput").ap() for k, s in outs.items()]
    hybrid_step(nc, *args)
    res = run(nc, [{"in_" + k: v for k, v in ins.items()}], core_ids=[0]).results[0]
    r = {k: np.asarray(res["out_" + k]) for k in outs}
    y = r["yT"].reshape(D, TS).T
    sh = r["shT"].transpose(2, 1, 0).reshape(1 + NS, D)
    wkvp = r["wkvp"].reshape(NP * 2, HD, HD).transpose(0, 2, 1)
    wkvs = r["wkvs"].reshape(2, NP, NS, HD, HD).transpose(2, 1, 0, 3, 4).reshape(NS, 2 * NP, HD, HD)
    glas = r["glas"].reshape(GH, DK, NS, DV).transpose(2, 0, 1, 3)
    return tuple(np.ascontiguousarray(v) for v in (
        y[None, :T], y[T:, None], sh[None, :1], wkvp[None, None], r["glap"][None, None],
        sh[None, 1:], wkvs[None], glas[None]))
```

```python
from contextlib import ExitStack

import concourse.bass as bass
from concourse import mybir

F32 = mybir.dt.float32
F32R = mybir.dt.float32r
I32 = mybir.dt.int32
ACT = mybir.ActivationFunctionType
ALU = mybir.AluOpType
AX_X = mybir.AxisListType.X

P = 128
D = 1024
KT = D // P
T = 1024
NS = 8
TS = T + NS
XC = T + 2 * NS
HD = 64
NP = D // P
CR = 64
NC = T // CR
GH = 4
DK = 128
DV = 256
VT = DV // P
CG = 128
NG = T // CG
F = 2816
FT = F // P
NORM_EPS = 1e-6
GN_EPS = 64e-5
GLA_EPS = 1e-5
GATE_NORM = 16.0
HALF_DECAY = 0.5 * float(2.718281828459045) ** -0.5

XB = [(0, 348), (348, 346), (694, 346)]
XT = [(0, 348), (348, 346), (694, 338)]
TB = [(0, 344), (344, 344), (688, 344)]
PB = [(0, 342), (342, 342), (684, 340)]

LEVELS = [2, 4, 8, 16, 32]
C_ONES, C_BONES, C_ID, C_IDS, C_NIDS = 0, 128, 256, 384, 448
C_MG, C_MK, C_ML, C_M2, C_M2T, C_OFF = 512, 640, 768, 832, 896, 960
C_MGB = C_OFF + 64 * len(LEVELS)
C_OFFB = C_MGB + 128
C_RR = C_OFFB + 128 * len(LEVELS)
C_RG = C_RR + T
C_CAUSAL = C_RG + T
C_DELTA = C_CAUSAL + 128
C_EPS = C_DELTA + NS
NCONST = C_EPS + 3

(P_MUR, P_MUK, P_MUV, P_W0, P_A0, P_KK, P_KA, P_RK, P_LNG, P_LNB) = range(10)
P_CMUR, P_CMUK, P_CMUV, P_HW0, P_HA0, P_CKA = range(10, 16)
NPAR = 16

W_R, W_K, W_V, W_G = 0, 1024, 2048, 3072
W_LORA = 4096
WP = 4224
G_Q, G_K, G_V, G_B = 0, 1024, 2048, 4096
WG = 6144


def hybrid_step(nc, xT, prevT, gains, consts, w_lo, w_glo, mu_lo, w_gla, w_gla2, glapar, w_pair, par,
                gla_s, wkv_s, w_o, w_gu, w_d, yT, shT, wkvp, glap, wkvs, glas):
    with ExitStack() as ctx:
        def rounded(name, off, n):
            with ExitStack() as below:
                if off:
                    below.enter_context(nc.sbuf_tensor(name + "_below", [P, off], F32))
                return below.enter_context(nc.sbuf_tensor(name, [P, n], F32R))

        A0 = 24832 + NCONST + 3 * KT
        A0 += -A0 % 8
        WOUT, WFFN = A0 + 8264, 24832 + C_BONES
        MGHR = [rounded(f"merged_high{kt}", kt * TS, TS) for kt in range(KT)]
        MGLR = [rounded(f"merged_low{kt}", 8320 + kt * TS, TS) for kt in range(KT)]
        WOHR = [rounded(f"wo_high{j}", WOUT + 1024 * j, D) for j in range(2)]
        WOLR = [rounded(f"wo_low{j}", WOUT + 2048 + 1024 * j, D) for j in range(2)]
        XHR = MGHR
        XLR = [rounded(f"x_low{kt}", 8256 + kt * TS, TS) for kt in range(KT)]
        WGHR = [rounded(f"gate_up_high{q}", WFFN + 2048 * q, D) for q in range(2)]
        WGLR = [rounded(f"gate_up_low{q}", WFFN + 2048 * q + 1024, D) for q in range(2)]
        arena = ctx.enter_context(nc.sbuf_tensor("arena", [P, 53200], F32))
        bank = [ctx.enter_context(nc.psum_tensor(f"bank{n}", [P, 512], F32)) for n in range(8)]

        def sem(name):
            return ctx.enter_context(nc.semaphore(name))

        def at(off, *dims):
            n = 1
            for d in dims:
                n *= d
            assert off + n <= 53200
            v = arena[:, off:off + n]
            if len(dims) == 1:
                return v
            names = "abcd"[:len(dims)]
            return v.rearrange("p (" + " ".join(names) + ") -> p " + " ".join(names),
                               **{names[j]: dims[j] for j in range(1, len(dims))})

        XN = at(0, KT, XC)
        MG = at(8320, KT, TS)
        WB = at(16576, WG)
        PAR = at(22720, NP, NPAR)
        MULO = at(22880, 2)
        GPAR = at(22882, GH + VT)
        CUR = at(22890, 24)
        GCUR = at(22914, 1)
        LO = at(22920, XC)
        SMALL = 23960
        CON = at(24832, NCONST)
        ONES = CON[:, C_ONES:C_ONES + 128]
        BONES = CON[:, C_BONES:C_BONES + 128]
        IDF = CON[:, C_ID:C_ID + 128]
        IDS = CON[:, C_IDS:C_IDS + 64]
        NIDS = CON[:, C_NIDS:C_NIDS + 64]
        GAINS = at(24832 + NCONST, 3, KT)

        EPS = [CON[:, C_EPS + j:C_EPS + j + 1] for j in range(3)]

        N_SQ = [at(A0 + 1032 * j, TS) for j in range(2)]
        N_RS = at(A0 + 2064, TS)
        N_WLO = at(A0 + 3096, KT, 128)
        N_T0 = at(A0 + 4120, 1 + XC)
        N_WGLO = at(A0 + 5168, KT, 16)
        o = A0
        def take(n):
            nonlocal o
            s = o
            o += n + (-n % 8)
            return s
        GLO = at(take(XC), XC)
        E0 = at(take(TS), TS)
        LA = at(take(TS), TS)
        GB = at(take(T), T)
        EPG = at(take(T), T)
        EMG = at(take(T), T)
        GK_ = at(take(TS), TS)
        GQ_ = at(take(TS), TS)
        TGB = at(take(2 * TS), VT, TS)
        VTM = at(take(9 * DV), 9, DV)
        ATT = at(take(T), NG, CG)
        KTM = at(take(T), NG, CG)
        OG = at(take(2 * TS), VT, TS)
        SP = [at(take(DV), DV) for _ in range(2)]
        SF = at(take(DV), DV)
        GSQ = at(take(2 * TS), VT, TS)
        GS0 = at(take(NS * DV), NS, DV)
        VEXP = at(take(NS * DV), NS, DV)
        GKS = at(take(128), 128)
        GA2 = at(take(128), 128)
        GDM = at(take(NG), NG)
        GDE = at(take(NG), NG)
        GF = at(take(NG), NG)
        GAS = at(take(NS), NS)
        gla_end = o
        o = A0
        t0ofs = take(1 + XC)
        T0 = at(t0ofs, 1 + XC)
        X_ = at(t0ofs, NC, CR)
        kofs = take(TS)
        K = at(kofs, TS)
        R = at(take(TS), TS)
        V = at(take(TS), TS)
        aofs = take(TS)
        A = at(aofs, TS)
        BE = at(aofs, T)
        PPB = [at(aofs + 1024 * j, 8, 2 * CR) for j in range(2)]
        KE = at(take(T), T)
        ldofs = take(TS)
        LD = at(ldofs, TS)
        B = at(ldofs, T)
        PP = at(ldofs, NC, CR)
        KP = at(take(TS), TS)
        KP_END = o
        EM = at(take(TS), TS)
        epofs = take(NC * 65)
        EP = at(epofs, NC, 65)
        GTB = [at(epofs, 8, 2 * CR), at(16576 + WP, 8, 2 * CR)]
        RK = at(take(TS), TS)
        TG = at(take(TS), TS)
        O = at(take(T), T)
        AR = at(take(2 * T), NC, 2, CR)
        GT = at(take(T), NC, CR)
        AK = at(take(2 * T), NC, 2, CR)
        Y = at(take(T), NC, CR)
        YB = [at(take(T), 8, 2 * CR), CON[:, C_RG:C_RG + T].rearrange("p (a b) -> p a b", b=2 * CR)]
        VTT = at(take(T), NC, CR)
        KTT = at(take(T), NC, CR)
        BTT = at(take(T), NC, CR)
        SS = [at(take(HD), HD) for _ in range(2)]
        SD = at(take(HD), HD)
        RH = at(take(HD), HD)
        U = at(take(HD), HD)
        DC = at(take(NC), NC)
        LNP = at(take(2), 2)
        pair_end = o
        assert max(gla_end, pair_end) <= 53200, (gla_end, pair_end)
        Q_R, Q_KP, Q_V, Q_KK, Q_KA, Q_W = range(6)
        SV = at(SMALL, 6, NP, NS)
        SB = at(SMALL + 384, NP, NS)
        STG = at(SMALL + 448, NP, NS)
        SO = at(SMALL + 512, NP, NS)
        SM_END = SMALL + 576
        assert SM_END <= 24832
        S0 = at(16576, HD, HD)
        S1 = at(A0 + 4096, HD, HD)
        S2 = at(A0, HD, HD)
        s_ = 16576 + 4096
        QQ = at(s_, 6, HD)
        SA = at(s_ + 384, HD)
        OO = at(s_ + 448, HD)
        ST = at(s_ + 512, 8)
        O2 = at(s_ + 520, 2 * HD)
        OSQ = at(s_ + 648, HD)
        assert s_ + 712 <= 22720 and KP_END >= A0 + 8192
        assert KP_END == WOUT
        f_ = WOUT
        WOL = [at(f_ + 2048 + 1024 * j, KT, 128) for j in range(2)]
        F_SQ = [at(A0 + TS * kt, TS) for kt in range(KT)]
        F_RS = at(f_ + 4096, TS)
        XL = at(8256, KT, TS)
        H = at(16576, KT, TS)
        w_ = WFFN
        WGL = [at(w_ + 2048 * j + 1024, KT, 128) for j in range(2)]
        assert C_BONES + 4096 <= C_EPS and C_ONES + 128 <= C_BONES
        f0 = A0
        ACTV = at(f0, FT, TS)
        assert f0 + FT * TS <= 53200, f0
        KH = FT // 2
        WD0 = [at(w_ + 2048 * j, KH, 128) for j in range(2)]
        WD = [at(8320 + 4096, FT, 128), at(8320, FT, 128)]
        Y_SQ = [at(TS * kt, TS) for kt in range(KT)]
        Y_RS = at(WFFN, TS)

        x_loaded, con_loaded, par_loaded = sem("x_loaded"), sem("con_loaded"), sem("par_loaded")
        lo_w_loaded = sem("lo_w_loaded")
        done = [sem(f"bank{b}_done") for b in range(3)]
        out_of = [sem(f"bank{b}_evacuated") for b in range(3)]
        sq_ready, sq_used, rs_ready, xn_ready = sem("sq_ready"), sem("sq_used"), sem("rs_ready"), sem("xn_ready")
        v_step = sem("vector_step")
        a_step = sem("scalar_step")
        lo_ready = sem("lo_ready")
        mu_ready = sem("mu_ready")
        gw_loaded = sem("gla_weights_loaded")
        gs_loaded = sem("gla_state_loaded")
        g_abs = sem("gla_abs_done")
        g_ln = sem("gla_ln_done")
        g_scan = sem("gla_decay_sum_ready")
        g_exp = sem("gla_decays_ready")
        g_vps = sem("gla_v_done")
        g_v = sem("gla_v_ready")
        g_at = sem("gla_att_done")
        g_am = sem("gla_att_ready")
        g_kt = sem("gla_kt_done")
        g_ktm = sem("gla_kt_ready")
        g_sp = sem("gla_state_ready")
        g_sf = sem("gla_state_scaled")
        g_sps = sem("gla_update_done")
        g_ops = sem("gla_out_done")
        g_og = sem("gla_out_ready")
        g_sq = sem("gla_square_ready")
        g_rt = sem("gla_root_ready")
        g_kst = sem("gla_samplek_done")
        g_ksm = sem("gla_samplek_ready")
        g_vx = sem("gla_samplev_ready")
        g_out = sem("gla_outer_done")
        g_s1 = sem("gla_sample_state_ready")
        g_os = sem("gla_sample_out_done")
        g_stored = sem("gla_stored")
        g_head = sem("gla_head_done")
        pw = sem("pair_weights_loaded")
        p_start = sem("pair_buffers_free")
        kk_ready = sem("kk_ready")
        merged = sem("pair_merged")
        pairs_over = sem("pairs_over")
        ksq = sem("k_square_ready")
        kln = sem("k_square_logs_ready")
        knorm = sem("k_inverse_length_ready")
        dev_ready = sem("inverse_deviation_ready")
        ldr = sem("decay_sum_ready")
        ept = sem("decays_ready")
        rkr = sem("bonus_product_ready")
        gram_in = sem("gram_inputs_ready")
        tr_done = sem("transposes_done")
        tr_ready = sem("transposes_ready")
        gram_done = sem("gram_done")
        gram_ready = sem("gram_ready")
        inv_p = sem("inverse_LX_done")
        inv_c, inv_b = sem("inverse_LX_ready"), sem("inverse_LX_blocks_ready")
        inv_xd, inv_yd = sem("inverse_X_step_done"), sem("inverse_Y_step_done")
        inv_xr, inv_yr, inv_yb = sem("inverse_X_ready"), sem("inverse_Y_ready"), sem("inverse_Y_blocks_ready")
        rhs_done, rhs_ready = sem("rhs_done"), sem("rhs_ready")
        u_done, u_ready = sem("u_done"), sem("u_ready")
        s_done, s_ready, s_scaled = sem("state_update_done"), sem("state_ready"), sem("state_scaled")
        o_done, o_ready = sem("pair_out_done"), sem("pair_out_ready")
        var_sq = sem("centred_square_ready")
        s_stored = sem("pair_state_stored")
        state_new = sem("sample_state_ready")
        st_loaded = sem("sample_state_loaded")
        sv_done = sem("sample_values_transposed")
        sv_ready = sem("sample_values_ready")
        pool_step = sem("gpsimd_step")
        sa_step = sem("sample_vector_step")
        so_ready, so_done = sem("sample_out_ready"), sem("sample_out_transposed")
        osq_ready = sem("sample_root_ready")
        mg_ready = sem("merged_ready")
        h_loaded = sem("h_loaded")
        wo_loaded = [sem(f"wo_loaded{j}") for j in range(2)]
        mg_hi, mg_lo = sem("merged_high_ready"), sem("merged_low_ready")
        wo_hi, wo_lo = sem("wo_high_ready"), sem("wo_low_ready")
        sq2, sq3 = sem("ffn_square_ready"), sem("final_square_ready")
        xn2_ready, x_hi, x_lo = sem("ffn_input_ready"), sem("ffn_input_high_ready"), sem("ffn_input_low_ready")
        gu_loaded = [sem(f"gate_up_loaded{j}") for j in range(2)]
        gu_hi, gu_lo = sem("gate_up_high_ready"), sem("gate_up_low_ready")
        wd0_loaded = [sem(f"first_down_loaded{j}") for j in range(2)]
        wd_loaded = [sem(f"down_loaded{j}") for j in range(2)]
        yn_ready = sem("y_ready")
        stored, shift_stored = sem("stored"), sem("shift_stored")

        J_NORM, J_LO, J_GLO = 1, 2, 3
        J_GLA, PER_GLA = 3, 6
        J_PAIR, PER_PAIR = J_GLA + GH * PER_GLA, 10
        J_WO = J_PAIR + NP * PER_PAIR
        J_N2 = J_WO + KT + 1
        J_FFN = J_N2
        J_DOWN = J_FFN + 2 * FT
        J_N3 = J_DOWN + KT + 1

        SLOTS = 3 * NC
        PRODUCTS = [(job, b, kt, n) for job, n in (("W", 1), ("A", 1), ("K", KT), ("R", KT), ("N", 1), ("V", KT))
                    for b in range(3) for kt in range(n)]

        SPREAD = len(PRODUCTS) - 6

        def slot(m):
            return m * (SLOTS - 1) // SPREAD if m < SPREAD else SLOTS

        ends = {(job, b): slot(m) for m, (job, b, kt, n) in enumerate(PRODUCTS) if kt == n - 1}
        JOB = {"W": 1, "A": 2, "K": 3, "R": 4, "N": 5, "V": 6}

        def base(i):
            return J_PAIR if isinstance(i, int) and i == 0 else i * PER_PAIR + (J_PAIR - 2)

        YBANK = (7, 4)

        block = ctx.enter_context(nc.Block())

        @block.sync
        def _(sp):
            for kt in range(KT):
                sp.dma_start(XN[:, kt, 0:TS], xT[kt, :, :]).then_inc(x_loaded, 16)
            sp.dma_start(CON, consts[:, :]).then_inc(con_loaded, 16)
            sp.dma_start(N_WLO, w_lo.rearrange("p (k n) -> p k n", n=128)).then_inc(lo_w_loaded, 16)
            sp.dma_start(N_WGLO, w_glo.rearrange("p (k n) -> p k n", n=16)).then_inc(lo_w_loaded, 16)
            sp.dma_start(XN[:, :, TS:XC], prevT[:, :, :]).then_inc(par_loaded, 16)
            sp.dma_start(PAR[:, :, 0:10], par[:, :, :]).then_inc(par_loaded, 16)
            sp.dma_start(GAINS, gains[:, :, :]).then_inc(par_loaded, 16)
            sp.dma_start(MULO[:, 0:1], mu_lo[:, :]).then_inc(par_loaded, 16)
            sp.dma_start(GPAR, glapar[:, :]).then_inc(par_loaded, 16)
            with sp.Fori(0, GH) as h:
                sp.wait_ge(done[2], h * PER_GLA + (J_GLA - 1))
                sp.dma_start(WB, w_gla[h, :, :]).then_inc(gw_loaded, 16)
                sp.dma_start(GA2[0:16, :], w_gla2[h, :, :]).then_inc(gw_loaded, 16)
            sp.wait_ge(done[2], J_PAIR - 1)
            sp.dma_start(WB[:, 0:WP], w_pair[0, :, :]).then_inc(pw, 16)
            with sp.Fori(1, NP) as i:
                sp.wait_ge(done[2], i * PER_PAIR + (J_PAIR - 3))
                sp.dma_start(WB[:, 0:WP], w_pair[i, :, :]).then_inc(pw, 16)
            sp.wait_ge(done[2], J_WO - 3)
            sp.dma_start(S0.rearrange("p a b -> p (a b)"), wkv_s[:, :]).then_inc(st_loaded, 16)
            sp.wait_ge(pairs_over, 1)
            for m in range(2):
                sp.dma_start(WOL[m], w_o[m, :, :].rearrange("p (k n) -> p k n", n=128)).then_inc(wo_loaded[m], 16)
            sp.wait_ge(state_new, 1)
            sp.dma_start(wkvs[:, :], S0.rearrange("p a b -> p (a b)")).then_inc(stored, 16)
            sp.wait_ge(mg_ready, 1)
            sp.wait_ge(stored, 16)
            for kt in range(KT):
                sp.dma_start(H[:, kt, :], xT[kt, :, :]).then_inc(h_loaded, 16)
            for q in range(2):
                sp.dma_start(WGL[q].rearrange("p k n -> p (k n)"), w_gu[0, :, q * D:(q + 1) * D]).then_inc(gu_loaded[q], 16)
            with sp.Fori(0, KT // 2 - 1) as g:
                for j in range(2):
                    sp.wait_ge(done[2], g * 2 + (J_WO + 1 + j))
                    sp.dma_start(WOL[j], w_o[g * 2 + (2 + j), :, :].rearrange("p (k n) -> p k n", n=128)
                                 ).then_inc(wo_loaded[j], 16)
            with sp.Fori(1, FT) as ft:
                for q in range(2):
                    sp.wait_ge(done[2], ft * 2 + (J_FFN - 1 + q))
                    sp.dma_start(WGL[q].rearrange("p k n -> p (k n)"), w_gu[ft, :, q * D:(q + 1) * D]
                                 ).then_inc(gu_loaded[q], 16)
            for j in range(2):
                sp.wait_ge(done[2], J_DOWN - 1 + j)
                sp.dma_start(WD0[j].rearrange("p k n -> p (k n)"), w_d[0, :, j * KH * P:(j + 1) * KH * P]
                             ).then_inc(wd0_loaded[j], 16)
            for m in range(1, KT):
                if m > 2:
                    sp.wait_ge(done[2], J_DOWN + m - 1)
                sp.dma_start(WD[m % 2].rearrange("p k n -> p (k n)"), w_d[m, :, :]).then_inc(wd_loaded[m % 2], 16)
            for kt in range(KT):
                sp.wait_ge(yn_ready, kt + 1)
                sp.dma_start(yT[kt, :, :], H[:, kt, :]).then_inc(stored, 16)
            sp.wait_ge(g_stored, 32 * GH)
            sp.wait_ge(s_stored, 16 * NP)
            sp.wait_ge(shift_stored, 16)
            sp.wait_ge(stored, 16 * (1 + KT))

        @block.gpsimd
        def _(pool):
            pool.wait_ge(xn_ready, KT)
            pool.dma_start(shT[:, :, :], XN[:, :, T - 1:TS]).then_inc(shift_stored, 16)
            with pool.Fori(0, GH) as h:
                pool.wait_ge(g_head, h + 1)
                pool.nop(nofuse=True)
                pool.dma_start(GS0, gla_s[h, :, :].rearrange("p (b v) -> p b v", v=DV)).then_inc(gs_loaded, 16)
                pool.wait_ge(g_sp, h * (NG + 1) + (NG + 1))
                pool.nop(nofuse=True)
                pool.dma_start(glap[h, :, :], SP[0]).then_inc(g_stored, 16)
                pool.wait_ge(g_s1, h * NS + NS)
                pool.nop(nofuse=True)
                pool.dma_start(glas[h, :, :].rearrange("p (b v) -> p b v", v=DV), GS0).then_inc(g_stored, 16)
            with pool.Fori(0, NP) as i:
                pool.wait_ge(s_ready, i * (NC + 1) + (NC + 1))
                pool.nop(nofuse=True)
                pool.dma_start(wkvp[i, :, :], SS[0]).then_inc(s_stored, 16)
            pool.wait_ge(sv_ready, 12)
            nc.gpsimd.tensor_tensor(S1, QQ[:, Q_V, :].unsqueeze(2).to_broadcast([P, HD, HD]),
                                    QQ[:, Q_KP, :].unsqueeze(1).to_broadcast([P, HD, HD]), ALU.mult).then_inc(pool_step, 1)

        @block.tensor
        def _(pe):
            def mm(out, lhsT, rhs, start, stop):
                return nc.tensor.matmul(out, lhsT, rhs, start=start, stop=stop)

            def gate(s, value):
                pe.wait_ge(s, value)
                pe.nop(nofuse=True)

            def project(weight, src, blocks, before):
                for b, (c0, n) in enumerate(blocks):
                    gate(out_of[b], before)
                    for kt in range(KT):
                        last = mm(bank[b][0:weight(kt).shape[1], 0:n], weight(kt), src[:, kt, c0:c0 + n],
                                  kt == 0, kt == KT - 1)
                    last.then_inc(done[b], 1)

            pe.wait_ge(con_loaded, 16)
            for kt in range(KT):
                pe.wait_ge(sq_ready, kt + 1)
                for b, (c0, n) in enumerate(TB):
                    last = mm(bank[b][:, 0:n], ONES, N_SQ[kt % 2][:, c0:c0 + n], kt == 0, kt == KT - 1)
                    if kt == KT - 1:
                        last.then_inc(done[b], 1)
                    elif b == 2:
                        last.then_inc(sq_used, 1)
            pe.wait_ge(lo_w_loaded, 32)
            pe.wait_ge(xn_ready, KT)
            pe.wait_ge(par_loaded, 16 * 5)
            project(lambda kt: N_WLO[:, kt, :], XN, XB, J_NORM)
            project(lambda kt: N_WGLO[:, kt, :], XN, XB, J_LO)

            with pe.Fori(0, GH) as h:
                j0 = h * PER_GLA + J_GLA
                gate(gw_loaded, h * 32 + 32)
                gate(g_head, h + 1)
                for b, (c0, n) in enumerate(XT):
                    gate(out_of[b], j0)
                    mm(bank[b][:, 0:n], GA2[0:16, :], GLO[0:16, c0:c0 + n], True, True).then_inc(done[b], 1)
                for vt in range(VT):
                    project(lambda kt: WB[:, G_B + vt * 1024 + kt * 128:G_B + vt * 1024 + kt * 128 + 128],
                            XN, XT, j0 + (1 + vt))
                for tt in range(9):
                    rows = P if tt < 8 else NS
                    if tt >= 2:
                        gate(g_v, h * 9 + (tt - 1))
                    for kt in range(KT):
                        last = mm(bank[3 + tt % 2][0:rows, 0:DV], XN[:, kt, tt * P:tt * P + rows],
                                  WB[:, G_V + kt * DV:G_V + (kt + 1) * DV], kt == 0, kt == KT - 1)
                    last.then_inc(g_vps, 1)
                project(lambda kt: WB[:, G_K + kt * 128:G_K + kt * 128 + 128], XN, XT, j0 + 3)
                project(lambda kt: WB[:, G_Q + kt * 128:G_Q + kt * 128 + 128], XN, XT, j0 + 4)
                for q in range(2):
                    if q == 0:
                        gate(out_of[2], j0 + 4)
                    else:
                        gate(g_ktm, h * 2 + 1)
                    for c in range(4):
                        cc = 4 * q + c
                        last = nc.tensor.transpose(bank[5][:, c * CG:(c + 1) * CG],
                                                   GK_[:, cc * CG:(cc + 1) * CG], IDF)
                    last.then_inc(g_kt, 1)
                    if q == 0:
                        gate(out_of[2], j0 + 5)
                    else:
                        gate(g_am, h * 2 + 1)
                    for c in range(4):
                        cc = 4 * q + c
                        last = mm(bank[6][:, c * CG:(c + 1) * CG], GK_[:, cc * CG:(cc + 1) * CG],
                                  GQ_[:, cc * CG:(cc + 1) * CG], True, True)
                    last.then_inc(g_at, 1)
                gate(g_ktm, h * 2 + 2)
                gate(g_am, h * 2 + 2)
                gate(g_v, h * 9 + 9)
                for c in range(NG):
                    gate(g_sp, h * (NG + 1) + (c + 1))
                    mm(bank[4][:, 0:DV], KTM[:, c, :], VTM[:, c, :], True, True).then_inc(g_sps, 1)
                    if c:
                        gate(g_og, h * (NG + 1) + c)
                    for vt in range(VT):
                        mm(bank[7][:, vt * CG:(vt + 1) * CG], VTM[:, c, vt * P:(vt + 1) * P], ATT[:, c, :],
                           True, False)
                        last = mm(bank[7][:, vt * CG:(vt + 1) * CG], SP[c % 2][:, vt * P:(vt + 1) * P],
                                  GQ_[:, c * CG:(c + 1) * CG], False, True)
                    last.then_inc(g_ops, 1)
                mm(bank[3][0:NS, 0:P], GK_[:, T:TS], IDF, True, True).then_inc(g_kst, 1)
                gate(g_ksm, h + 1)
                gate(g_vx, h + 1)
                for q in range(4):
                    if q >= 2:
                        gate(g_s1, h * NS + (2 * q - 2))
                    mm(bank[3 + 2 * (q % 2)][:, :], GKS[0:NS, :],
                       VEXP[0:NS, 2 * q:2 * q + 2, :].rearrange("p a b -> p (a b)"), True, True).then_inc(g_out, 1)
                gate(g_s1, h * NS + NS)
                for b in range(NS):
                    for vt in range(VT):
                        last = mm(bank[6][:, vt * NS + b:vt * NS + b + 1], GS0[:, b, vt * P:(vt + 1) * P],
                                  GQ_[:, T + b:T + b + 1], True, True)
                last.then_inc(g_os, 1)
                gate(g_sq, h + 1)
                for b, (c0, n) in enumerate(TB):
                    gate(out_of[b], j0 + 5)
                    for vt in range(VT):
                        last = mm(bank[b][:, 0:n], ONES, GSQ[:, vt, c0:c0 + n], vt == 0, vt == VT - 1)
                    last.then_inc(done[b], 1)

            HALVES = [slice(64 * e, 64 * e + 64) for e in range(2)]

            def projection(i, m):
                job, b, kt, count = PRODUCTS[m]
                c0, n = {"W": XT, "A": XT, "N": TB}.get(job, XB)[b]
                if m == 0:
                    gate(pw, i * 16 + 16)
                if job == "N" and b == 0:
                    gate(ksq, i + 1)
                if kt == 0:
                    gate(out_of[b], base(i) + (JOB[job] - 1))
                if job in "WA":
                    r = HALVES["WA".index(job)]
                    last = mm(bank[b][:, 0:n], WB[r, W_LORA:W_LORA + 128], LO[r, c0:c0 + n], True, True)
                elif job == "N":
                    last = mm(bank[b][:, 0:n], BONES, EM[:, c0:c0 + n], True, True)
                else:
                    w = {"K": W_K, "R": W_R, "V": W_V}[job] + kt * 128
                    last = mm(bank[b][:, 0:n], WB[:, w:w + 128], XN[:, kt, c0:c0 + n], kt == 0, kt == KT - 1)
                if kt == count - 1:
                    last.then_inc(done[b], 1)

            def chunk_step(i, c, stage):
                S = SS[c % 2]
                if stage == 0:
                    gate(s_ready, i * (NC + 1) + (c + 1))
                    for r in HALVES:
                        mm(bank[3][r, 0:HD], AK[r, c, 0, :], VTT[r, c, :], True, False)
                        last = mm(bank[3][r, 0:HD], AR[r, c, 0, :], S[r, :], False, True)
                    last.then_inc(rhs_done, 1)
                if stage == 1:
                    if c == 0:
                        gate(inv_yb, i * 24 + 24)
                    gate(rhs_ready, i * NC + (c + 1))
                    mm(bank[4][:, 0:HD], YB[c // 8][:, c % 8, :], RH, True, True).then_inc(u_done, 1)
                if stage == 2:
                    gate(u_ready, i * NC + (c + 1))
                    for r in HALVES:
                        mm(bank[5][r, 0:HD], KTT[r, c, :], VTT[r, c, :], True, False)
                        last = mm(bank[5][r, 0:HD], BTT[r, c, :], U[r, :], False, True)
                    last.then_inc(s_done, 1)
                    ob = bank[6 + c // 8]
                    cols = slice((c % 8) * CR, (c % 8 + 1) * CR)
                    for r in HALVES:
                        mm(ob[r, cols], VTT[r, c, :], AK[r, c, 1, :], True, False)
                        mm(ob[r, cols], S[r, :], AR[r, c, 1, :], False, False)
                        last = mm(ob[r, cols], U[r, :], GT[r, c, :], False, True)
                    last.then_inc(o_done, 1)

            def head_sums(src, blocks, before):
                for b, (c0, n) in enumerate(blocks):
                    gate(out_of[b], before)
                    mm(bank[b][:, 0:n], BONES, src[:, c0:c0 + n], True, True).then_inc(done[b], 1)

            def merge_gate(m, before):
                b, kt = divmod(m, KT)
                c0, n = XT[b]
                if kt == 0:
                    gate(out_of[b], before)
                last = mm(bank[b][:, 0:n], WB[:, W_G + kt * 128:W_G + kt * 128 + 128],
                          XN[:, kt, c0:c0 + n], kt == 0, kt == KT - 1)
                if kt == KT - 1:
                    last.then_inc(done[b], 1)

            def chunk_products(i, previous):
                job = base(i) + 6
                gate(gram_in, i * 4 + 2)
                for n_, (src, idn) in enumerate(((KE, IDS), (BE, NIDS), (V, IDS))):
                    if n_ == 2:
                        for b in range(3):
                            gate(out_of[b], base(i) + JOB["V"])
                        if previous:
                            head_sums(O, PB, job)
                            job = job + 1
                    for hf in range(2):
                        m = 2 * n_ + hf
                        if m >= 2:
                            gate(tr_ready, i * 6 + (m - 1))
                        elif previous:
                            gate(o_ready, (i - 1) * 2 + (m + 1))
                        for c in range(8):
                            for r in HALVES:
                                last = mm(bank[6 + m % 2][r, c * CR:(c + 1) * CR],
                                          src[r, (8 * hf + c) * CR:(8 * hf + c + 1) * CR], idn[r, :], True, True)
                        last.then_inc(tr_done, 1)
                        if m < 3:
                            projection(i, SPREAD + 2 * m)
                            projection(i, SPREAD + 2 * m + 1)
                gate(gram_in, i * 4 + 4)
                for q in range(4):
                    for g, src in ((3, BE), (4, KE)):
                        if q:
                            gate(gram_ready, i * 12 + (3 * q + g - 5))
                        for c in range(4):
                            for r in HALVES:
                                cc = 4 * q + c
                                last = mm(bank[g][r, c * 128:(c + 1) * 128], src[r, cc * CR:(cc + 1) * CR],
                                          AR[r, cc, :, :].rearrange("p a t -> p (a t)"), True, True)
                        last.then_inc(gram_done, 1)
                    if q:
                        gate(gram_ready, i * 12 + 3 * q)
                    for c in range(4):
                        for r in HALVES:
                            cc = 4 * q + c
                            last = mm(bank[5][r, c * CR:(c + 1) * CR], AR[r, cc, 0, :],
                                      BE[r, cc * CR:(cc + 1) * CR], True, True)
                    last.then_inc(gram_done, 1)
                if previous:
                    gate(var_sq, i)
                    head_sums(EM[:, 0:T], PB, job)
                    job = job + 1
                gate(tr_ready, i * 6 + 6)
                LAST = len(LEVELS) - 1
                for lv in range(len(LEVELS)):
                    fill = 6 * lv
                    for hf in range(2):
                        if lv == 0:
                            gate(inv_xr, i * 9 + 1)
                        else:
                            gate(inv_xr, i * 9 + (2 * lv + hf))
                            if hf == 1:
                                gate(inv_yr, i * 11 + (2 * lv + 1))
                        for c in range(8):
                            last = mm(bank[3 + hf][:, c * CR:(c + 1) * CR], GTB[hf][:, c, :], X_[:, 8 * hf + c, :], True, True)
                        last.then_inc(inv_p, 1)
                        for _ in range(1 + hf):
                            if lv < LAST:
                                merge_gate(fill, job)
                            fill += 1
                    if lv == LAST:
                        gate(rkr, i + 1)
                        head_sums(RK, TB, job + 1)
                    for hf in range(2):
                        if lv < LAST:
                            gate(inv_c, i * 8 + (2 * lv + hf + 1))
                            gate(inv_yb, i * 24 + (4 * lv + 2 * hf + 2))
                            for c in range(8):
                                cc = 8 * hf + c
                                last = mm(bank[5 + hf][:, c * CR:(c + 1) * CR], YB[hf][:, c, :], PP[:, cc, :], True, True)
                            last.then_inc(inv_xd, 1)
                        gate(inv_b, i * 10 + (2 * lv + hf + 1))
                        if lv == LAST:
                            gate(inv_yr, i * 11 + (2 * lv + hf))
                        for c in range(8):
                            cc = 8 * hf + c
                            last = mm(bank[YBANK[hf]][:, c * CR:(c + 1) * CR], PPB[hf][:, c, :], Y[:, cc, :], True, True)
                        last.then_inc(inv_yd, 1)
                        for _ in range(1 + hf):
                            if lv < LAST:
                                merge_gate(fill, job)
                            fill += 1

            for m in range(SPREAD):
                projection(0, m)
            chunk_products(0, False)
            with pe.Fori(1, NP) as i:
                for s in range(SLOTS):
                    chunk_step(i - 1, s // 3, s % 3)
                    for m in range(SPREAD):
                        if slot(m) == s:
                            projection(i, m)
                chunk_products(i, True)
            for s in range(SLOTS):
                chunk_step(NP - 1, s // 3, s % 3)
            for g in range(3):
                last = nc.tensor.transpose(bank[3][:, g * P:(g + 1) * P],
                                           SV[:, 2 * g:2 * g + 2, :, :].rearrange("p a b c -> p (a b c)"), IDF)
            last.then_inc(sv_done, 1)
            pe.wait_ge(o_ready, 2 * NP)
            head_sums(O, PB, J_WO - 2)
            pe.wait_ge(var_sq, NP)
            head_sums(EM[:, 0:T], PB, J_WO - 1)

            pe.wait_ge(so_ready, 2)
            mm(bank[4][:, 0:64], O2[0:64, :], CON[0:64, C_ID:C_ID + 64], True, True).then_inc(so_done, 1)

            def split_products(b, n, wh, wl, xh, xl, c0):
                for kt in range(KT):
                    hi = wh[:, kt * P:kt * P + P]
                    xs = [x[kt][:, c0:c0 + n] for x in (xh, xl)]
                    mm(bank[b][:, 0:n], hi, xs[0], kt == 0, False)
                    mm(bank[b][:, 0:n], hi, xs[1], False, False)
                    last = mm(bank[b][:, 0:n], wl[:, kt * P:kt * P + P], xs[0], False, kt == KT - 1)
                last.then_inc(done[b], 1)

            pe.wait_ge(mg_lo, 2 * KT)
            with pe.Fori(0, KT // 2) as g:
                for j in range(2):
                    gate(wo_lo, g * 2 + (j + 1))
                    for b, (c0, n) in enumerate(TB):
                        gate(out_of[b], g * 2 + (J_WO + j))
                        split_products(b, n, WOHR[j], WOLR[j], MGHR, MGLR, c0)

            def mean_square(sq, bufs, before):
                for kt in range(KT):
                    pe.wait_ge(sq, kt + 1)
                    for b, (c0, n) in enumerate(TB):
                        if kt == 0:
                            pe.wait_ge(out_of[b], before)
                        last = mm(bank[b][:, 0:n], ONES, bufs[kt][:, c0:c0 + n], kt == 0, kt == KT - 1)
                        if kt == KT - 1:
                            last.then_inc(done[b], 1)

            mean_square(sq2, F_SQ, J_N2 - 1)
            pe.wait_ge(x_lo, KT)
            with pe.Fori(0, FT) as ft:
                for q in range(2):
                    gate(gu_lo, ft * 2 + (q + 1))
                    for b, (c0, n) in enumerate(TB):
                        gate(out_of[b], ft * 2 + (J_FFN + q))
                        split_products(b, n, WGHR[q], WGLR[q], XHR, XLR, c0)
            for j in range(2):
                pe.wait_ge(wd0_loaded[j], 16)
                for b, (c0, n) in enumerate(TB):
                    if j == 0:
                        pe.wait_ge(out_of[b], J_DOWN)
                    for kt in range(KH):
                        last = mm(bank[b][:, 0:n], WD0[j][:, kt, :], ACTV[:, j * KH + kt, c0:c0 + n],
                                  j + kt == 0, j == 1 and kt == KH - 1)
                    if j == 1:
                        last.then_inc(done[b], 1)

            def down(m, odd, loads):
                gate(wd_loaded[odd], loads)
                for b, (c0, n) in enumerate(TB):
                    gate(out_of[b], m + J_DOWN)
                    for kt in range(FT):
                        last = mm(bank[b][:, 0:n], WD[odd][:, kt, :], ACTV[:, kt, c0:c0 + n], kt == 0, kt == FT - 1)
                    last.then_inc(done[b], 1)

            with pe.Fori(0, KT // 2 - 1) as g:
                down(g * 2 + 1, 1, g * 16 + 16)
                down(g * 2 + 2, 0, g * 16 + 16)
            down(KT - 1, 1, 16 * (KT // 2))
            mean_square(sq3, Y_SQ, J_N3 - 1)

        @block.scalar
        def _(act):
            def f(out, in_, func, bias=0.0, scale=1.0):
                return nc.scalar.activation(out, in_, func, bias=bias, scale=scale)

            for kt in range(KT):
                if kt == 0:
                    act.wait_ge(x_loaded, 16 * KT)
                if kt >= 2:
                    act.wait_ge(sq_used, kt - 1)
                f(N_SQ[kt % 2], XN[:, kt, 0:TS], ACT.Square).then_inc(sq_ready, 1)
            act.wait_ge(con_loaded, 16)
            act.wait_ge(par_loaded, 16 * 5)
            for b, (c0, n) in enumerate(TB):
                act.wait_ge(done[b], J_NORM)
                f(N_RS[:, c0:c0 + n], bank[b][:, 0:n], ACT.Ln, EPS[0], 1.0 / D).then_inc(out_of[b], 1)
            for b in range(3):
                act.wait_ge(out_of[b], J_NORM)
            f(N_RS, N_RS, ACT.Exp, scale=-0.5).then_inc(rs_ready, 1)
            for b, (c0, n) in enumerate(XB):
                act.wait_ge(done[b], J_LO)
                f(N_T0[:, 1 + c0:1 + c0 + n], bank[b][:, 0:n], ACT.Copy, scale=MULO[:, 0:1]).then_inc(mu_ready, 1)
            for b, (c0, n) in enumerate(XB):
                act.wait_ge(done[b], J_GLO)
                nc.scalar.copy(GLO[0:16, c0:c0 + n], bank[b][0:16, 0:n]).then_inc(out_of[b], 1)
            act.wait_ge(lo_ready, 1)
            f(LO[0:64, 0:TS], LO[0:64, 0:TS], ACT.Tanh).then_inc(a_step, 1)


            with act.Fori(0, GH) as h:
                j0 = h * PER_GLA + J_GLA
                act.wait_ge(g_head, h + 1)
                for b, (c0, n) in enumerate(XT):
                    act.wait_ge(done[b], j0 + 1)
                    f(E0[:, c0:c0 + n], bank[b][:, 0:n], ACT.Abs, GCUR).then_inc(g_abs, 1)
                act.wait_ge(g_abs, h * 3 + 3)
                f(E0, E0, ACT.Exp, scale=-1.0).then_inc(a_step, 1)
                act.wait_ge(a_step, h + 2)
                f(E0, E0, ACT.Ln, bias=1.0).then_inc(g_ln, 1)
                for vt in range(VT):
                    for b, (c0, n) in enumerate(XT):
                        act.wait_ge(done[b], j0 + (2 + vt))
                        f(TGB[:, vt, c0:c0 + n], bank[b][:, 0:n], ACT.Tanh, scale=0.5).then_inc(out_of[b], 1)
                act.wait_ge(g_scan, h + 1)
                f(EPG, GB, ACT.Exp, scale=1.0 / GATE_NORM).then_inc(g_exp, 1)
                f(EMG, GB, ACT.Exp, scale=-1.0 / GATE_NORM).then_inc(g_exp, 1)
                f(GDM, GDE, ACT.Exp, scale=1.0 / GATE_NORM).then_inc(g_exp, 1)
                f(GAS, LA[:, T:TS], ACT.Exp, scale=1.0 / GATE_NORM).then_inc(g_exp, 1)
                for tt in range(9):
                    rows = P if tt < 8 else NS
                    act.wait_ge(g_vps, h * 9 + (tt + 1))
                    nc.scalar.copy(VTM[0:rows, tt, :], bank[3 + tt % 2][0:rows, 0:DV]).then_inc(g_v, 1)
                for q in range(2):
                    act.wait_ge(g_kt, h * 2 + (q + 1))
                    nc.scalar.copy(KTM[:, 4 * q:4 * q + 4, :].rearrange("p a b -> p (a b)"), bank[5][:, :]).then_inc(g_ktm, 1)
                for c in range(NG):
                    act.wait_ge(g_sp, h * (NG + 1) + (c + 1))
                    f(SF, SP[c % 2], ACT.Copy, scale=GF[:, c:c + 1]).then_inc(g_sf, 1)
                    act.wait_ge(g_ops, h * NG + (c + 1))
                    nc.scalar.copy(OG[:, :, c * CG:(c + 1) * CG],
                                   bank[7][:, 0:DV].rearrange("p (a b) -> p a b", b=CG)).then_inc(g_og, 1)
                act.wait_ge(g_kst, h + 1)
                nc.scalar.copy(GKS[0:NS, :], bank[3][0:NS, 0:P]).then_inc(g_ksm, 1)
                act.wait_ge(g_os, h + 1)
                nc.scalar.copy(OG[:, :, T:TS], bank[6][:, 0:VT * NS].rearrange("p (a b) -> p a b", b=NS)).then_inc(g_og, 1)
                act.wait_ge(g_og, h * (NG + 1) + NG + 1)
                f(GSQ, OG, ACT.Square).then_inc(g_sq, 1)
                for b, (c0, n) in enumerate(TB):
                    act.wait_ge(done[b], j0 + 6)
                    f(E0[:, c0:c0 + n], bank[b][:, 0:n], ACT.Ln, EPS[2], 1.0 / DV).then_inc(out_of[b], 1)
                for b in range(3):
                    act.wait_ge(out_of[b], j0 + 6)
                f(E0, E0, ACT.Exp, scale=-0.5).then_inc(g_rt, 1)

            def first_phase(i, s):
                j0 = base(i)

                def tanh(dst, job, b, bias):
                    c0, n = XT[b]
                    act.wait_ge(done[b], j0 + JOB[job])
                    f(dst[:, c0:c0 + n], bank[b][:, 0:n], ACT.Tanh, CUR[:, bias:bias + 1], 0.5).then_inc(out_of[b], 1)

                def mix(job, b, mu):
                    c0, n = XB[b]
                    act.wait_ge(done[b], j0 + JOB[job])
                    if job != "K" and b == 0:
                        act.wait_ge(out_of[2], j0 + (4 if job == "V" else 3))
                    f(T0[:, 1 + c0:1 + c0 + n], bank[b][:, 0:n], ACT.Copy, scale=CUR[:, mu:mu + 1]).then_inc(mu_ready, 1)

                def squares_of_k():
                    act.wait_ge(out_of[2], j0 + 3)
                    f(EM, K, ACT.Square, scale=CUR[:, P_KK:P_KK + 1]).then_inc(ksq, 1)

                def inverse_length():
                    for b in range(3):
                        act.wait_ge(out_of[b], j0 + JOB["N"])
                    f(EM, EM, ACT.Ln).then_inc(kln, 1)
                    act.wait_ge(kln, i + 1)
                    f(EM, EM, ACT.Exp, scale=-0.5).then_inc(knorm, 1)

                def decays():
                    act.wait_ge(ldr, i + 1)
                    f(EP[:, :, 1:65], B.rearrange("p (c t) -> p c t", t=CR), ACT.Exp).then_inc(ept, 1)
                    f(SV[:, Q_W, i, :], LD[:, T:TS], ACT.Exp).then_inc(ept, 1)

                def inverse_decays():
                    act.wait_ge(kk_ready, i + 1)
                    f(EM[:, 0:T], B, ACT.Exp, scale=-1.0).then_inc(ept, 1)

                for b in range(3):
                    if s == ends["W", b] + 1:
                        tanh(LD, "W", b, P_HW0)
                    if s == ends["A", b] + 1:
                        tanh(A, "A", b, P_HA0)
                    for job, mu in (("K", P_MUK), ("R", P_MUR), ("V", P_MUV)):
                        if s == ends[job, b] + 1:
                            mix(job, b, mu)
                if s == ends["A", 2] + 3:
                    decays()
                if s == ends["K", 2] + 2:
                    squares_of_k()
                if s == ends["N", 2] + 2:
                    inverse_length()
                if s == ends["N", 2] + 7:
                    inverse_decays()

            def chunk_side(i, s):
                c = s // 3
                if s % 3 == 0:
                    act.wait_ge(s_ready, i * (NC + 1) + (c + 1))
                    f(SD, SS[c % 2], ACT.Copy, scale=DC[:, c:c + 1]).then_inc(s_scaled, 1)
                if s % 3 == 2 and c % 8 == 7:
                    act.wait_ge(o_done, i * NC + (c + 1))
                    nc.scalar.copy(O[:, (c - 7) * CR:(c + 1) * CR], bank[6 + c // 8][:, :]).then_inc(o_ready, 1)

            def norm_square(i, job):
                act.wait_ge(out_of[2], job)
                f(EM[:, 0:T], O, ACT.Square).then_inc(var_sq, 1)

            def norm_root(i, job):
                for b, (c0, n) in enumerate(PB):
                    act.wait_ge(done[b], job)
                    f(EM[:, c0:c0 + n], bank[b][:, 0:n], ACT.Ln, EPS[1], 1.0 / HD).then_inc(out_of[b], 1)
                for b in range(3):
                    act.wait_ge(out_of[b], job)
                f(EM[:, 0:T], EM[:, 0:T], ACT.Exp, scale=-0.5).then_inc(dev_ready, 1)

            def second_phase(i, previous):
                job = base(i) + 6
                for n_, dst in enumerate((KTT, BTT, VTT)):
                    for hf in range(2):
                        m = 2 * n_ + hf
                        act.wait_ge(tr_done, i * 6 + (m + 1))
                        nc.scalar.copy(dst[:, 8 * hf:8 * hf + 8, :].rearrange("p a b -> p (a b)"),
                                       bank[6 + m % 2][:, :]).then_inc(tr_ready, 1)
                        if m == 2:
                            first_phase(i, SLOTS + 1)
                if previous:
                    norm_square(i, job + 1)
                    norm_root(i, job + 2)
                    job = job + 2
                for lv in range(len(LEVELS) + 1):
                    for hf in range(2):
                        act.wait_ge(inv_yr, i * 11 + (1 if lv == 0 else 2 * lv + hf))
                        for e in range(2):
                            r = slice(64 * e, 64 * e + 64)
                            nc.scalar.copy(YB[hf][r, :, r], Y[r, 8 * hf:8 * hf + 8, :]).then_inc(inv_yb, 1)
                    for b, (c0, n) in enumerate(XT):
                        if lv != (3, 4, 4)[b]:
                            continue
                        if previous and b == 0:
                            act.wait_ge(merged, i)
                        act.wait_ge(done[b], job + 1)
                        f(TG[:, c0:c0 + n], bank[b][:, 0:n], ACT.Tanh, scale=0.5).then_inc(out_of[b], 1)

            act.wait_ge(p_start, 1)
            for s in range(SLOTS):
                first_phase(0, s)
            second_phase(0, False)
            with act.Fori(1, NP) as i:
                act.wait_ge(p_start, i + 1)
                for s in range(SLOTS):
                    chunk_side(i - 1, s)
                    first_phase(i, s)
                second_phase(i, True)
            for s in range(SLOTS):
                chunk_side(NP - 1, s)
            act.wait_ge(sv_done, 1)
            for g in range(3):
                for q in range(2):
                    for e in range(2):
                        nc.scalar.copy(QQ[64 * e:64 * e + 64, 2 * g + q, :],
                                       bank[3][64 * q:64 * q + 64, g * P + 64 * e:g * P + 64 * e + 64]).then_inc(sv_ready, 1)
            norm_square(NP, J_WO - 1)
            norm_root(NP, J_WO)
            act.wait_ge(merged, NP)
            for kt in range(KT):
                nc.scalar.copy(MGHR[kt][:, 0:T], MG[:, kt, 0:T]).then_inc(mg_hi, 1)
            act.wait_ge(sa_step, 1)
            f(ST[:, 4:5], ST[:, 3:4], ACT.Sqrt, EPS[1], 1.0 / HD).then_inc(osq_ready, 1)
            act.wait_ge(so_done, 1)
            nc.scalar.copy(SO.rearrange("p a b -> p (a b)"), bank[4][:, 0:64]).then_inc(a_step, 1)

            def wo_high(m):
                act.wait_ge(wo_loaded[m % 2], 16 * (m // 2 + 1))
                nc.scalar.copy(WOHR[m % 2][:, :], WOL[m % 2].rearrange("p k n -> p (k n)")).then_inc(wo_hi, 1)

            wo_high(0)
            wo_high(1)
            act.wait_ge(mg_ready, 1)
            for kt in range(KT):
                nc.scalar.copy(MGHR[kt][:, T:TS], MG[:, kt, T:TS]).then_inc(mg_hi, 1)

            def squares(bufs, ready, job, kt):
                act.wait_ge(out_of[2], job + kt + 1)
                f(bufs[kt], H[:, kt, :], ACT.Square).then_inc(ready, 1)

            def inverse_roots(dst, job):
                for b, (c0, n) in enumerate(TB):
                    act.wait_ge(done[b], job)
                    f(dst[:, c0:c0 + n], bank[b][:, 0:n], ACT.Ln, EPS[0], 1.0 / D).then_inc(out_of[b], 1)
                for b, (c0, n) in enumerate(TB):
                    act.wait_ge(out_of[b], job)
                    f(dst[:, c0:c0 + n], dst[:, c0:c0 + n], ACT.Exp, scale=-0.5).then_inc(rs_ready, 1)

            for kt in range(KT):
                if kt + 2 < KT:
                    wo_high(kt + 2)
                squares(F_SQ, sq2, J_WO, kt)
            inverse_roots(F_RS, J_N2)

            def gate_up_high(ft, q):
                act.wait_ge(gu_loaded[q], ft * 16 + 16)
                nc.scalar.copy(WGHR[q][:, :], WGL[q].rearrange("p k n -> p (k n)")).then_inc(gu_hi, 1)

            def silu(ft):
                for b, (c0, n) in enumerate(TB):
                    act.wait_ge(done[b], ft * 2 + (J_FFN + 1))
                    f(ACTV[:, ft, c0:c0 + n], bank[b][:, 0:n], ACT.Silu).then_inc(out_of[b], 1)

            gate_up_high(0, 0)
            for kt in range(KT):
                act.wait_ge(xn2_ready, kt + 1)
                nc.scalar.copy(XHR[kt][:, :], XL[:, kt, :]).then_inc(x_hi, 1)
            with act.Fori(0, FT - 1) as ft:
                gate_up_high(ft, 1)
                silu(ft)
                gate_up_high(ft + 1, 0)
            gate_up_high(FT - 1, 1)
            silu(FT - 1)
            act.wait_ge(done[2], J_DOWN)
            for kt in range(KT):
                squares(Y_SQ, sq3, J_DOWN, kt)
            inverse_roots(Y_RS, J_N3)

        @block.vector
        def _(dve):
            V_ = nc.vector
            steps = [0]

            def step(ins):
                ins.then_inc(v_step, 1)
                steps[0] += 1
                dve.wait_ge(v_step, steps[0])

            def loop_step(i, per):
                base, n = steps[0], [0]

                def inner(ins):
                    ins.then_inc(v_step, 1)
                    n[0] += 1
                    dve.wait_ge(v_step, i * per + (base + n[0]))

                def end(passes):
                    assert n[0] == per, n[0]
                    steps[0] = base + per * passes
                return inner, end

            def over(a, n):
                return a.unsqueeze(1).to_broadcast([a.shape[0], n, a.shape[1]])

            def each(a, n):
                return a.unsqueeze(2).to_broadcast([a.shape[0], a.shape[1], n])

            dve.wait_ge(par_loaded, 16 * 5)
            dve.wait_ge(con_loaded, 16)
            V_.tensor_scalar(PAR[:, :, P_CMUR:P_CMUR + 3], PAR[:, :, P_MUR:P_MUR + 3], -1.0, 1.0, ALU.mult, ALU.add)
            V_.tensor_scalar(PAR[:, :, P_HW0:P_HW0 + 2], PAR[:, :, P_W0:P_W0 + 2], 0.5, None, ALU.mult)
            V_.tensor_scalar(PAR[:, :, P_CKA:P_CKA + 1], PAR[:, :, P_KA:P_KA + 1], -1.0, 1.0, ALU.mult, ALU.add)
            V_.tensor_scalar(MULO[:, 1:2], MULO[:, 0:1], -1.0, 1.0, ALU.mult, ALU.add)
            step(V_.memset(N_T0[:, 0:1], 0.0))
            dve.wait_ge(rs_ready, 1)
            for kt in range(KT):
                V_.scalar_tensor_tensor(XN[:, kt, 0:TS], XN[:, kt, 0:TS], GAINS[:, 0, kt:kt + 1], N_RS,
                                        ALU.mult, ALU.mult).then_inc(xn_ready, 1)

            def shift(dst, t0, rest, ready, job):
                for b, (c0, n) in enumerate(XB):
                    dve.wait_ge(mu_ready, ready(b))
                    m = min(n, T - c0)
                    ins = V_.scalar_tensor_tensor(dst[:, c0:c0 + m], bank[b][:, 0:m], rest, t0[:, c0:c0 + m],
                                                  ALU.mult, ALU.add)
                    if b == 2:
                        ins = V_.scalar_tensor_tensor(dst[:, T:TS], bank[b][:, T - c0:TS - c0], rest,
                                                      t0[:, 1 + TS:1 + XC], ALU.mult, ALU.add)
                    ins.then_inc(out_of[b], 1)

            shift(LO, N_T0, MULO[:, 1:2], lambda b: b + 1, J_LO)
            dve.wait_ge(out_of[2], J_LO)
            step(V_.memset(ATT[:, 0:1, 0:1], 0.0))
            V_.memset(GDE, 0.0).then_inc(lo_ready, 1)

            for b in range(3):
                dve.wait_ge(out_of[b], J_GLO)
            step(V_.memset(ATT.rearrange("p a b -> p (a b)"), 0.0))
            with dve.Fori(0, GH) as h:
                st, end = loop_step(h, 9)
                j0 = h * PER_GLA + J_GLA
                V_.memset(SP[0], 0.0).then_inc(g_sp, 1)
                V_.tensor_copy(GCUR, GPAR[:, bass.ds(h, 1)]).then_inc(g_head, 1)
                dve.wait_ge(g_head, h + 1)
                for b, (c0, n) in enumerate(XT):
                    dve.wait_ge(g_abs, h * 3 + (b + 1))
                    V_.tensor_scalar(LA[:, c0:c0 + n], bank[b][:, 0:n], GCUR, 0.0, ALU.add, ALU.min).then_inc(out_of[b], 1)
                dve.wait_ge(out_of[2], j0 + 1)
                dve.wait_ge(g_ln, h + 1)
                st(V_.tensor_tensor(LA, LA, E0, ALU.subtract))
                st(V_.tensor_tensor_scan(GB, CON[:, C_RG:C_RG + T], LA[:, 0:T], 0.0, ALU.mult, ALU.add))
                B3 = GB.rearrange("p (c t) -> p c t", t=CG)
                st(V_.tensor_copy(GDE, B3[:, :, CG // 2 - 1]))
                V_.tensor_tensor(B3, B3, each(GDE, CG), ALU.subtract).then_inc(g_scan, 1)
                dve.wait_ge(g_exp, h * 4 + 4)
                E3 = EPG.rearrange("p (c t) -> p c t", t=CG)
                st(V_.tensor_copy(GF[:, NG - 1:NG], E3[:, NG - 1, CG - 1:CG]))
                st(V_.tensor_tensor(GF[:, 0:NG - 1], E3[:, 0:NG - 1, CG - 1], GDM[:, 1:NG], ALU.mult))
                for b, (c0, n) in enumerate(XT):
                    dve.wait_ge(done[b], j0 + 4)
                    m = min(n, T - c0)
                    ins = V_.tensor_tensor(GK_[:, c0:c0 + m], bank[b][:, 0:m], EMG[:, c0:c0 + m], ALU.mult)
                    if b == 2:
                        ins = V_.tensor_copy(GK_[:, T:TS], bank[b][:, T - c0:TS - c0])
                    ins.then_inc(out_of[b], 1)
                for b, (c0, n) in enumerate(XT):
                    dve.wait_ge(done[b], j0 + 5)
                    m = min(n, T - c0)
                    ins = V_.scalar_tensor_tensor(GQ_[:, c0:c0 + m], bank[b][:, 0:m], DK ** -0.5, EPG[:, c0:c0 + m],
                                                  ALU.mult, ALU.mult)
                    if b == 2:
                        ins = V_.tensor_scalar(GQ_[:, T:TS], bank[b][:, T - c0:TS - c0], DK ** -0.5, None, ALU.mult)
                    ins.then_inc(out_of[b], 1)
                for q in range(2):
                    dve.wait_ge(g_at, h * 2 + (q + 1))
                    dve.nop(nofuse=True)
                    V_.copy_predicated(ATT[:, 4 * q:4 * q + 4, :],
                                       over(CON[:, C_CAUSAL:C_CAUSAL + CG].bitcast(I32), 4),
                                       bank[6][:, :].rearrange("p (a b) -> p a b", b=CG)).then_inc(g_am, 1)
                for c in range(NG):
                    dve.wait_ge(g_sps, h * NG + (c + 1))
                    dve.wait_ge(g_sf, h * NG + (c + 1))
                    V_.scalar_tensor_tensor(SP[(c + 1) % 2], bank[4][:, 0:DV], GF[:, c:c + 1], SF,
                                            ALU.mult, ALU.add).then_inc(g_sp, 1)
                dve.wait_ge(g_v, h * 9 + 9)
                V_.tensor_tensor(VEXP[0:NS, :, :], over(VTM[0:NS, 8, :], NS), each(CON[0:NS, C_DELTA:C_DELTA + NS], DV),
                                 ALU.mult).then_inc(g_vx, 1)
                dve.wait_ge(gs_loaded, h * 16 + 16)
                for q in range(4):
                    dve.wait_ge(g_out, h * 4 + (q + 1))
                    for j in range(2):
                        b = 2 * q + j
                        V_.scalar_tensor_tensor(GS0[:, b, :], GS0[:, b, :], GAS[:, b:b + 1],
                                                bank[3 + 2 * (q % 2)][:, j * DV:(j + 1) * DV],
                                                ALU.mult, ALU.add).then_inc(g_s1, 1)
                dve.wait_ge(g_rt, h + 1)
                for vt in range(VT):
                    st(V_.scalar_tensor_tensor(OG[:, vt, :], OG[:, vt, :], GPAR[:, GH + vt:GH + vt + 1], E0,
                                               ALU.mult, ALU.mult))
                    st(V_.scalar_tensor_tensor(MG[:, h * 2 + vt, :], TGB[:, vt, :], 1.0, OG[:, vt, :],
                                               ALU.add, ALU.mult))
                dve.wait_ge(g_stored, h * 32 + 32)
                end(GH)

            for j in range(2):
                step(V_.memset(YB[j].rearrange("p a b -> p (a b)"), 0.0))

            def par1(j):
                return CUR[:, j:j + 1]

            def first_phase(i, s, st):
                j0 = base(i)
                mu0 = i * 9 + 3

                def log_decay():
                    for b in range(3):
                        dve.wait_ge(out_of[b], j0 + 1)
                    st(V_.tensor_scalar(LD, LD, -HALF_DECAY, -HALF_DECAY, ALU.mult, ALU.add))
                    V_.tensor_tensor_scan(B, CON[:, C_RR:C_RR + T], B, 0.0, ALU.mult, ALU.add).then_inc(ldr, 1)

                def rate():
                    for b in range(3):
                        dve.wait_ge(out_of[b], j0 + 2)
                    st(V_.tensor_scalar(A, A, 0.5, 0.5, ALU.mult, ALU.add))
                    st(V_.tensor_scalar(KP, A, par1(P_KA), par1(P_CKA), ALU.mult, ALU.add))

                def shift_block(dst, job, b, rest):
                    c0, n = XB[b]
                    dve.wait_ge(mu_ready, mu0 + (3 * "KRV".index(job) + b + 1))
                    m = min(n, T - c0)
                    ins = V_.scalar_tensor_tensor(dst[:, c0:c0 + m], bank[b][:, 0:m], par1(rest), T0[:, c0:c0 + m],
                                                  ALU.mult, ALU.add)
                    if b == 2:
                        ins = V_.scalar_tensor_tensor(dst[:, T:TS], bank[b][:, T - c0:TS - c0], par1(rest),
                                                      T0[:, 1 + TS:1 + XC], ALU.mult, ALU.add)
                    ins.then_inc(out_of[b], 1)

                def scale_k():
                    dve.wait_ge(out_of[2], j0 + 3)
                    st(V_.tensor_tensor(KP, KP, K, ALU.mult))

                def bound_k(b):
                    c0, n = TB[b]
                    dve.wait_ge(done[b], j0 + JOB["N"])
                    V_.tensor_scalar(EM[:, c0:c0 + n], bank[b][:, 0:n], 1e-24, None, ALU.max).then_inc(out_of[b], 1)

                def kk():
                    dve.wait_ge(knorm, i + 1)
                    V_.scalar_tensor_tensor(K, K, par1(P_KK), EM, ALU.mult, ALU.mult).then_inc(kk_ready, 1)
                    dve.wait_ge(kk_ready, i + 1)
                    st(V_.tensor_tensor(A, K, A, ALU.mult))

                def decayed_keys():
                    dve.wait_ge(ept, i * 3 + 3)
                    V_.tensor_tensor(KE, KP[:, 0:T], EM[:, 0:T], ALU.mult).then_inc(gram_in, 1)
                    V_.tensor_tensor(BE, BE, EM[:, 0:T], ALU.mult).then_inc(gram_in, 1)

                for b in range(3):
                    for dst, job, rest in ((K, "K", P_CMUK), (R, "R", P_CMUR), (V, "V", P_CMUV)):
                        if s == ends[job, b] + 1:
                            shift_block(dst, job, b, rest)
                    if s == ends["N", b] + 1:
                        bound_k(b)
                if s == ends["W", 2] + 2:
                    log_decay()
                if s == ends["A", 2] + 4:
                    rate()
                if s == ends["K", 2] + 2:
                    scale_k()
                if s == ends["N", 2] + 5:
                    kk()
                if s == ends["N", 2] + 9:
                    decayed_keys()

            def chunk_side(i, s):
                c = s // 3
                if s % 3 == 0:
                    dve.wait_ge(rhs_done, i * NC + (c + 1))
                    V_.tensor_copy(RH, bank[3][:, 0:HD]).then_inc(rhs_ready, 1)
                if s % 3 == 1:
                    dve.wait_ge(u_done, i * NC + (c + 1))
                    V_.tensor_copy(U, bank[4][:, 0:HD]).then_inc(u_ready, 1)
                if s % 3 == 2:
                    dve.wait_ge(s_done, i * NC + (c + 1))
                    dve.wait_ge(s_scaled, i * NC + (c + 1))
                    V_.scalar_tensor_tensor(SS[(c + 1) % 2], bank[5][:, 0:HD], DC[:, c:c + 1], SD,
                                            ALU.mult, ALU.add).then_inc(s_ready, 1)

            def centre(i, job, st):
                st(V_.tensor_copy(LNP, PAR[:, i, P_LNG:P_LNG + 2]))
                dve.wait_ge(o_ready, i * 2 + 2)
                for b, (c0, n) in enumerate(PB):
                    dve.wait_ge(done[b], job)
                    V_.scalar_tensor_tensor(O[:, c0:c0 + n], bank[b][:, 0:n], -1.0 / HD, O[:, c0:c0 + n],
                                            ALU.mult, ALU.add).then_inc(out_of[b], 1)

            def merge(i, job, part, st):
                if part < 3:
                    c0, n = PB[part]
                    dve.wait_ge(dev_ready, i + 1)
                    st(V_.tensor_tensor(O[:, c0:c0 + n], O[:, c0:c0 + n], EM[:, c0:c0 + n], ALU.mult))
                if part == 3:
                    st(V_.tensor_scalar(O, O, LNP[:, 0:1], LNP[:, 1:2], ALU.mult, ALU.add))
                    st(V_.tensor_tensor(O, O, RK[:, 0:T], ALU.add))
                if part == 4:
                    st(V_.scalar_tensor_tensor(O, TG[:, 0:T], 1.0, O, ALU.add, ALU.mult))
                    st(V_.tensor_copy(STG[:, i, :], TG[:, T:TS]))
                    st(V_.tensor_copy(SB[:, i, :], RK[:, T:TS]))
                    V_.tensor_tensor(MG[:, i, 0:T], MG[:, i, 0:T], O, ALU.add).then_inc(merged, 1)

            def second_phase(i, previous, st):
                job = base(i) + 6
                if previous:
                    dve.wait_ge(o_done, i * NC)
                    dve.wait_ge(s_ready, i * (NC + 1))
                K3 = K[:, 0:T].rearrange("p (c t) -> p c t", t=CR)
                R3 = R[:, 0:T].rearrange("p (c t) -> p c t", t=CR)
                V_.tensor_tensor(AR[:, :, 0, :], K3, EP[:, :, 0:CR], ALU.mult).then_inc(gram_in, 1)
                V_.tensor_tensor(AR[:, :, 1, :], R3, EP[:, :, 1:CR + 1], ALU.mult).then_inc(gram_in, 1)
                st(V_.tensor_copy(DC, EP[:, :, CR]))
                first_phase(i, SLOTS + 1, st)
                if previous:
                    centre(i - 1, job + 1, st)
                    job = job + 2
                dve.wait_ge(out_of[2], base(i) + JOB["V"])
                for q, src in ((Q_R, R), (Q_KP, KP), (Q_KK, K), (Q_KA, A), (Q_V, V)):
                    st(V_.tensor_copy(SV[:, q, i, :], src[:, T:TS]))
                for q in range(4):
                    cs = slice(4 * q, 4 * q + 4)
                    dve.wait_ge(gram_done, i * 12 + (3 * q + 1))
                    g4 = bank[3][:, :].rearrange("p (c a t) -> p c a t", a=2, t=CR)
                    V_.tensor_tensor(GTB[q // 2][:, 4 * (q % 2):4 * (q % 2) + 4, :].rearrange("p c (h t) -> p c h t", t=CR),
                                     g4[:, :, 0:1, :].to_broadcast([P, 4, 2, CR]),
                                     over(CON[:, C_MGB:C_MGB + 2 * CR], 4).rearrange("p c (h t) -> p c h t", t=CR),
                                     ALU.mult)
                    V_.tensor_tensor(Y[:, cs, :], g4[:, :, 0, :], over(CON[:, C_M2T:C_M2T + CR], 4), ALU.mult)
                    V_.tensor_tensor(GT[:, cs, :], g4[:, :, 1, :], over(CON[:, C_MG + CR:C_MG + 2 * CR], 4),
                                     ALU.mult).then_inc(gram_ready, 1)
                    dve.wait_ge(gram_done, i * 12 + (3 * q + 2))
                    V_.tensor_tensor(AK[:, cs, :, :].rearrange("p c a t -> p c (a t)"),
                                     bank[4][:, :].rearrange("p (c t) -> p c t", t=2 * CR),
                                     over(CON[:, C_MK:C_MK + 2 * CR], 4), ALU.mult).then_inc(gram_ready, 1)
                    dve.wait_ge(gram_done, i * 12 + (3 * q + 3))
                    V_.tensor_tensor(X_[:, cs, :], bank[5][:, 0:4 * CR].rearrange("p (c t) -> p c t", t=CR),
                                     over(CON[:, C_M2:C_M2 + CR], 4), ALU.mult).then_inc(gram_ready, 1)
                dve.wait_ge(gram_ready, i * 12 + 12)
                V_.tensor_tensor(X_, over(IDS, NC), X_, ALU.subtract).then_inc(inv_xr, 1)
                V_.tensor_tensor(Y, over(IDS, NC), Y, ALU.subtract).then_inc(inv_yr, 1)
                for lv in range(len(LEVELS)):
                    for hf in range(2):
                        cs = slice(8 * hf, 8 * hf + 8)
                        lx = bank[3 + hf][:, :].rearrange("p (c t) -> p c t", t=CR)
                        dve.wait_ge(inv_p, i * 10 + (2 * lv + hf + 1))
                        if lv < len(LEVELS) - 1:
                            V_.tensor_tensor(PP[:, cs, :], lx, over(CON[:, C_OFF + 64 * lv:C_OFF + 64 * lv + 64], 8),
                                             ALU.mult).then_inc(inv_c, 1)
                        V_.tensor_tensor(PPB[hf].rearrange("p c (h t) -> p c h t", t=CR),
                                         lx.unsqueeze(2).to_broadcast([P, 8, 2, CR]),
                                         over(CON[:, C_OFFB + 128 * lv:C_OFFB + 128 * lv + 128], 8).rearrange(
                                             "p c (h t) -> p c h t", t=CR), ALU.mult).then_inc(inv_b, 1)
                    if lv == 0:
                        if previous:
                            dve.wait_ge(s_stored, i * 16)
                        V_.memset(SS[0], 0.0).then_inc(s_ready, 1)
                    if lv == len(LEVELS) - 1:
                        for b, (c0, n) in enumerate(TB):
                            dve.wait_ge(done[b], job + 2)
                            V_.tensor_tensor(RK[:, c0:c0 + n], bank[b][:, 0:n], V[:, c0:c0 + n],
                                             ALU.mult).then_inc(out_of[b], 1)
                    for hf in range(2):
                        cs = slice(8 * hf, 8 * hf + 8)
                        if lv < len(LEVELS) - 1:
                            dve.wait_ge(inv_xd, i * 8 + (2 * lv + hf + 1))
                            V_.tensor_tensor(X_[:, cs, :], X_[:, cs, :],
                                             bank[5 + hf][:, :].rearrange("p (c t) -> p c t", t=CR),
                                             ALU.subtract).then_inc(inv_xr, 1)
                        dve.wait_ge(inv_yd, i * 10 + (2 * lv + hf + 1))
                        V_.tensor_tensor(Y[:, cs, :], Y[:, cs, :],
                                         bank[YBANK[hf]][:, :].rearrange("p (c t) -> p c t", t=CR),
                                         ALU.subtract).then_inc(inv_yr, 1)
                        if previous:
                            merge(i - 1, job, 2 * lv + hf, st)
                    if lv == 2:
                        V_.scalar_tensor_tensor(RK, R, par1(P_RK), KP, ALU.mult, ALU.mult).then_inc(rkr, 1)

            def begin(i):
                V_.memset(T0[:, 0:1], 0.0)
                V_.memset(EP[:, :, 0:1], 1.0)
                V_.tensor_copy(CUR[:, 0:NPAR], PAR[:, i, :]).then_inc(p_start, 1)
                dve.wait_ge(p_start, i + 1)

            begin(0)
            for s in range(SLOTS):
                first_phase(0, s, step)
            second_phase(0, False, step)
            with dve.Fori(1, NP) as i:
                st, end = loop_step(i - 1, 20)
                begin(i)
                for s in range(SLOTS):
                    chunk_side(i - 1, s)
                    first_phase(i, s, st)
                second_phase(i, True, st)
                end(NP - 1)
            for s in range(SLOTS):
                chunk_side(NP - 1, s)
            centre(NP - 1, J_WO - 1, step)
            for part in range(5):
                merge(NP - 1, J_WO, part, step)
            dve.wait_ge(s_stored, 16 * NP)
            dve.wait_ge(merged, NP)
            V_.memset(ST, 0.0).then_inc(pairs_over, 1)
            for kt in range(KT):
                dve.wait_ge(mg_hi, kt + 1)
                V_.tensor_tensor(MGLR[kt][:, 0:T], MG[:, kt, 0:T], MGHR[kt][:, 0:T].bitcast(F32),
                                 ALU.subtract).then_inc(mg_lo, 1)

            dve.wait_ge(sv_ready, 12)
            dve.wait_ge(st_loaded, 16)

            def vec(q):
                return QQ[:, q, :]

            step(V_.tensor_tensor(S2, S0, over(vec(Q_KK), HD), ALU.mult))
            step(V_.tensor_reduce(SA, S2, AX_X, ALU.add))
            step(V_.tensor_tensor(S2, each(SA, HD), over(vec(Q_KA), HD), ALU.mult))
            step(V_.tensor_tensor(S0, S0, over(vec(Q_W), HD), ALU.mult))
            step(V_.tensor_tensor(S0, S0, S2, ALU.subtract))
            dve.wait_ge(pool_step, 1)
            V_.tensor_tensor(S0, S0, S1, ALU.add).then_inc(state_new, 1)
            dve.wait_ge(state_new, 1)
            step(V_.tensor_tensor(S2, S0, over(vec(Q_R), HD), ALU.mult))
            step(V_.tensor_reduce(OO, S2, AX_X, ALU.add))
            step(V_.tensor_reduce(ST[:, 0:1], OO, AX_X, ALU.add))
            step(V_.tensor_scalar(ST[:, 1:2], ST[:, 0:1], 1.0 / HD, None, ALU.mult))
            step(V_.tensor_scalar(OO, OO, ST[:, 1:2], None, ALU.subtract))
            step(V_.tensor_tensor(OSQ, OO, OO, ALU.mult))
            V_.tensor_reduce(ST[:, 3:4], OSQ, AX_X, ALU.add).then_inc(sa_step, 1)
            dve.wait_ge(osq_ready, 1)
            step(V_.reciprocal(ST[:, 5:6], ST[:, 4:5]))
            for e in range(2):
                V_.tensor_scalar(O2[0:64, e * HD:(e + 1) * HD], OO[64 * e:64 * e + 64, :],
                                 ST[64 * e:64 * e + 64, 5:6], None, ALU.mult).then_inc(so_ready, 1)
            dve.wait_ge(a_step, 2 + GH)
            step(V_.tensor_tensor(SO, SO, each(PAR[:, :, P_LNG], NS), ALU.mult))
            step(V_.tensor_tensor(SO, SO, each(PAR[:, :, P_LNB], NS), ALU.add))
            step(V_.tensor_tensor(SO, SO, SB, ALU.add))
            step(V_.scalar_tensor_tensor(SO, STG, 1.0, SO, ALU.add, ALU.mult))
            V_.tensor_tensor(MG[:, :, T:TS], MG[:, :, T:TS], SO, ALU.add).then_inc(mg_ready, 1)

            for kt in range(KT):
                dve.wait_ge(mg_hi, KT + kt + 1)
                V_.tensor_tensor(MGLR[kt][:, T:TS], MG[:, kt, T:TS], MGHR[kt][:, T:TS].bitcast(F32),
                                 ALU.subtract).then_inc(mg_lo, 1)

            def wo_low(m):
                dve.wait_ge(wo_hi, m + 1)
                V_.tensor_tensor(WOLR[m % 2][:, :], WOL[m % 2].rearrange("p k n -> p (k n)"),
                                 WOHR[m % 2][:, :].bitcast(F32), ALU.subtract).then_inc(wo_lo, 1)

            wo_low(0)
            dve.wait_ge(h_loaded, 16 * KT)
            for m in range(KT):
                if m + 1 < KT:
                    wo_low(m + 1)
                for b, (c0, n) in enumerate(TB):
                    dve.wait_ge(done[b], m + (J_WO + 1))
                    V_.scalar_tensor_tensor(H[:, m, c0:c0 + n], bank[b][:, 0:n], 0.5, H[:, m, c0:c0 + n],
                                            ALU.mult, ALU.add).then_inc(out_of[b], 1)

            def gate_up_low(job, q):
                dve.wait_ge(gu_hi, job + 1)
                V_.tensor_tensor(WGLR[q][:, :], WGL[q].rearrange("p k n -> p (k n)"),
                                 WGHR[q][:, :].bitcast(F32), ALU.subtract).then_inc(gu_lo, 1)

            def up(ft):
                for b, (c0, n) in enumerate(TB):
                    dve.wait_ge(out_of[b], ft * 2 + (J_FFN + 1))
                    dve.wait_ge(done[b], ft * 2 + (J_FFN + 2))
                    V_.tensor_tensor(ACTV[:, ft, c0:c0 + n], bank[b][:, 0:n], ACTV[:, ft, c0:c0 + n],
                                     ALU.mult).then_inc(out_of[b], 1)

            dve.wait_ge(rs_ready, 4)
            for kt in range(KT):
                V_.scalar_tensor_tensor(XL[:, kt, :], H[:, kt, :], GAINS[:, 1, kt:kt + 1], F_RS,
                                        ALU.mult, ALU.mult).then_inc(xn2_ready, 1)
            for kt in range(KT):
                dve.wait_ge(x_hi, kt + 1)
                V_.tensor_tensor(XLR[kt][:, :], XL[:, kt, :], XHR[kt][:, :].bitcast(F32), ALU.subtract).then_inc(x_lo, 1)
            gate_up_low(0, 0)
            with dve.Fori(0, FT - 1) as ft:
                gate_up_low(ft * 2 + 1, 1)
                gate_up_low(ft * 2 + 2, 0)
                up(ft)
            gate_up_low(2 * FT - 1, 1)
            up(FT - 1)
            with dve.Fori(0, KT) as m:
                for b, (c0, n) in enumerate(TB):
                    dve.wait_ge(done[b], m + (J_DOWN + 1))
                    V_.tensor_tensor(H[:, m, c0:c0 + n], bank[b][:, 0:n], H[:, m, c0:c0 + n],
                                     ALU.add).then_inc(out_of[b], 1)
            dve.wait_ge(rs_ready, 7)
            for kt in range(KT):
                V_.scalar_tensor_tensor(H[:, kt, :], H[:, kt, :], GAINS[:, 2, kt:kt + 1], Y_RS,
                                        ALU.mult, ALU.mult).then_inc(yn_ready, 1)


def constants():
    import numpy as np
    c = np.zeros((P, NCONST), np.float32)
    t = np.arange(P) % HD
    j = np.arange(CR)
    eye = np.eye(HD, dtype=np.float32)
    c[:, C_ONES:C_ONES + 128] = 1
    c[:, C_BONES:C_BONES + 128] = np.arange(P)[:, None] // HD == np.arange(P)[None] // HD
    c[:, C_ID:C_ID + 128] = np.eye(P)
    c[:, C_IDS:C_IDS + 64] = np.concatenate([eye, eye])
    c[:, C_NIDS:C_NIDS + 64] = -np.concatenate([eye, eye])
    strict = t[:, None] < j[None]
    incl = t[:, None] <= j[None]
    c[:, C_MG:C_MG + 64], c[:, C_MG + 64:C_MG + 128] = strict, -1.0 * incl
    head = (np.arange(P)[:, None] // HD == np.arange(P)[None] // HD)
    c[:, C_MGB:C_MGB + 128] = head & np.tile(strict, (1, 2))
    c[:, C_MK:C_MK + 64], c[:, C_MK + 64:C_MK + 128] = strict, incl
    c[:, C_ML:C_ML + 64] = t[:, None] > j[None]
    pair = (t[:, None] // 2 == j[None] // 2)
    c[:, C_M2:C_M2 + 64] = pair & (t[:, None] > j[None])
    c[:, C_M2T:C_M2T + 64] = pair & (t[:, None] < j[None])
    for n, m in enumerate(LEVELS):
        off = (t[:, None] // (2 * m) == j[None] // (2 * m)) & (t[:, None] // m > j[None] // m)
        c[:, C_OFF + 64 * n:C_OFF + 64 * n + 64] = off
        c[:, C_OFFB + 128 * n:C_OFFB + 128 * n + 128] = head & np.tile(off, (1, 2))
    c[:, C_RR:C_RR + T] = np.arange(T) % CR != 0
    c[:, C_RG:C_RG + T] = np.arange(T) % CG != 0
    c[:, C_CAUSAL:C_CAUSAL + CG] = np.arange(P)[:, None] <= np.arange(CG)[None]
    c[:NS, C_DELTA:C_DELTA + NS] = np.eye(NS)
    c[:, C_EPS:C_EPS + 3] = np.array([NORM_EPS, GN_EPS, GLA_EPS], np.float32)
    return c


def kernel(**inputs):
    import numpy as np
    import concourse.bacc as bacc
    from concourse.bass_utils import run_bass_kernel_spmd as run
    a = {k: np.asarray(v) for k, v in inputs.items()}

    def chans(x):
        return x.T.reshape(KT, P, -1)

    def tiles(w, c0, n):
        return w[:, c0:c0 + n].reshape(-1, P, n).transpose(1, 0, 2).reshape(P, -1)

    w = a["w_in"][0]
    q0, k0, v0, gl0, ga0, gb0 = 3200, 3712, 4224, 5248, 5264, 6288
    wgu, wd = a["ffn_w_gu"][0], a["ffn_w_down"][0]
    mu = a["mu_shift"][0]
    percol = [mu[0:D], mu[D:2 * D], mu[2 * D:3 * D], a["rwkv_w0"][0], a["rwkv_a0"][0], a["rwkv_k_k"][0],
              a["rwkv_k_a"][0], a["rwkv_r_k"][0].reshape(D), a["rwkv_lnx_g"][0], a["rwkv_lnx_b"][0]]
    ins = {
        "xT": np.concatenate([chans(a["x_prompt"][0]), chans(a["x_sample"][:, 0])], 2),
        "prevT": chans(a["state_shift"][0]).transpose(1, 0, 2),
        "gains": np.stack([a["norm_mix"][0], a["norm_ffn"][0], a["norm_final"]]).reshape(3, KT, P).transpose(2, 0, 1),
        "consts": constants(),
        "w_lo": tiles(w, 3072, 128),
        "w_glo": tiles(w, gl0, 16),
        "mu_lo": mu[3072:3200].reshape(P, 1),
        "w_gla": np.stack([np.concatenate([tiles(w, q0 + h * DK, DK), tiles(w, k0 + h * DK, DK),
                                           tiles(w, v0 + h * DV, DV), tiles(w, gb0 + h * DV, 128),
                                           tiles(w, gb0 + h * DV + 128, 128)], 1) for h in range(GH)]),
        "w_gla2": np.stack([a["gla_a2"][0][:, h * DK:(h + 1) * DK] for h in range(GH)]),
        "glapar": np.concatenate([a["gla_ab"][0].reshape(GH, DK).T, a["gla_norm_g"][0].reshape(VT, P).T], 1),
        "w_pair": np.stack([np.concatenate([tiles(w, i * 128, 128), tiles(w, D + i * 128, 128),
                                            tiles(w, 2 * D + i * 128, 128), tiles(w, ga0 + i * 128, 128),
                                            np.concatenate([a["rwkv_w2"][0][:, i * 128:i * 128 + 128],
                                                            a["rwkv_a2"][0][:, i * 128:i * 128 + 128]], 0)], 1)
                            for i in range(NP)]),
        "par": np.stack(percol, 1).reshape(NP, P, 10).transpose(1, 0, 2),
        "gla_s": a["state_gla"][0].transpose(1, 2, 0, 3).reshape(GH, DK, NS * DV),
        "wkv_s": a["state_wkv"][0].reshape(NS, NP, 2, HD * HD).transpose(2, 1, 0, 3).reshape(P, HD * HD),
        "w_o": np.stack([tiles(a["w_o"][0], m * 128, 128) for m in range(KT)]),
        "w_gu": np.stack([np.concatenate([tiles(wgu, f * 128, 128), tiles(wgu, F + f * 128, 128)], 1)
                          for f in range(FT)]),
        "w_d": np.stack([tiles(wd, m * 128, 128) for m in range(KT)]),
    }
    ins = {k: np.ascontiguousarray(v) for k, v in ins.items()}
    outs = {"yT": (KT, P, TS), "shT": (P, KT, 1 + NS), "wkvp": (NP, P, HD), "glap": (GH, DK, DV),
            "wkvs": (P, HD * HD), "glas": (GH, DK, NS * DV)}
    nc = bacc.Bacc("TRN2", target_bir_lowering=False, num_devices=1)
    args = [nc.dram_tensor("in_" + k, v.shape, F32, kind="ExternalInput").ap() for k, v in ins.items()]
    args += [nc.dram_tensor("out_" + k, s, F32, kind="ExternalOutput").ap() for k, s in outs.items()]
    hybrid_step(nc, *args)
    res = run(nc, [{"in_" + k: v for k, v in ins.items()}], core_ids=[0]).results[0]
    r = {k: np.asarray(res["out_" + k]) for k in outs}
    y = r["yT"].reshape(D, TS).T
    sh = r["shT"].transpose(2, 1, 0).reshape(1 + NS, D)
    wkvp = r["wkvp"].reshape(NP * 2, HD, HD).transpose(0, 2, 1)
    wkvs = r["wkvs"].reshape(2, NP, NS, HD, HD).transpose(2, 1, 0, 3, 4).reshape(NS, 2 * NP, HD, HD)
    glas = r["glas"].reshape(GH, DK, NS, DV).transpose(2, 0, 1, 3)
    return tuple(np.ascontiguousarray(v) for v in (
        y[None, :T], y[T:, None], sh[None, :1], wkvp[None, None], r["glap"][None, None],
        sh[None, 1:], wkvs[None], glas[None]))
```
